# Optimizing a Trainium2 kernel written in Bass

```python
import math
import jax, jax.numpy as jnp
from jax import lax
import numpy as np
import jax
import jax.numpy as jnp

D_MODEL = 1024
BATCH = 1
SEQ = 512
DEPTH = 2

N_META = 16
BLOCK_Q = 128
N_A_LAYERS = DEPTH // 2
N_B_LAYERS = DEPTH - N_A_LAYERS
SB_HEADS = 16
SB_HEAD_DIM = D_MODEL // SB_HEADS
DIFF_HEADS = 8
DIFF_QK_DIM = D_MODEL // DIFF_HEADS // 2
DIFF_V_DIM = 2 * DIFF_QK_DIM
ROPE_DIM = DIFF_QK_DIM // 4
ROPE_THETA = 500000.0
D_FF = 4 * D_MODEL
EPS = 1e-6


def rmsnorm(x, g):
    xf = x.astype(jnp.float32)
    y = xf * lax.rsqrt(jnp.mean(xf * xf, axis=-1, keepdims=True) + EPS)
    return (y * g.astype(jnp.float32)).astype(x.dtype)

def rope_tables(T):
    inv_freq = jnp.power(ROPE_THETA, -jnp.arange(0, ROPE_DIM, 2, dtype=jnp.float32) / ROPE_DIM)
    ang = jnp.arange(T, dtype=jnp.float32)[:, None] * inv_freq[None, :]
    return jnp.cos(ang), jnp.sin(ang)

def apply_partial_rope(x, cos, sin):
    half = ROPE_DIM // 2
    x1 = x[..., :half]
    x2 = x[..., half:ROPE_DIM]
    c = cos[:, None, :]
    s = sin[:, None, :]
    return jnp.concatenate([x1 * c - x2 * s, x2 * c + x1 * s, x[..., ROPE_DIM:]], axis=-1)

def to_blocks(q):
    B, H, T, D = q.shape
    return q.reshape(B, H, T // BLOCK_Q, BLOCK_Q, D).transpose(2, 0, 1, 3, 4)

def from_blocks(o):
    NB, B, H, BQ, D = o.shape
    return o.transpose(1, 2, 0, 3, 4).reshape(B, H, NB * BQ, D)

def merge_heads(o):
    B, H, T, D = o.shape
    return o.transpose(0, 2, 1, 3).reshape(B, T, H * D)

def stick_breaking_attention(q, k, v):
    T = q.shape[2]
    scale = SB_HEAD_DIM ** -0.5
    kf = k.astype(jnp.float32)
    key_pos = jnp.arange(T)

    def one_block(args):
        qb, q0 = args
        z = jnp.einsum('bhqd,bhkd->bhqk', qb.astype(jnp.float32), kf) * scale
        q_pos = q0 + jnp.arange(BLOCK_Q)
        past = key_pos[None, :] < q_pos[:, None]
        log_keep = jnp.where(past, jax.nn.log_sigmoid(-z), 0.0)
        after = lax.cumsum(log_keep, axis=3, reverse=True) - log_keep
        w = jnp.where(past, jnp.exp(jax.nn.log_sigmoid(z) + after), 0.0)
        return jnp.einsum('bhqk,bhkd->bhqd', w.astype(v.dtype), v)

    starts = jnp.arange(T // BLOCK_Q) * BLOCK_Q
    return from_blocks(lax.map(one_block, (to_blocks(q), starts)))

def differential_attention(q1, q2, k1, k2, v, lam):
    T = q1.shape[2]
    scale = DIFF_QK_DIM ** -0.5
    k1f = k1.astype(jnp.float32)
    k2f = k2.astype(jnp.float32)
    key_pos = jnp.arange(T)

    def one_block(args):
        q1b, q2b, q0 = args
        q_pos = q0 + jnp.arange(BLOCK_Q)
        causal = key_pos[None, :] <= q_pos[:, None]

        def probs(qb, kk):
            s = jnp.einsum('bhqd,bhkd->bhqk', qb.astype(jnp.float32), kk) * scale
            return jax.nn.softmax(jnp.where(causal, s, -jnp.inf), axis=-1)

        w = probs(q1b, k1f) - lam * probs(q2b, k2f)
        return jnp.einsum('bhqk,bhkd->bhqd', w.astype(v.dtype), v)

    starts = jnp.arange(T // BLOCK_Q) * BLOCK_Q
    return from_blocks(lax.map(one_block, (to_blocks(q1), to_blocks(q2), starts)))

def squared_relu_mlp(x, g, w_in, w_out):
    h = rmsnorm(x, g)
    return jnp.square(jax.nn.relu(h @ w_in)) @ w_out

def first_inputs(seed: int = 0) -> dict:
    key = jax.random.key(seed)
    ks = jax.random.split(key, 20)
    nrm = jax.random.normal
    f32 = jnp.float32

    def w(k, shape, fan_in):
        return nrm(k, shape, f32) * fan_in ** -0.5

    def gain(k, shape):
        return 1.0 + 0.05 * nrm(k, shape, f32)

    return {
        "x": nrm(ks[0], (BATCH, SEQ, D_MODEL), f32),
        "meta_tokens": nrm(ks[1], (N_META, D_MODEL), f32),
        "a_norm_g": gain(ks[2], (N_A_LAYERS, D_MODEL)),
        "a_w_qkv": w(ks[3], (N_A_LAYERS, D_MODEL, 3 * D_MODEL), D_MODEL),
        "a_w_o": w(ks[4], (N_A_LAYERS, D_MODEL, D_MODEL), D_MODEL),
        "kv_norm_g": gain(ks[5], (D_MODEL,)),
        "kv_w": w(ks[6], (D_MODEL, DIFF_HEADS * (2 * DIFF_QK_DIM + DIFF_V_DIM)), D_MODEL),
        "kv_k_norm_g": gain(ks[7], (2, DIFF_QK_DIM)),
        "b_norm_g": gain(ks[8], (N_B_LAYERS, D_MODEL)),
        "b_w_q": w(ks[9], (N_B_LAYERS, D_MODEL, DIFF_HEADS * 2 * DIFF_QK_DIM), D_MODEL),
        "b_q_norm_g": gain(ks[10], (N_B_LAYERS, 2, DIFF_QK_DIM)),
        "b_lambda": 0.1 * nrm(ks[11], (N_B_LAYERS, 4, DIFF_QK_DIM), f32),
        "b_subln_g": gain(ks[12], (N_B_LAYERS, DIFF_V_DIM)),
        "b_w_o": w(ks[13], (N_B_LAYERS, DIFF_HEADS * DIFF_V_DIM, D_MODEL), DIFF_HEADS * DIFF_V_DIM),
        "mlp_norm_g": gain(ks[14], (DEPTH, D_MODEL)),
        "mlp_w_in": w(ks[15], (DEPTH, D_MODEL, D_FF), D_MODEL),
        "mlp_w_out": w(ks[16], (DEPTH, D_FF, D_MODEL), D_FF),
    }

def first_block(x, meta_tokens, a_norm_g, a_w_qkv, a_w_o, kv_norm_g, kv_w, kv_k_norm_g,
              b_norm_g, b_w_q, b_q_norm_g, b_lambda, b_subln_g, b_w_o,
              mlp_norm_g, mlp_w_in, mlp_w_out):
    B, S, D = x.shape
    L = S + N_META
    pad = (-L) % BLOCK_Q
    meta = jnp.broadcast_to(meta_tokens.astype(x.dtype)[None], (B, N_META, D))
    h = jnp.concatenate([meta, x, jnp.zeros((B, pad, D), x.dtype)], axis=1)
    T = L + pad
    cos, sin = rope_tables(T)

    shared = None
    for layer in range(DEPTH):
        if layer < N_A_LAYERS:
            i = layer
            hn = rmsnorm(h, a_norm_g[i])
            qkv = (hn @ a_w_qkv[i]).reshape(B, T, 3, SB_HEADS, SB_HEAD_DIM)
            q = qkv[:, :, 0].transpose(0, 2, 1, 3)
            k = qkv[:, :, 1].transpose(0, 2, 1, 3)
            v = qkv[:, :, 2].transpose(0, 2, 1, 3)
            o = stick_breaking_attention(q, k, v)
            h = h + merge_heads(o) @ a_w_o[i]
        else:
            j = layer - N_A_LAYERS
            if shared is None:
                kvn = rmsnorm(h, kv_norm_g)
                kv = kvn @ kv_w
                kk = kv[..., :DIFF_HEADS * 2 * DIFF_QK_DIM].reshape(B, T, DIFF_HEADS, 2, DIFF_QK_DIM)
                k1 = apply_partial_rope(rmsnorm(kk[..., 0, :], kv_k_norm_g[0]), cos, sin)
                k2 = apply_partial_rope(rmsnorm(kk[..., 1, :], kv_k_norm_g[1]), cos, sin)
                vv = kv[..., DIFF_HEADS * 2 * DIFF_QK_DIM:].reshape(B, T, DIFF_HEADS, DIFF_V_DIM)
                shared = (k1.transpose(0, 2, 1, 3), k2.transpose(0, 2, 1, 3), vv.transpose(0, 2, 1, 3))
            k1, k2, vv = shared
            lam_init = 0.8 - 0.6 * math.exp(-0.3 * layer)
            lp = b_lambda[j].astype(jnp.float32)
            lam = jnp.exp(jnp.sum(lp[0] * lp[1])) - jnp.exp(jnp.sum(lp[2] * lp[3])) + lam_init
            hn = rmsnorm(h, b_norm_g[j])
            qq = (hn @ b_w_q[j]).reshape(B, T, DIFF_HEADS, 2, DIFF_QK_DIM)
            q1 = apply_partial_rope(rmsnorm(qq[..., 0, :], b_q_norm_g[j, 0]), cos, sin)
            q2 = apply_partial_rope(rmsnorm(qq[..., 1, :], b_q_norm_g[j, 1]), cos, sin)
            o = differential_attention(q1.transpose(0, 2, 1, 3), q2.transpose(0, 2, 1, 3), k1, k2, vv, lam)
            o = rmsnorm(o, b_subln_g[j]) * (1.0 - lam_init)
            h = h + merge_heads(o).astype(h.dtype) @ b_w_o[j]
        h = h + squared_relu_mlp(h, mlp_norm_g[layer], mlp_w_in[layer], mlp_w_out[layer])

    return h[:, N_META:N_META + S]


DEPTH_2 = 1


ATT_HEADS = 8
ATT_HEAD_DIM = 64
ATT_WIDTH = ATT_HEADS * ATT_HEAD_DIM
Q_BLOCK = 128

HGRN_HEADS = 8
HGRN_K = 128
HGRN_V = 128
HGRN_KEY_WIDTH = HGRN_HEADS * HGRN_K
HGRN_WIDTH = HGRN_HEADS * HGRN_V
HGRN_CHUNK = 64

N_GROUPS = 4
EXPERTS_PER_GROUP = 8
N_EXPERTS = N_GROUPS * EXPERTS_PER_GROUP
TOP_K = 2
EXPERT_FF = 512
MOE_BLOCK = 128

IN_SIZES = (ATT_WIDTH, ATT_WIDTH, ATT_WIDTH, ATT_HEADS, HGRN_KEY_WIDTH, HGRN_KEY_WIDTH, HGRN_WIDTH, HGRN_WIDTH, D_MODEL, D_MODEL)
IN_WIDTH = sum(IN_SIZES)


def split_points(sizes):
    pts, acc = [], 0
    for s in sizes[:-1]:
        acc += s
        pts.append(acc)
    return pts

def rms_norm(x, w):
    xf = x.astype(jnp.float32)
    y = xf * lax.rsqrt(jnp.mean(xf * xf, axis=-1, keepdims=True) + EPS)
    return (y * w.astype(jnp.float32)).astype(x.dtype)

def forgetting_attention(q, k, v, log_f):
    B, L, H, Dh = q.shape
    scale = Dh ** -0.5
    c = jnp.cumsum(log_f, axis=1)
    c_k = jnp.transpose(c, (0, 2, 1))

    def attend(q_blk, c_q, q_pos, k_blk, v_blk, c_kb, k_pos):
        s = jnp.einsum('bqhd,bkhd->bhqk', q_blk, k_blk).astype(jnp.float32) * scale
        s = s + jnp.transpose(c_q, (0, 2, 1))[..., :, None] - c_kb[:, :, None, :]
        mask = k_pos[None, :] <= q_pos[:, None]
        s = jnp.where(mask[None, None], s, -jnp.inf)
        p = jax.nn.softmax(s, axis=-1).astype(v_blk.dtype)
        return jnp.einsum('bhqk,bkhd->bqhd', p, v_blk)

    meta_pos = jnp.arange(N_META)
    o_meta = attend(q[:, :N_META], c[:, :N_META], meta_pos, k[:, :N_META], v[:, :N_META], c_k[:, :, :N_META], meta_pos)

    n_blk = (L - N_META) // Q_BLOCK
    k_pos = jnp.arange(L)

    def real_block(i):
        start = N_META + i * Q_BLOCK
        q_blk = lax.dynamic_slice_in_dim(q, start, Q_BLOCK, axis=1)
        c_q = lax.dynamic_slice_in_dim(c, start, Q_BLOCK, axis=1)
        q_pos = start + jnp.arange(Q_BLOCK)
        return attend(q_blk, c_q, q_pos, k, v, c_k, k_pos)

    o_real = lax.map(real_block, jnp.arange(n_blk))
    o_real = jnp.moveaxis(o_real, 0, 1).reshape(B, n_blk * Q_BLOCK, H, Dh)
    return jnp.concatenate([o_meta, o_real], axis=1)

def hgrn2_chunk(state, chunk):
    q, log_f, k, v = chunk
    C = q.shape[1]
    b = jnp.cumsum(log_f, axis=1)
    o_inter = jnp.einsum('bchk,bhkv->bchv', q * jnp.exp(b), state)
    causal = jnp.tril(jnp.ones((C, C), dtype=bool))
    diff = b[:, :, None] - b[:, None, :]
    decay = jnp.exp(jnp.where(causal[None, :, :, None, None], diff, -jnp.inf))
    scores = jnp.sum(q[:, :, None] * k[:, None] * decay, axis=-1)
    o_intra = jnp.einsum('btsh,bshv->bthv', scores, v)
    b_last = b[:, -1]
    k_dec = k * jnp.exp(b_last[:, None] - b)
    new_state = jnp.exp(b_last)[..., None] * state + jnp.einsum('bshk,bshv->bhkv', k_dec, v)
    return new_state, o_inter + o_intra

def hgrn2_recurrence(q, log_f, k, v):
    B, L, H, K = q.shape
    V = v.shape[-1]
    state0 = jnp.zeros((B, H, K, V), jnp.float32)
    state1, o_meta = hgrn2_chunk(state0, (q[:, :N_META], log_f[:, :N_META], k[:, :N_META], v[:, :N_META]))
    n_chunks = (L - N_META) // HGRN_CHUNK

    def to_chunks(a):
        return jnp.moveaxis(a[:, N_META:].reshape(B, n_chunks, HGRN_CHUNK, H, a.shape[-1]), 1, 0)

    _, o_real = lax.scan(hgrn2_chunk, state1, (to_chunks(q), to_chunks(log_f), to_chunks(k), to_chunks(v)))
    o_real = jnp.moveaxis(o_real, 0, 1).reshape(B, L - N_META, H, V)
    return jnp.concatenate([o_meta, o_real], axis=1)

def hierarchical_moe(v2d, w_rg, b_rg, w_re, b_re, w_e_in, w_e_out):
    T, D = v2d.shape
    dtype = v2d.dtype
    vf = v2d.astype(jnp.float32)
    g_logits = vf @ w_rg.astype(jnp.float32) + b_rg.astype(jnp.float32)
    g_prob = jax.nn.softmax(g_logits, axis=-1)
    g_idx = jnp.argmax(g_logits, axis=-1)
    p_g = jnp.take_along_axis(g_prob, g_idx[:, None], axis=1)[:, 0]
    e_logits = (vf @ w_re.astype(jnp.float32) + b_re.astype(jnp.float32)).reshape(T, N_GROUPS, EXPERTS_PER_GROUP)
    e_sel = jnp.take_along_axis(e_logits, g_idx[:, None, None], axis=1)[:, 0]
    top_v, top_i = lax.top_k(e_sel, TOP_K)
    gate = jax.nn.softmax(top_v, axis=-1) * p_g[:, None]
    expert_id = (g_idx[:, None] * EXPERTS_PER_GROUP + top_i).astype(jnp.int32)

    A = T * TOP_K
    eid = expert_id.reshape(-1)
    tok = jnp.repeat(jnp.arange(T, dtype=jnp.int32), TOP_K)
    wt = gate.reshape(-1)
    order = jnp.argsort(eid)
    se, st, sw = eid[order], tok[order], wt[order]
    counts = jnp.bincount(eid, length=N_EXPERTS).astype(jnp.int32)
    starts = jnp.cumsum(counts) - counts
    pcounts = (counts + MOE_BLOCK - 1) // MOE_BLOCK * MOE_BLOCK
    pends = jnp.cumsum(pcounts)
    pstarts = pends - pcounts
    dest = pstarts[se] + jnp.arange(A, dtype=jnp.int32) - starts[se]
    n_blocks = -(-A // MOE_BLOCK) + N_EXPERTS
    rows_tok = jnp.full((n_blocks * MOE_BLOCK,), T, jnp.int32).at[dest].set(st)
    rows_w = jnp.zeros((n_blocks * MOE_BLOCK,), jnp.float32).at[dest].set(sw)
    blk_exp = jnp.clip(jnp.searchsorted(pends, jnp.arange(n_blocks, dtype=jnp.int32) * MOE_BLOCK, side='right'), 0, N_EXPERTS - 1)
    v_pad = jnp.concatenate([v2d, jnp.zeros((1, D), dtype)], axis=0)

    def run(args):
        tok_b, e = args
        xb = v_pad[tok_b]
        hu = xb @ w_e_in[e]
        a, u = jnp.split(hu, 2, axis=-1)
        return (jax.nn.silu(a) * u) @ w_e_out[e]

    ys = lax.map(run, (rows_tok.reshape(n_blocks, MOE_BLOCK), blk_exp)).reshape(-1, D)
    ys = ys * rows_w[:, None].astype(ys.dtype)
    out = jnp.zeros((T + 1, D), ys.dtype).at[rows_tok].add(ys)
    return out[:T].astype(dtype)

def second_inputs(seed: int = 0) -> dict:
    key = jax.random.key(seed)
    ks = jax.random.split(key, 18)
    n = jax.random.normal
    f32 = jnp.float32
    return {
        'x': n(ks[0], (BATCH, SEQ, D_MODEL), f32),
        'meta_tokens': n(ks[1], (N_META, D_MODEL), f32),
        'norm_mix_w': 1.0 + 0.02 * n(ks[2], (DEPTH_2, D_MODEL), f32),
        'w_in': n(ks[3], (DEPTH_2, D_MODEL, IN_WIDTH), f32) * D_MODEL ** -0.5,
        'attn_forget_b': 3.0 + 0.5 * n(ks[4], (DEPTH_2, ATT_HEADS), f32),
        'hgrn_lb_logits': 0.1 * n(ks[5], (DEPTH_2 + 1, HGRN_KEY_WIDTH), f32),
        'hgrn_norm_w': 1.0 + 0.02 * n(ks[6], (DEPTH_2, HGRN_V), f32),
        'w_attn_out': n(ks[7], (DEPTH_2, ATT_WIDTH, D_MODEL), f32) * ATT_WIDTH ** -0.5,
        'w_hgrn_out': n(ks[8], (DEPTH_2, HGRN_WIDTH, D_MODEL), f32) * HGRN_WIDTH ** -0.5,
        'w_o': n(ks[9], (DEPTH_2, D_MODEL, D_MODEL), f32) * D_MODEL ** -0.5,
        'norm_ffn_w': 1.0 + 0.02 * n(ks[10], (DEPTH_2, D_MODEL), f32),
        'w_router_group': n(ks[11], (DEPTH_2, D_MODEL, N_GROUPS), f32) * D_MODEL ** -0.5,
        'b_router_group': 0.01 * n(ks[12], (DEPTH_2, N_GROUPS), f32),
        'w_router_expert': n(ks[13], (DEPTH_2, D_MODEL, N_EXPERTS), f32) * D_MODEL ** -0.5,
        'b_router_expert': 0.01 * n(ks[14], (DEPTH_2, N_EXPERTS), f32),
        'w_expert_in': n(ks[15], (DEPTH_2, N_EXPERTS, D_MODEL, 2 * EXPERT_FF), f32) * D_MODEL ** -0.5,
        'w_expert_out': n(ks[16], (DEPTH_2, N_EXPERTS, EXPERT_FF, D_MODEL), f32) * EXPERT_FF ** -0.5,
        'norm_final_w': 1.0 + 0.02 * n(ks[17], (D_MODEL,), f32),
    }

def second_block(x, meta_tokens, norm_mix_w, w_in, attn_forget_b, hgrn_lb_logits, hgrn_norm_w, w_attn_out, w_hgrn_out, w_o, norm_ffn_w, w_router_group, b_router_group, w_router_expert, b_router_expert, w_expert_in, w_expert_out, norm_final_w):
    B, S, D = x.shape
    L = S + N_META
    meta = jnp.broadcast_to(meta_tokens.astype(x.dtype)[None], (B, N_META, D))
    h = jnp.concatenate([meta, x], axis=1)
    lb_all = jnp.cumsum(jax.nn.softmax(hgrn_lb_logits.astype(jnp.float32), axis=0), axis=0)
    for layer in range(DEPTH_2):
        u = rms_norm(h, norm_mix_w[layer])
        proj = u @ w_in[layer]
        q_a, k_a, v_a, f_a, q_h, f_h, i_h, g_h, gate_a, gate_h = jnp.split(proj, split_points(IN_SIZES), axis=-1)

        log_f_a = jax.nn.log_sigmoid(f_a.astype(jnp.float32) + attn_forget_b[layer].astype(jnp.float32))
        att_shape = (B, L, ATT_HEADS, ATT_HEAD_DIM)
        o_a = forgetting_attention(q_a.reshape(att_shape), k_a.reshape(att_shape), v_a.reshape(att_shape), log_f_a)
        y_a = o_a.reshape(B, L, ATT_WIDTH) @ w_attn_out[layer]

        lb = lb_all[layer]
        f_val = lb + (1.0 - lb) * jax.nn.sigmoid(f_h.astype(jnp.float32))
        key_shape = (B, L, HGRN_HEADS, HGRN_K)
        log_f_h = jnp.log(f_val).reshape(key_shape)
        k_h = (1.0 - f_val).reshape(key_shape)
        q_hr = q_h.astype(jnp.float32).reshape(key_shape) * HGRN_K ** -0.5
        v_h = i_h.astype(jnp.float32).reshape(B, L, HGRN_HEADS, HGRN_V)
        o_h = hgrn2_recurrence(q_hr, log_f_h, k_h, v_h)
        o_h = rms_norm(o_h, hgrn_norm_w[layer]) * jax.nn.sigmoid(g_h.astype(jnp.float32)).reshape(B, L, HGRN_HEADS, HGRN_V)
        y_h = o_h.reshape(B, L, HGRN_WIDTH).astype(x.dtype) @ w_hgrn_out[layer]

        mixed = jax.nn.sigmoid(gate_a) * y_a + jax.nn.sigmoid(gate_h) * y_h
        h = h + mixed @ w_o[layer]

        v_in = rms_norm(h, norm_ffn_w[layer]).reshape(B * L, D)
        moe_out = hierarchical_moe(v_in, w_router_group[layer], b_router_group[layer], w_router_expert[layer], b_router_expert[layer], w_expert_in[layer], w_expert_out[layer])
        h = h + moe_out.reshape(B, L, D)
    return rms_norm(h, norm_final_w)[:, N_META:]


def setup_inputs(seed=0):
    out = dict(first_inputs(seed))
    for name, value in second_inputs(seed + 1).items():
        if name != "x":
            out[name + "_2"] = value
    return out


def reference(
    x, meta_tokens, a_norm_g, a_w_qkv, a_w_o, kv_norm_g, kv_w, kv_k_norm_g, b_norm_g, b_w_q,
    b_q_norm_g, b_lambda, b_subln_g, b_w_o, mlp_norm_g, mlp_w_in, mlp_w_out, meta_tokens_2,
    norm_mix_w_2, w_in_2, attn_forget_b_2, hgrn_lb_logits_2, hgrn_norm_w_2, w_attn_out_2,
    w_hgrn_out_2, w_o_2, norm_ffn_w_2, w_router_group_2, b_router_group_2, w_router_expert_2,
    b_router_expert_2, w_expert_in_2, w_expert_out_2, norm_final_w_2,
):
    x = first_block(
        x, meta_tokens, a_norm_g, a_w_qkv, a_w_o, kv_norm_g, kv_w, kv_k_norm_g, b_norm_g, b_w_q,
        b_q_norm_g, b_lambda, b_subln_g, b_w_o, mlp_norm_g, mlp_w_in, mlp_w_out,
    )
    return second_block(
        x, meta_tokens_2, norm_mix_w_2, w_in_2, attn_forget_b_2, hgrn_lb_logits_2,
        hgrn_norm_w_2, w_attn_out_2, w_hgrn_out_2, w_o_2, norm_ffn_w_2, w_router_group_2,
        b_router_group_2, w_router_expert_2, b_router_expert_2, w_expert_in_2, w_expert_out_2,
        norm_final_w_2,
    )


_drawn_inputs = setup_inputs


def setup_inputs(seed=0):
    import zlib

    import numpy as np

    out = dict(_drawn_inputs(seed))
    spreads = {}
    factors = {'kv_k_norm_g': 3.336,
     'b_norm_g': 3.814,
     'b_q_norm_g': 3.225,
     'meta_tokens_2': 4.107,
     'norm_mix_w_2': 5.606,
     'attn_forget_b_2': 2.866,
     'hgrn_lb_logits_2': 3.952,
     'hgrn_norm_w_2': 8.0,
     'norm_ffn_w_2': 4.145,
     'b_router_group_2': 8.0,
     'b_router_expert_2': 7.438,
     'norm_final_w_2': 2.861}
    for name, (base, spread) in spreads.items():
        noise = np.random.default_rng([zlib.crc32(name.encode()), seed]).standard_normal(out[name].shape)
        drawn = base * np.exp(spread * noise) if base else spread * noise
        out[name] = jnp.asarray(drawn.astype(out[name].dtype))
    for name, factor in factors.items():
        out[name] = (out[name] * factor).astype(out[name].dtype)
    return out
```

```python
import numpy as np
import concourse.bass as bass
from concourse import mybir
from contextlib import ExitStack

F32 = mybir.dt.float32
F32R = mybir.dt.float32r
I32 = mybir.dt.int32
U32 = mybir.dt.uint32
ALU = mybir.AluOpType
ACT = mybir.ActivationFunctionType
AX = mybir.AxisListType

P = 128
D = 1024
KC = D // P
META = 16
SEQ = 512
T = META + SEQ
TH = T // 2
NT = 5
TAIL = T - 4 * P
TP = NT * P
HD = 64
EPS = 1e-6
RING = 16
MLP_STEPS = 16
NEG = -1e30
LEVELS = 7
EXPERTS, EFF, SLOTS = 32, 512, 128
GROUPS, PER_GROUP = 4, 8
ROUTES = GROUPS + EXPERTS
BLOCKS_IN_ALL = EXPERTS * SEQ // SLOTS
LAM_INIT = 0.8 - 0.6 * float(np.exp(-0.3))
QG = 7 * KC
G0 = 4

SP_A = 3 * P + NT * TAIL
SP_B = 7 * P


class Steps:

    def __init__(self, eng, sem):
        self.eng, self.sem, self.base, self.per, self.at, self.k = eng, sem, 0, 0, 0, 0

    def body(self, i, per):
        self.per, self.at, self.k = per, self.base + i * per, 0

    def end(self, count):
        assert self.k == self.per, (self.k, self.per)
        self.base += self.per * count
        self.at, self.k, self.per = self.base, 0, 0

    def mark(self, ins):
        ins.then_inc(self.sem, 1)
        self.k += 1
        if not self.per:
            self.base += 1
            self.at, self.k = self.base, 0
        return self.at + self.k

    def done(self, ins):
        self.eng.wait_ge(self.sem, self.mark(ins))


def repeat(eng, first, last, body):
    if last - first > 1:
        with eng.Fori(first, last) as i:
            body(i)
    elif last > first:
        body(first)


def build(nc, a):
    top = ExitStack()

    def sb(name, shape, dt=F32, ctx=top):
        return ctx.enter_context(nc.sbuf_tensor(name, shape, dt))

    def sem(name):
        return top.enter_context(nc.semaphore(name))

    psG = top.enter_context(nc.psum_tensor("psG", [P, 4, 512], F32))
    psA = top.enter_context(nc.psum_tensor("psA", [P, 4, 512], F32))

    h = sb("h", [P, KC, T])
    con = sb("con", [P, 4 * P])
    gains = sb("gains", [P, a["gains"].shape[1]])
    N_r = sb("N_r", [P, T])
    N_t = sb("N_t", [P, T])
    stat = sb("stat", [P, 2, 8])
    lam = sb("lam", [P, 4])
    ident, ones, neg_tri, neg_ones = (con[:, i * P:(i + 1) * P] for i in range(4))

    pr = ExitStack()
    raw = sb("raw", [P, 2, RING * P], ctx=pr)
    whi = sb("whi", [P, 2, RING * P], F32R, ctx=pr)
    wlo = sb("wlo", [P, 2, RING * P], F32R, ctx=pr)
    xhi = sb("xhi", [P, KC, T], F32R, ctx=pr)
    xlo = sb("xlo", [P, KC, T], F32R, ctx=pr)

    pa = ExitStack()
    A_o = sb("A_o", [P, KC, T], ctx=pa)
    A_q = sb("A_q", [P, 2, T], ctx=pa)
    A_k = sb("A_k", [P, 2, TP], ctx=pa)
    A_v = sb("A_v", [P, T], ctx=pa)
    A_vt = sb("A_vt", [P, 2, NT, P], ctx=pa)
    A_t = sb("A_t", [P, SP_A + SP_B], ctx=pa)
    A_sp = sb("A_sp", [P, SP_A + SP_B], ctx=pa)
    A_w = sb("A_w", [P, SP_A + SP_B], ctx=pa)
    pa.close()
    pn = ExitStack()
    N_sq = sb("N_sq", [P, KC, T], ctx=pn)
    pn.close()
    pb = ExitStack()
    B_o = sb("B_o", [P, KC, T], ctx=pb)
    B_q = sb("B_q", [P, KC, SEQ], ctx=pb)
    B_k = sb("B_k", [P, 2, T], ctx=pb)
    B_qs = sb("B_qs", [P, 2, SEQ], ctx=pb)
    B_v = sb("B_v", [P, T], ctx=pb)
    B_vt = sb("B_vt", [P, 2, NT, P], ctx=pb)
    B_raw = sb("B_raw", [P, 2, T], ctx=pb)
    B_sq = sb("B_sq", [P, T], ctx=pb)
    B_r = sb("B_r", [P, T], ctx=pb)
    B_t = sb("B_t", [P, 2, T], ctx=pb)
    B_con = sb("B_con", [P, 3 * P + 2 * T], ctx=pb)
    B_p = sb("B_p", [P, 2, 2, T], ctx=pb)
    B_w = sb("B_w", [P, T], ctx=pb)
    B_wt = sb("B_wt", [P, NT, P], ctx=pb)
    B_lam = sb("B_lam", [P, 4 * HD], ctx=pb)
    pb.close()
    head_ones, rotate, future = (B_con[:, i * P:(i + 1) * P] for i in range(3))
    cosine, sine = (B_con[:, 3 * P + i * T:3 * P + (i + 1) * T] for i in range(2))
    pc = ExitStack()
    C_hold = sb("C_hold", [P, KC, T], ctx=pc)
    C_con = sb("C_con", [P, 9 * P + T], ctx=pc)
    C_oa = sb("C_oa", [P, 4, SEQ], ctx=pc)
    C_oh = sb("C_oh", [P, KC, SEQ], ctx=pc)
    C_lb = sb("C_lb", [P, 5, KC], ctx=pc)
    pf = ExitStack()
    F_w = sb("F_w", [P, KC, KC], ctx=pf)
    F_q = sb("F_q", [P, T], ctx=pf)
    F_k = sb("F_k", [P, T], ctx=pf)
    F_v = sb("F_v", [P, T], ctx=pf)
    F_vt = sb("F_vt", [P, NT, P], ctx=pf)
    F_p = sb("F_p", [P, 2, T], ctx=pf)
    F_wt = sb("F_wt", [P, NT, P], ctx=pf)
    F_g = sb("F_g", [KC, 3, T], ctx=pf)
    F_row = sb("F_row", [1, KC * T], ctx=pf)
    pf.close()
    ph = ExitStack()
    R_q = sb("R_q", [P, SEQ], ctx=ph)
    R_qb = sb("R_qb", [P, SEQ], ctx=ph)
    R_k = sb("R_k", [P, T], ctx=ph)
    R_l = sb("R_l", [P, T], ctx=ph)
    R_s = sb("R_s", [P, T], ctx=ph)
    R_b = sb("R_b", [P, T], ctx=ph)
    R_v = sb("R_v", [P, T], ctx=ph)
    R_gl = sb("R_gl", [P, SEQ], ctx=ph)
    R_g = sb("R_g", [P, SEQ], ctx=ph)
    R_kd = sb("R_kd", [P, T], ctx=ph)
    R_eb = sb("R_eb", [P, SEQ], ctx=ph)
    R_d = sb("R_d", [P, NT], ctx=ph)
    R_x = sb("R_x", [P, LEVELS, SEQ], ctx=ph)
    R_m = sb("R_m", [P, LEVELS + 1, P], ctx=ph)
    R_at = sb("R_at", [P, 4, P], ctx=ph)
    R_vt = sb("R_vt", [P, NT, P], ctx=ph)
    R_kt = sb("R_kt", [P, NT, P], ctx=ph)
    R_S = sb("R_S", [P, 4, P], ctx=ph)
    R_sq = sb("R_sq", [P, SEQ], ctx=ph)
    R_r = sb("R_r", [P, SEQ], ctx=ph)
    R_t = sb("R_t", [P, SEQ], ctx=ph)
    ph.close()
    px = ExitStack()
    X_ah = sb("X_ah", [P, 4, SEQ], F32R, ctx=px)
    X_al = sb("X_al", [P, 4, SEQ], F32R, ctx=px)
    X_hh = sb("X_hh", [P, KC, SEQ], F32R, ctx=px)
    X_hl = sb("X_hl", [P, KC, SEQ], F32R, ctx=px)
    X_t = sb("X_t", [P, 2, SEQ], ctx=px)
    px.close()
    pc.close()
    X_m = C_hold[:, :, 0:SEQ]
    level_masks, future2 = C_con[:, 0:8 * P].rearrange("p (l n) -> p l n", l=8), C_con[:, 8 * P:9 * P]
    resets = C_con[:, 9 * P:9 * P + T]
    pm = ExitStack()
    M_r = sb("M_r", [P, 2, T], ctx=pm)
    M_t = sb("M_t", [P, 2, T], ctx=pm)
    M_hi = sb("M_hi", [P, 2, 2, T], F32R, ctx=pm)
    M_lo = sb("M_lo", [P, 2, 2, T], F32R, ctx=pm)
    pm.close()
    pr.close()
    E_win = sb("E_win", [P, 2, KC, D])
    E_S = sb("E_S", [P, 4, SLOTS], F32R)
    E_x = sb("E_x", [P, KC, SLOTS])
    E_l = sb("E_l", [P, EFF])
    E_s = sb("E_s", [P, EFF])
    E_hid = sb("E_hid", [P, EFF])
    E_y = sb("E_y", [P, D])
    E_con = sb("E_con", [P, 2 * P])
    E_hold = sb("E_hold", [P, KC, T])
    E_hT = sb("E_hT", [P, 4, SLOTS])
    E_wout = sb("E_wout", [P, 2, 4, D])
    E_vhi = sb("E_vhi", [P, 4, D], F32R)
    E_vlo = sb("E_vlo", [P, 4, D], F32R)
    E_h = sb("E_h", [P, 4, D])
    E_wr = sb("E_wr", [P, KC, ROUTES])
    E_br = sb("E_br", [1, ROUTES])
    E_lg = sb("E_lg", [P, 4, ROUTES])
    E_t = sb("E_t", [P, 4, EXPERTS])
    E_M = sb("E_M", [P, 3, 4, EXPERTS])
    E_sel = sb("E_sel", [P, 4, PER_GROUP])
    E_c = sb("E_c", [P, 4, PER_GROUP])
    E_oh = sb("E_oh", [P, 3, 4, PER_GROUP])
    E_mx = sb("E_mx", [P, 4, 4])
    E_e = sb("E_e", [P, 20])
    E_g = sb("E_g", [P, 4, 4])
    E_pos = sb("E_pos", [P, 8])
    E_idx = sb("E_idx", [P, 8], U32)
    E_rel = sb("E_rel", [P, 8])
    E_cnt = sb("E_cnt", [P, 2])
    E_flag = sb("E_flag", [P, 1], I32)
    y_rows = nc.dram_tensor("y_rows", (EXPERTS * SEQ, D), F32).ap()
    slot_of = E_con[:, 0:P]
    first_row = E_con[:, P:2 * P]

    s_con = sem("constants_loaded")
    s_h = sem("hidden_loaded")
    s_out = sem("output_stored")
    w_loaded = [sem(f"weights_loaded{s}") for s in range(2)]
    w_high = [sem(f"weights_high{s}") for s in range(2)]
    w_split = [sem(f"weights_split{s}") for s in range(2)]
    g_done = sem("product_done")
    s_phase = sem("phase_over")
    act_own, dve_own, pool_own = sem("act_steps"), sem("dve_steps"), sem("pool_steps")
    n_sq, n_sum, n_r0, n_t, n_hi, n_lo = (sem(f"norm_{x}") for x in ("squares", "sums", "root", "scaled", "high", "low"))
    a_stage, a_vt, a_z, a_abs, a_sp, a_spm, a_cum, a_w, a_wm, a_o, a_free = (
        sem(f"stick_{x}") for x in ("staged", "vt", "scores", "softplus_log", "softplus", "masked", "summed",
                                    "weights", "weights_masked", "outputs", "free"))
    a_begun = sem("stick_masks_begun")
    o_hi, o_lo = sem("attn_high"), sem("attn_low")
    m_r, m_t, m_hi, m_lo = (sem(f"mlp_{x}") for x in ("relu", "square", "high", "low"))
    r_add = sem("residual_added")
    b_con, b_lam = sem("diff_constants"), sem("diff_lambda")
    b_raw, b_sq, b_ss, b_root, b_t, b_rot, b_rope = (
        sem(f"diff_{x}") for x in ("raw", "squares", "sums", "root", "scaled", "rotated", "roped"))
    b_v, b_vt, b_qs, b_s, b_max, b_exp, b_w, b_T, b_wt, b_pv, b_o = (
        sem(f"diff_{x}") for x in ("v", "v_turned", "queries_staged", "scores", "max", "exp", "weights", "turned", "turned_read",
                                   "outputs", "outputs_read"))
    l_sq, l_ss, l_root, l_t, l_hi, l_lo = (sem(f"subln_{x}") for x in ("squares", "sums", "root", "scaled", "high", "low"))

    c_con, c_gate, c_lb = sem("block2_constants"), sem("forget_gates"), sem("lower_bounds")
    f_sig, f_cum, f_row, f_stage, f_vT, f_vt, f_s, f_max, f_exp, f_w, f_T, f_wt, f_pv, f_o = (
        sem(f"forget_{x}") for x in ("softplus", "sums", "row", "staged", "v_turned", "v", "scores", "max", "exp",
                                     "weights", "turned", "turned_read", "outputs", "outputs_read"))
    r_q, r_fl, r_fm, r_sig, r_fv, r_lf, r_b, r_v, r_gl, r_gm, r_gs, r_d, r_eb, r_ex, r_kd, r_x = (
        sem(f"hgrn_{x}") for x in ("q", "f_log", "f_minus", "f_sigmoid", "f_values", "log_f", "sums", "v", "g_log",
                                   "g_minus", "g_sigmoid", "differences", "decays", "level_decays", "k_decayed",
                                   "levels"))
    r_vT, r_kT, r_kvs, r_U, r_S, r_sc, r_A, r_at, r_o, r_sq, r_ss, r_r, r_end = (
        sem(f"hgrn_{x}") for x in ("v_turned", "k_turned", "turned_read", "updates", "states", "scores", "masked",
                                   "matrix", "outputs", "squares", "norm_sums", "root", "head_over"))
    x_hi, x_lo, x_l, x_m, x_s, x_end, y_hi, y_lo = (
        sem(f"mix_{x}") for x in ("high", "low", "log", "minus", "sigmoid", "over", "mixed_high", "mixed_low"))

    e_con, e_lg, e_d, e_x, e_m, e_rank, e_route, e_vhi, e_vlo, e_ht, e_tr = (
        sem(f"route_{x}") for x in ("constants", "logits", "differences", "exponentials", "chosen", "ranks", "rows",
                                    "v_high", "v_low", "h_turned", "turned"))
    e_lgd = sem("route_logits_read")
    e_win, e_wout = ([sem(f"expert_w_{x}{s}") for s in range(2)] for x in ("in", "out"))
    e_S, e_gath, e_xT, e_in, e_l, e_min, e_sig, e_hid, e_hT, e_hTs, e_out, e_y, y_stored, e_prod, e_add, e_newton = (
        sem(f"expert_{x}") for x in ("slots", "gathered", "inputs", "hidden", "log", "minus", "sigmoid", "gated",
                                     "turned", "turned_read", "product", "outputs", "stored", "silu", "added", "newton"))
    e_rows, e_acc, e_sq, e_rr, e_fin = (sem(f"final_{x}") for x in ("rows", "added", "squares", "root", "normed"))

    STREAM = [("a_qkv", 16, (16, 8)), ("a_o", 4, 16), ("mlp0", 32, 16), ("b_q", 4, 16), ("b_kv", 8, 16), ("b_o", 4, 16),
              ("mlp1", 32, 16), ("c_f", 8, (16, 8)), ("c_h", 16, 16), ("c_mix", 16, (12, 16)), ("c_o", 4, 16)]
    FIRST = {}
    n = 0
    for name, blocks, tiles in STREAM:
        FIRST[name] = n
        n += blocks
    TILES = {name: tiles if isinstance(tiles, tuple) else (tiles, tiles) for name, _, tiles in STREAM}
    BLOCKS = {name: blocks for name, blocks, _ in STREAM}
    NEXT = {x[0]: y[0] for x, y in zip(STREAM, STREAM[1:])}
    GC = 400

    block = top.enter_context(nc.Block())

    def use(name, i, s):
        return FIRST[name] // 2 + i

    def experts(eng, step):
        step(0, 0, 0, 0, first=True)
        step(1, 1, 1, 0)

        def two(i):
            step(2 * i, 2 * i, 0, i)
            step(2 * i + 1, 2 * i + 1, 1, i)
        repeat(eng, 1, EXPERTS // 2, two)
        overflow(eng, lambda k, i, s: step(EXPERTS * k + 2 * i + s, 2 * i + s, s, EXPERTS // 2 * k + i))

    def overflow(eng, step):
        eng.wait_ge(e_route, 1)
        more = eng.value_load(E_flag[0:1, 0:1], min_val=0, max_val=1)
        with eng.If(more > 0):
            with eng.Fori(1, SEQ // SLOTS) as k:
                with eng.Fori(0, EXPERTS // 2) as i:
                    step(k, i, 0)
                    step(k, i, 1)

    @block.sync
    def _(sp):
        sp.dma_start(con[:, :], a["con"]).then_inc(s_con, 16)
        sp.dma_start(gains[:, :], a["gains"]).then_inc(s_con, 16)
        sp.dma_start(h[:, :, :], a["h"]).then_inc(s_h, 16)
        for name, blocks, _ in STREAM:
            src = a["w_" + name]
            def load(i, s, first=False):
                if not first:
                    sp.wait_ge(w_split[s], use(name, i, s))
                n = TILES[name][s] * P
                sp.dma_start(raw[:, s, 0:n],
                             src[bass.ds(2 * i + s, 1), :, 0:n].rearrange("a p n -> p (a n)")).then_inc(w_loaded[s], 16)
            start = 0
            if FIRST[name] == 0:
                load(0, 0, True)
                load(0, 1, True)
                start = 1
            def body(i):
                load(i, 0)
                load(i, 1)
            repeat(sp, start, blocks // 2, body)
        sp.wait_ge(s_phase, 4 * 7)
        def expert(n, e, s, first=False):
            if not first:
                sp.wait_ge(e_in, n - 1)
            sp.dma_start(E_win[:, s, :, :].rearrange("p k n -> p (k n)"),
                         a["w_ein"][bass.ds(e, 1)].rearrange("a p n -> p (a n)")).then_inc(e_win[s], 16)
            if not first:
                sp.wait_ge(e_out, n - 1)
            sp.dma_start(E_wout[:, s, :, :].rearrange("p k n -> p (k n)"),
                         a["w_eout"][bass.ds(e, 1)].rearrange("a p n -> p (a n)")).then_inc(e_wout[s], 16)
        expert(0, 0, 0, True)
        expert(1, 1, 1, True)

        def two(i):
            expert(2 * i, 2 * i, 0)
            expert(2 * i + 1, 2 * i + 1, 1)
        repeat(sp, 1, EXPERTS // 2, two)
        overflow(sp, lambda k, i, s: expert(EXPERTS * k + 2 * i + s, 2 * i + s, s))
        for t in range(4):
            sp.wait_ge(e_fin, t + 1)
            sp.dma_start(a["out"][t * P:(t + 1) * P, :], E_win[:, 1, t, :]).then_inc(s_out, 16)
        sp.wait_ge(s_out, 64)

    @block.tensor
    def _(pe):
        tiles_before = 0
        pe.sem_inc(g_done, G0)
        phases = 0

        def product(par, wslot, k0, xh, xl, tok, ks=KC, bank=None):
            halves = [(0, tok)] if tok <= 512 else [(0, tok // 2), (tok // 2, tok)]
            for b, (lo, hi) in enumerate(halves):
                out = psG[:, (2 * par if bank is None else bank) + b, 0:hi - lo]
                for k in range(ks):
                    wt = slice((k0 + k) * P, (k0 + k + 1) * P)
                    pe.matmul(out, whi[:, wslot, wt], xh[:, k, lo:hi], start=(k == 0), stop=False)
                    pe.matmul(out, whi[:, wslot, wt], xl[:, k, lo:hi], start=False, stop=False)
                    mm = pe.matmul(out, wlo[:, wslot, wt], xh[:, k, lo:hi], start=False, stop=(k == ks - 1))
            mm.then_inc(g_done, 1)

        def over():
            nonlocal phases
            phases += 1
            pe.drain().then_inc(s_phase, 1)
            pe.wait_ge(s_phase, 4 * phases)

        norms = 0

        def norm_sums(cols):
            nonlocal norms
            width = cols[1] - cols[0]
            halves = [(0, width)] if width <= 512 else [(0, width // 2), (width // 2, width)]
            for c in range(KC):
                pe.wait_ge(n_sq, norms * KC + c + 1)
                for b, (lo, hi) in enumerate(halves):
                    mm = pe.matmul(psA[:, b, 0:hi - lo], ones, N_sq[:, c, cols[0] + lo:cols[0] + hi],
                                   start=(c == 0), stop=(c == KC - 1), skip_group_check=True)
            mm.then_inc(n_sum, 1)
            norms += 1

        pe.wait_ge(s_con, 32)
        norm_sums((0, T))
        pe.wait_ge(n_lo, KC)


        def qkv(i, s, j, first=False):
            p = 2 * i + s
            if j != 1:
                pe.wait_ge(w_split[j // 2], use("a_qkv", p, 0) + 1)
            if j == 0 and not first:
                pe.wait_ge(a_stage, 3 * p)
            if j == 1 and not first:
                pe.wait_ge(a_vt, p)
            if j == 2:
                pe.wait_ge(a_stage, 3 * p + 1)
            product(j % 2, j // 2, (j % 2) * KC, xhi, xlo, T)

        def vt(i, s):
            par = 1
            pe.wait_ge(a_stage, 3 * (2 * i + s) + 3)
            for c in range(NT):
                w = P if c < 4 else TAIL
                mm = pe.transpose(psG[0:w, 2 * par + c // 4, (c % 4) * P:(c % 4) * P + P],
                                  A_v[:, c * P:c * P + w], ident)
            mm.then_inc(g_done, 1)

        def scores(i, s, hh, first=False):
            n = 4 * i + 2 * s + hh
            rows = slice(HD * hh, HD * hh + HD)
            q, k = A_q[rows, s, :], A_k[rows, s, :]
            if not first:
                pe.wait_ge(a_free, n)
            if hh == 0:
                pe.wait_ge(a_stage, 3 * (2 * i + s) + 3)
                pe.wait_ge(a_vt, 2 * i + s + 1)

            def z(bank, col, c, q0, q1, start=False):
                return pe.matmul(psA[:, bank, col:col + q1 - q0], k[:, c * P:c * P + P], q[:, q0:q1],
                                 start=start, stop=False, skip_group_check=True)
            z(0, 0, 0, 0, 256, True)
            z(0, 256, 1, 128, 256)
            for c in range(NT):
                mm = z(0, 384 + TAIL * c, c, 512, T)
            mm.then_inc(a_z, 1)
            z(1, 0, 0, 256, 512, True)
            z(1, 256, 1, 256, 512)
            z(2, 0, 2, 256, 512, True)
            z(2, 256, 3, 384, 512).then_inc(a_z, 1)

        def sums(i, s, hh):
            n = 4 * i + 2 * s + hh

            def take(bank, c0, c1, tri, src):
                return pe.matmul(psA[:, bank, c0:c1], tri, src, start=False, stop=False, skip_group_check=True)
            pe.wait_ge(a_spm, 2 * n + 1)
            take(0, 0, SP_A, neg_tri, A_sp[:, 0:SP_A])
            take(0, 128, 256, neg_ones, A_sp[:, 256:384])
            for c in range(1, NT):
                src = A_sp[:, 384 + TAIL * c:384 + TAIL * (c + 1)].rearrange("p (a n) -> p a n", a=1)
                mm = take(0, 384, 384 + TAIL * c, neg_ones, src.broadcast_to([P, c, TAIL]))
            mm.then_inc(a_cum, 1)
            pe.wait_ge(a_spm, 2 * n + 2)
            B = SP_A
            take(1, 0, 512, neg_tri, A_sp[:, B:B + 512])
            take(2, 0, 384, neg_tri, A_sp[:, B + 512:B + 896])
            take(1, 0, 256, neg_ones, A_sp[:, B + 256:B + 512])
            src = A_sp[:, B + 512:B + 768].rearrange("p (a n) -> p a n", a=1)
            take(1, 0, 512, neg_ones, src.broadcast_to([P, 2, 256]))
            src = A_sp[:, B + 768:B + 896].rearrange("p (a n) -> p a n", a=1)
            pe.matmul(psA[:, 1, :].rearrange("p (a n) -> p a n", a=2)[:, :, 128:256], neg_ones,
                      src.broadcast_to([P, 2, 128]), start=False, stop=False, skip_group_check=True)
            take(2, 128, 256, neg_ones, A_sp[:, B + 768:B + 896]).then_inc(a_cum, 1)

        def values(i, s, hh):
            n = 4 * i + 2 * s + hh
            rows = slice(HD * hh, HD * hh + HD)

            def pv(out, c, src, start=False, keys=P):
                return pe.matmul(out, A_vt[0:keys, s, c, rows], src[0:keys], start=start, stop=False,
                                 skip_group_check=True)
            o, B = psA[rows, 3, :], SP_A
            pe.wait_ge(a_wm, 2 * n + 1)
            pv(o[:, 0:256], 0, A_w[:, 0:256], True)
            pv(o[:, 128:256], 1, A_w[:, 256:384])
            for c in range(NT):
                keys = P if c < 4 else TAIL
                pv(psA[rows, 0, SP_A:SP_A + TAIL], c, A_w[:, 384 + TAIL * c:384 + TAIL * (c + 1)], keys=keys)
            pe.wait_ge(a_wm, 2 * n + 2)
            for c in range(3):
                pv(o[:, 256:512], c, A_w[:, B + 256 * c:B + 256 * c + 256])
            pv(o[:, 384:512], 3, A_w[:, B + 768:B + 896]).then_inc(a_o, 1)

        def pair(i, s, more=True, first=False):
            ni, ns = (i, 1) if s == 0 else (i + 1, 0)
            for hh in range(2):
                scores(i, s, hh, first=first and hh == 0)
                if more:
                    qkv(ni, ns, 2 * hh)
                sums(i, s, hh)
                if more and hh == 0:
                    qkv(ni, ns, 1)
                if more and hh == 1:
                    vt(ni, ns)
                values(i, s, hh)

        for j in range(3):
            qkv(0, 0, j, first=True)
        vt(0, 0)

        def both(i):
            pair(i, 0)
            pair(i, 1)
        pair(0, 0, first=True)
        pair(0, 1)
        repeat(pe, 1, 3, both)
        pair(3, 0)
        pair(3, 1, more=False)

        def project(name, tok, r0):
            for b in range(4):
                i, s = b // 2, b % 2
                pe.wait_ge(w_split[s], use(name, i, s) + 1)
                for j in range(2):
                    if b:
                        pe.wait_ge(r_add, r0 + 2 * b + j - 1)
                    product(j, s, j * KC, xhi[:, :, T - tok:], xlo[:, :, T - tok:], tok)

        pe.wait_ge(o_lo, KC)
        project("a_o", T, 0)
        over()
        norm_sums((0, T))
        pe.wait_ge(n_lo, 2 * KC)

        def mlp(name, tok, before, r0):
            xh, xl = xhi[:, :, T - tok:], xlo[:, :, T - tok:]

            def into(s):
                for j in range(2):
                    product(j, s, j * KC, xh, xl, tok)

            def step(j, buf, last=False, first=False):
                if not last:
                    pe.wait_ge(w_split[1], FIRST[name] // 2 + j + 1)
                    if first:
                        pe.wait_ge(m_r, before + 2)
                    else:
                        pe.wait_ge(r_add, r0 + KC * j)
                    into(1)
                s = 1 if last else 0
                pe.wait_ge(w_split[s], FIRST[name] // 2 + j + (1 if last else 2))
                pe.wait_ge(m_lo, before + 2 * j + 2)
                for m in range(KC):
                    if m < 2 and not last:
                        pe.wait_ge(m_r, before + 2 * j + 3 + m)
                    else:
                        pe.wait_ge(r_add, r0 + KC * j + m - 1)
                    product(m % 2, s, 2 * m, M_hi[:, buf, :, 0:tok], M_lo[:, buf, :, 0:tok], tok, ks=2)

            pe.wait_ge(w_split[0], FIRST[name] // 2 + 1)
            into(0)
            step(0, 0, first=True)
            step(1, 1)

            def two(i):
                step(2 * i, 0)
                step(2 * i + 1, 1)
            repeat(pe, 1, 7, two)
            step(14, 0)
            step(15, 1, last=True)
        mlp("mlp0", T, 0, 8)
        over()

        def product_q(m):
            i, s = m // 4, (m // 2) % 2
            if m % 2 == 0:
                pe.wait_ge(w_split[s], use("b_q", i, s) + 1)
            if m >= 2:
                pe.wait_ge(b_sq, m - 1)
            product(m % 2, s, (m % 2) * KC, xhi[:, :, META:], xlo[:, :, META:], SEQ)

        def halves_of(tok):
            return [(0, tok)] if tok <= 512 else [(0, tok // 2), (tok // 2, tok)]

        def head_sums(n, ps, tok):
            pe.wait_ge(b_sq, n + 1)
            for b, (lo, hi) in enumerate(halves_of(tok)):
                mm = pe.matmul(ps[:, b, 0:hi - lo], head_ones, B_sq[:, lo:hi], start=True, stop=True)
            mm.then_inc(b_ss, 1)

        def head_rotation(n, ps, tok, par):
            pe.wait_ge(b_t, n + 1)
            for b, (lo, hi) in enumerate(halves_of(tok)):
                mm = pe.matmul(ps[:, b, 0:hi - lo], rotate, B_t[:, par, lo:hi], start=True, stop=True)
            mm.then_inc(b_rot, 1)

        norm_sums((0, T))
        pe.wait_ge(n_lo, 3 * KC)
        pe.wait_ge(b_con, 32)
        for m in range(KC + 2):
            if m < KC:
                product_q(m)
            if 1 <= m <= KC:
                if m >= 2:
                    pe.wait_ge(b_t, m - 1)
                head_sums(m - 1, psA[:, 0:1, :], SEQ)
            if m >= 2:
                if m >= 3:
                    pe.wait_ge(b_rope, m - 2)
                head_rotation(m - 2, psA[:, 2:3, :], SEQ, m % 2)

        def kv_k(i, s):
            if not isinstance(i, int) or 2 * i + s > 0:
                pe.wait_ge(b_rope, KC + 2 * i + s)
            pe.wait_ge(w_split[s], use("b_kv", i, s) + 1)
            product(0, s, 0, xhi, xlo, T)

        def kv_v(i, s):
            n = 2 * i + s
            pe.wait_ge(b_t, KC + n + 1)
            product(0, s, KC, xhi, xlo, T)

        def kv_vt(i, s):
            n = 2 * i + s
            pe.wait_ge(b_v, n + 1)
            for c in range(NT):
                w = P if c < 4 else TAIL
                mm = pe.transpose(psG[0:w, c // 4, (c % 4) * P:(c % 4) * P + P], B_v[:, c * P:c * P + w], ident)
            mm.then_inc(g_done, 1)

        def kv_rot(i, s):
            n = 2 * i + s
            pe.wait_ge(b_vt, n + 1)
            head_rotation(KC + n, psG[:, 0:2, :], T, s)

        def s_qi(i, s, qi, first=False):
            u = 4 * (2 * i + s) + qi
            L = META + P * (qi + 1)
            if qi == 0:
                pe.wait_ge(b_rope, KC + 2 * i + s + 1)
                pe.wait_ge(b_qs, 2 * i + s + 1)
            if not first:
                pe.wait_ge(b_exp, 2 * u)
            for m in range(2):
                rows = slice(HD * m, HD * m + HD)
                for b, (lo, hi) in enumerate(halves_of(L)):
                    pe.matmul(psA[:, 2 * m + b, 0:hi - lo], B_qs[rows, s, qi * P:(qi + 1) * P], B_k[rows, s, lo:hi],
                              start=True, stop=(hi < L))
                    if hi == L:
                        mm = pe.matmul(psA[:, 2 * m + b, hi - lo - P:hi - lo], ident, future, start=False, stop=True)
            mm.then_inc(b_s, 1)

        def t_qi(i, s, qi, first=False):
            u = 4 * (2 * i + s) + qi
            pe.wait_ge(b_w, u + 1)
            if not first:
                pe.wait_ge(b_wt, u)
                pe.wait_ge(b_o, u)
            for c in range(qi + 2):
                w = P if c <= qi else TAIL
                mm = pe.transpose(psG[0:w, 2 + c // 4, (c % 4) * P:(c % 4) * P + P], B_w[:, c * P:c * P + w], ident)
            mm.then_inc(b_T, 1)

        def v_qi(i, s, qi):
            u = 4 * (2 * i + s) + qi
            pe.wait_ge(b_wt, u + 1)
            if qi == 0:
                pe.wait_ge(b_vt, 2 * i + s + 1)
            for c in range(qi + 2):
                w = P if c <= qi else TAIL
                mm = pe.matmul(psG[:, 3, 128:256], B_vt[0:w, s, c, :], B_wt[0:w, c, :], start=(c == 0), stop=(c == qi + 1),
                               skip_group_check=True)
            mm.then_inc(b_pv, 1)

        def head(i, s, more=True, first=False):
            ni, ns = (i, 1) if s == 0 else (i + 1, 0)
            s_qi(i, s, 0, first)
            if more:
                kv_k(ni, ns)
            s_qi(i, s, 1)
            t_qi(i, s, 0, first)
            v_qi(i, s, 0)
            if more:
                pe.wait_ge(b_sq, KC + 2 * ni + ns + 1)
                head_sums(KC + 2 * ni + ns, psG[:, 0:2, :], T)
                kv_v(ni, ns)
            s_qi(i, s, 2)
            t_qi(i, s, 1)
            v_qi(i, s, 1)
            if more:
                kv_vt(ni, ns)
            s_qi(i, s, 3)
            t_qi(i, s, 2)
            v_qi(i, s, 2)
            if more:
                kv_rot(ni, ns)
            t_qi(i, s, 3)
            v_qi(i, s, 3)

        pe.wait_ge(n_lo, 4 * KC)
        kv_k(0, 0)
        pe.wait_ge(b_sq, KC + 1)
        head_sums(KC, psG[:, 0:2, :], T)
        kv_v(0, 0)
        kv_vt(0, 0)
        kv_rot(0, 0)

        def heads(i):
            head(i, 0)
            head(i, 1)
        head(0, 0, first=True)
        head(0, 1)
        repeat(pe, 1, 3, heads)
        head(3, 0)
        head(3, 1, more=False)
        for n in range(KC):
            pe.wait_ge(l_sq, n + 1)
            if n >= 4:
                pe.wait_ge(l_t, n - 3)
            pe.matmul(psA[:, n % 4, :], ones, B_t[:, n % 2, 0:SEQ], start=True, stop=True).then_inc(l_ss, 1)
        pe.wait_ge(l_lo, KC)
        project("b_o", SEQ, 136)
        over()
        norm_sums((META, T))
        pe.wait_ge(n_lo, 5 * KC)
        mlp("mlp1", SEQ, 32, 144)
        over()

        norm_sums((0, T))
        pe.wait_ge(n_lo, 6 * KC)
        for b in range(2):
            for c in range(KC):
                mm = pe.matmul(psA[0:KC, b, 0:TH], F_w[:, c, :], N_sq[:, c, b * TH:(b + 1) * TH],
                               start=(c == 0), stop=(c == KC - 1))
        mm.then_inc(c_gate, 1)

        def f_scores(p, hh, qi, first=False):
            u = 8 * p + 4 * hh + qi
            L, bank, rows = META + P * (qi + 1), 2 * (qi % 2), slice(HD * hh, HD * hh + HD)
            if not first:
                pe.wait_ge(f_exp, u - 1)
            for b, (lo, hi) in enumerate(halves_of(L)):
                pe.matmul(psA[:, bank + b, 0:hi - lo], F_q[rows, META + qi * P:META + (qi + 1) * P], F_k[rows, lo:hi],
                          start=True, stop=False)
                mm = pe.matmul(psA[:, bank + b, 0:hi - lo], ones[0:1, :], F_row[0:1, bass.ds((2 * p + hh) * T + lo, hi - lo)],
                               start=False, stop=(hi < L))
                if hi == L:
                    mm = pe.matmul(psA[:, bank + b, hi - lo - P:hi - lo], ident, future2, start=False, stop=True)
            mm.then_inc(f_s, 1)

        def f_turn(p, hh, qi, first=False):
            u = 8 * p + 4 * hh + qi
            pe.wait_ge(f_w, u + 1)
            if not first:
                pe.wait_ge(f_wt, u)
                pe.wait_ge(f_o, u)
            for c in range(qi + 2):
                w = P if c <= qi else TAIL
                mm = pe.transpose(psG[0:w, 2 + c // 4, (c % 4) * P:(c % 4) * P + P],
                                  F_p[:, qi % 2, c * P:c * P + w], ident)
            mm.then_inc(f_T, 1)
            pe.wait_ge(f_wt, u + 1)
            rows = slice(HD * hh, HD * hh + HD)
            for c in range(qi + 2):
                w = P if c <= qi else TAIL
                mm = pe.matmul(psG[rows, 3, 128:256], F_vt[0:w, c, rows], F_wt[0:w, c, :], start=(c == 0),
                               stop=(c == qi + 1), skip_group_check=True)
            mm.then_inc(f_pv, 1)

        def forget_pair(p, first=False):
            pe.wait_ge(w_split[0], use("c_f", p, 0) + 1)
            if not first:
                pe.wait_ge(f_o, 8 * p)
            product(0, 0, 0, xhi, xlo, T)
            product(1, 0, KC, xhi, xlo, T)
            pe.wait_ge(w_split[1], use("c_f", p, 1) + 1)
            pe.wait_ge(f_stage, 3 * p + 1)
            product(0, 1, 0, xhi, xlo, T)
            pe.wait_ge(f_stage, 3 * p + 3)
            for c in range(NT):
                w = P if c < 4 else TAIL
                mm = pe.transpose(psG[0:w, 2 + c // 4, (c % 4) * P:(c % 4) * P + P], F_v[:, c * P:c * P + w], ident)
            mm.then_inc(f_vT, 1)
            units = [(hh, qi) for hh in range(2) for qi in range(4)]
            f_scores(p, 0, 0, first)
            for k, (hh, qi) in enumerate(units):
                if k < 7:
                    f_scores(p, *units[k + 1], first=first and k < 1)
                if k == 0:
                    pe.wait_ge(f_vt, p + 1)
                f_turn(p, hh, qi, first and k == 0)

        pe.wait_ge(f_row, 16)
        forget_pair(0, True)
        repeat(pe, 1, 4, forget_pair)
        over()

        def hgrn_head(n, first=False):
            g = GC + 12 + 4 * n
            pe.wait_ge(w_split[0], use("c_h", n, 0) + 1)
            if not first:
                pe.wait_ge(r_end, n)
            product(0, 0, 0, xhi[:, :, META:], xlo[:, :, META:], SEQ)
            product(1, 0, KC, xhi, xlo, T)
            pe.wait_ge(w_split[1], use("c_h", n, 1) + 1)
            pe.wait_ge(r_q, n + 1)
            product(0, 1, 0, xhi, xlo, T)
            pe.wait_ge(r_fm, n + 1)
            product(1, 1, KC, xhi[:, :, META:], xlo[:, :, META:], SEQ)
            pe.wait_ge(r_v, n + 1)
            for c in range(1, NT):
                pe.transpose(psG[:, 0, (c - 1) * P:c * P], R_v[:, META + (c - 1) * P:META + c * P], ident)
            pe.transpose(psG[0:META, 1, 0:P], R_v[:, 0:META], ident).then_inc(r_vT, 1)
            pe.wait_ge(r_kd, n + 1)
            for c in range(1, 4):
                pe.transpose(psG[:, 1, c * P:(c + 1) * P], R_kd[:, META + (c - 1) * P:META + c * P], ident)
            pe.transpose(psG[0:META, 3, 0:P], R_kd[:, 0:META], ident).then_inc(r_kT, 1)
            pe.wait_ge(r_kvs, 2 * n + 2)
            for c in range(4):
                w = META if c == 0 else P
                mm = pe.matmul(psA[:, 2, c * P:(c + 1) * P], R_kt[0:w, c, :], R_vt[0:w, c, :], start=(c == 0), stop=(c == 3),
                               skip_group_check=True)
            mm.then_inc(r_U, 1)
            pe.wait_ge(r_x, n + 1)
            for j in range(5):
                if j < 4:
                    if j:
                        pe.wait_ge(r_A, 4 * n + j)
                    t = slice(j * P, (j + 1) * P)
                    for l in range(LEVELS):
                        pe.matmul(psA[:, l // 4, (l % 4) * P:(l % 4 + 1) * P], R_x[:, l, t], R_x[:, l, t],
                                  start=(l % 4 == 0), stop=False, skip_group_check=True)
                    pe.matmul(psA[:, 1, 3 * P:4 * P], R_k[:, META + j * P:META + (j + 1) * P], R_q[:, t],
                              start=False, stop=True, skip_group_check=True).then_inc(r_sc, 1)
                if j:
                    c = j - 1
                    t = slice(c * P, (c + 1) * P)
                    if c == 0:
                        pe.wait_ge(r_S, n + 1)
                    pe.matmul(psA[:, 3, t], R_S[:, c, :], R_qb[:, t], start=(c == 0), stop=False, skip_group_check=True)
                    pe.wait_ge(r_at, 4 * n + c + 1)
                    mm = pe.matmul(psA[:, 3, t], R_vt[:, c + 1, :], R_at[:, c, :], start=False, stop=(c == 3),
                                   skip_group_check=True)
            mm.then_inc(r_o, 1)
            pe.wait_ge(r_sq, n + 1)
            pe.matmul(psA[:, 2, :], ones, R_sq[:, :], start=True, stop=True).then_inc(r_ss, 1)
        hgrn_head(0, True)
        repeat(pe, 1, 8, hgrn_head)
        over()

        def mix(m, first=False):
            pe.wait_ge(w_split[0], use("c_mix", m, 0) + 1)
            if not first:
                pe.wait_ge(x_end, m)
            product(0, 0, 0, xhi[:, :, META:], xlo[:, :, META:], SEQ, bank=0)
            product(0, 0, KC, X_ah, X_al, SEQ, ks=4, bank=2)
            pe.wait_ge(w_split[1], use("c_mix", m, 1) + 1)
            product(0, 1, 0, xhi[:, :, META:], xlo[:, :, META:], SEQ, bank=1)
            product(0, 1, KC, X_hh, X_hl, SEQ, bank=3)
        pe.wait_ge(x_lo, 12)
        mix(0, True)
        repeat(pe, 1, 8, mix)
        pe.wait_ge(y_lo, KC)
        project("c_o", SEQ, 272)
        over()

        norm_sums((META, T))
        pe.wait_ge(n_t, 7 * KC)
        pe.wait_ge(e_con, 48)
        for t in range(4):
            for c in range(KC):
                pe.matmul(psG[:, 3, t * ROUTES:(t + 1) * ROUTES], N_sq[:, c, META + t * P:META + (t + 1) * P], E_wr[:, c, :],
                          start=(t == 0 and c == 0), stop=False, skip_group_check=True)
            mm = pe.matmul(psG[:, 3, t * ROUTES:(t + 1) * ROUTES], ones[0:1, :], E_br[0:1, :], start=False, stop=(t == 3),
                           skip_group_check=True)
        mm.then_inc(e_lg, 1)
        for t in range(4):
            b = 2 * (t % 2)
            if t == 1:
                pe.wait_ge(e_lgd, 1)
            if t >= 2:
                pe.wait_ge(e_ht, t - 1)
                pe.wait_ge(e_vlo, t - 1)
            tok = slice(META + t * P, META + (t + 1) * P)
            for c in range(KC):
                pe.transpose(psG[:, b + c // 4, (c % 4) * P:(c % 4 + 1) * P], h[:, c, tok], ident)
            for c in range(KC):
                mm = pe.transpose(psA[:, b + c // 4, (c % 4) * P:(c % 4 + 1) * P], N_sq[:, c, tok], ident)
            mm.then_inc(e_tr, 1)
        pe.wait_ge(e_m, 1)
        pe.wait_ge(e_ht, 4)
        for t in range(4):
            out = psG[:, 0, t * EXPERTS:(t + 1) * EXPERTS]
            for u in range(t + 1):
                pe.matmul(out, ones, E_M[:, 2, u, :], start=(t == 0), stop=False, skip_group_check=True)
            pe.matmul(out, neg_tri, E_M[:, 2, t, :], start=False, stop=False, skip_group_check=True)
        for u in range(4):
            mm = pe.matmul(psG[:, 0, P:P + EXPERTS], ones, E_M[:, 2, u, :], start=False, stop=(u == 3), skip_group_check=True)
        mm.then_inc(e_rank, 1)
        pe.wait_ge(e_vlo, 4)

        def expert(n, e, s, i, first=False):
            pe.wait_ge(e_S, n + 1)
            if not first:
                pe.wait_ge(e_xT, n)
            for c in range(KC):
                out = psG[:, c // 4, (c % 4) * P:(c % 4 + 1) * P]
                for t in range(4):
                    for v in (E_vhi, E_vlo):
                        mm = pe.matmul(out, v[:, t, c * P:(c + 1) * P], E_S[:, t, :], start=(c % 4 == 0 and t == 0 and v is E_vhi),
                                       stop=False, skip_group_check=True)
            mm.then_inc(e_gath, 1)
            pe.wait_ge(e_xT, n + 1)
            pe.wait_ge(e_win[s], 16 * i + 16)
            if not first:
                pe.wait_ge(e_hid, n)
            for half in range(2):
                for k in range(KC):
                    mm = pe.matmul(psA[:, half, :], E_x[:, k, :], E_win[:, s, k, half * EFF:(half + 1) * EFF],
                                   start=(k == 0), stop=(k == KC - 1))
            mm.then_inc(e_in, 1)
            pe.wait_ge(e_hid, n + 1)
            for k in range(4):
                mm = pe.transpose(psA[:, 2, k * P:(k + 1) * P], E_hid[:, k * P:(k + 1) * P], ident)
            mm.then_inc(e_hT, 1)
            pe.wait_ge(e_hTs, n + 1)
            pe.wait_ge(e_wout[s], 16 * i + 16)
            if not first:
                pe.wait_ge(e_y, 2 * n)
            for half in range(2):
                for k in range(4):
                    mm = pe.matmul(psG[:, 2 + half, :], E_hT[:, k, :], E_wout[:, s, k, half * 512:(half + 1) * 512],
                                   start=(k == 0), stop=(k == 3))
            mm.then_inc(e_out, 1)

        experts(pe, expert)
        over()

    @block.scalar
    def _(act):
        act.preload_act_table_set("natural_log_exp_and_others")
        own = Steps(act, act_own)
        phases = 0

        def over():
            nonlocal phases
            phases += 1
            act.drain().then_inc(s_phase, 1)
            act.wait_ge(s_phase, 4 * phases)

        def high(name, i, s, over):
            tiles = TILES[name][s]
            act.wait_ge(w_loaded[s], 16 * use(name, i, s) + 16)
            if over is not None:
                act.wait_ge(g_done, G0 + over)
            act.activation(whi[:, s, 0:tiles * P], raw[:, s, 0:tiles * P], ACT.Copy).then_inc(w_high[s], 1)

        roots = scalings = 0

        def norm_root(cols):
            nonlocal roots
            width = cols[1] - cols[0]
            halves = 1 if width <= 512 else 2
            for c in range(KC):
                act.activation(N_sq[:, c, cols[0]:cols[1]], h[:, c, cols[0]:cols[1]], ACT.Square).then_inc(n_sq, 1)
            act.wait_ge(n_sum, roots + 1)
            r = N_r[:, cols[0]:cols[1]].rearrange("p (b n) -> p b n", b=halves)
            own.done(act.activation(r, psA[:, 0:halves, 0:width // halves], ACT.Ln, scale=1.0 / D, bias=EPS))
            act.activation(r, r, ACT.Exp, scale=-0.5).then_inc(n_r0, 1)
            roots += 1

        def norm_high(cols):
            nonlocal scalings
            for c in range(KC):
                act.wait_ge(n_t, scalings * KC + c + 1)
                act.activation(xhi[:, c, cols[0]:cols[1]], N_sq[:, c, cols[0]:cols[1]], ACT.Copy).then_inc(n_hi, 1)
            scalings += 1

        act.wait_ge(s_con, 32)
        act.wait_ge(s_h, 16)
        norm_root((0, T))
        norm_high((0, T))

        def stage(i, s, j):
            t = 8 * i + 4 * s + j
            par = j % 2
            act.wait_ge(g_done, G0 + t + 1)
            src = psG[:, 2 * par:2 * par + 2, 0:TH]
            if j == 0:
                dst, scale = A_q[:, s, :], HD ** -0.5
            elif j == 1:
                dst, scale = A_k[:, s, 0:T], 1.0
            else:
                dst, scale = A_v[:, :], 1.0
            act.activation(dst.rearrange("p (b n) -> p b n", b=2), src, ACT.Copy, scale=scale).then_inc(a_stage, 1)

        def exps(n, u):
            c0, c1 = (0, SP_A) if u == 0 else (SP_A, SP_A + SP_B)
            act.wait_ge(a_z, 2 * n + u + 1)
            if u == 0:
                src = psA[:, 0, 0:SP_A]
            else:
                src = psA[:, 1:3, :].rearrange("p b n -> p (b n)")[:, 0:SP_B]
            own.done(act.activation(A_t[:, c0:c1], src, ACT.Abs))
            own.done(act.activation(A_t[:, c0:c1], A_t[:, c0:c1], ACT.Exp, scale=-1.0))
            act.activation(A_t[:, c0:c1], A_t[:, c0:c1], ACT.Ln, bias=1.0).then_inc(a_abs, 1)

        def weights(n, u):
            c0, c1 = (0, SP_A) if u == 0 else (SP_A, SP_A + SP_B)
            act.wait_ge(a_cum, 2 * n + u + 1)
            if u == 0:
                src = psA[:, 0, 0:SP_A]
            else:
                src = psA[:, 1:3, :].rearrange("p b n -> p (b n)")[:, 0:SP_B]
            act.activation(A_w[:, c0:c1], src, ACT.Exp).then_inc(a_w, 1)

        def pair(i, s, more=True, nxt="a_qkv"):
            ni, ns = (i, 1) if s == 0 else (i + 1, 0)
            p = 2 * i + s
            b = p + 2 if nxt == "a_qkv" else 0
            for hh in range(2):
                n = 2 * p + hh
                exps(n, 0)
                exps(n, 1)
                if more:
                    stage(ni, ns, 2 * hh)
                weights(n, 0)
                weights(n, 1)
                if more and hh == 0:
                    stage(ni, ns, 1)
                    high(nxt, b, 0, 4 * p + 6)
                if more and hh == 1:
                    high(nxt, b, 1, 4 * p + 7)

        high("a_qkv", 0, 0, None)
        high("a_qkv", 0, 1, None)
        for j in range(3):
            stage(0, 0, j)
        high("a_qkv", 1, 0, 2)
        high("a_qkv", 1, 1, 3)

        def both(i):
            own.body(i, 16)
            pair(i, 0)
            pair(i, 1)
        repeat(act, 0, 3, both)
        own.end(3)
        own.body(0, 16)
        pair(3, 0, nxt="a_o")
        pair(3, 1, more=False)
        own.end(1)

        act.wait_ge(a_free, 16)
        for c in range(KC):
            act.activation(xhi[:, c, :], A_o[:, c, :], ACT.Copy).then_inc(o_hi, 1)
        high("a_o", 1, 0, 32 + 2)
        high("a_o", 1, 1, 32 + 4)
        high("mlp0", 0, 0, 32 + 6)
        high("mlp0", 0, 1, 32 + 8)
        over()
        norm_root((0, T))
        norm_high((0, T))

        def mlp(name, nxt, tok, before, g0):
            def into(step, at, first=False):
                for j in range(2):
                    act.wait_ge(g_done, G0 + g0 + at + j + 1)
                    if tok > 512:
                        src, dst = psG[:, 2 * j:2 * j + 2, 0:tok // 2], M_r[:, j, 0:tok].rearrange("p (b n) -> p b n", b=2)
                    else:
                        src, dst = psG[:, 2 * j, 0:tok], M_r[:, j, 0:tok]
                    if not first:
                        act.wait_ge(m_t, before + 2 * step + j - 1)
                    act.activation(dst, src, ACT.Relu).then_inc(m_r, 1)

            def highs(step, buf):
                for j in range(2):
                    act.wait_ge(m_t, before + 2 * step + j + 1)
                    act.activation(M_hi[:, buf, j, 0:tok], M_t[:, j, 0:tok], ACT.Copy).then_inc(m_hi, 1)

            into(0, 0, True)
            highs(0, 0)
            high(name, 1, 0, g0 + 2)

            def step(j, buf, nxt0=None):
                g = g0 + 2 + 10 * j
                into(j + 1, 2 + 10 * j)
                highs(j + 1, 1 - buf)
                act_high_at(name, j + 1, 1, g + 2)
                if nxt0 is None:
                    act_high_at(name, j + 2, 0, g + 10)
                else:
                    high(nxt0, 0, 0, g + 10)

            def act_high_at(name, i, s, over):
                high(name, i, s, over)

            def two(i):
                step(2 * i, 0)
                step(2 * i + 1, 1)
            repeat(act, 0, 7, two)
            step(14, 0, nxt)
            high(nxt, 0, 1, g0 + 160)
        mlp("mlp0", NEXT["mlp0"], T, 0, 40)
        over()

        norm_root((0, T))
        norm_high((META, T))

        def fold(x, tok):
            return x.rearrange("p (b n) -> p b n", b=2) if tok > 512 else x

        def bank(pair, tok):
            return psG[:, 2 * pair:2 * pair + 2, 0:tok // 2] if tok > 512 else psG[:, 2 * pair, 0:tok]

        def raw_and_square(n, g, pair, par, tok):
            act.wait_ge(g_done, G0 + g + 1)
            late = not isinstance(n, int)
            if late or n >= 2:
                act.wait_ge(b_t, n - 1)
            act.activation(fold(B_raw[:, par, 0:tok], tok), bank(pair, tok), ACT.Copy).then_inc(b_raw, 1)
            if late or n >= 1:
                act.wait_ge(b_ss, n)
            act.activation(fold(B_sq[:, 0:tok], tok), bank(pair, tok), ACT.Square).then_inc(b_sq, 1)

        def root(n, src, tok):
            act.wait_ge(b_ss, n + 1)
            if not isinstance(n, int) or n >= 1:
                act.wait_ge(b_t, n)
            r = fold(B_r[:, 0:tok], tok)
            own.done(act.activation(r, src, ACT.Ln, scale=1.0 / HD, bias=EPS))
            act.activation(r, r, ACT.Exp, scale=-0.5).then_inc(b_root, 1)

        act.wait_ge(b_lam, 1)
        act.activation(lam[:, 0:2], lam[:, 0:2], ACT.Exp).then_inc(b_lam, 1)
        for m in range(KC + 1):
            if m < KC:
                raw_and_square(m, 200 + m, m % 2, m % 2, SEQ)
            if m >= 1:
                root(m - 1, psA[:, 0, :], SEQ)
            if m in (1, 3):
                high("b_q", 1, m // 2, 200 + m + 1)
            if m in (5, 7):
                high("b_kv", 0, (m - 5) // 2, 200 + m + 1)
        norm_high((0, T))

        GK = 208

        def exps(i, s, qi, first=False):
            u = 4 * (2 * i + s) + qi
            par, L = qi % 2, META + P * (qi + 1)
            act.wait_ge(b_max, u + 1)
            if not (first and qi < 2):
                act.wait_ge(b_w, u - 1)
            for m in range(2):
                if L > 512:
                    src, dst = psA[:, 2 * m:2 * m + 2, 0:L // 2], B_p[:, par, m, 0:L].rearrange("p (b n) -> p b n", b=2)
                else:
                    src, dst = psA[:, 2 * m, 0:L], B_p[:, par, m, 0:L]
                act.activation(dst, src, ACT.Exp, scale=HD ** -0.5, bias=stat[:, par, 2 + m:3 + m],
                               accum_out=stat[:, par, 4 + m:5 + m]).then_inc(b_exp, 1)

        def turned(i, s, qi, first=False):
            u = 4 * (2 * i + s) + qi
            act.wait_ge(b_T, u + 1)
            if not (first and qi == 0):
                act.wait_ge(b_pv, u)
            n = min(qi + 1, 4)
            act.activation(B_wt[:, 0:n, :].rearrange("p c n -> p (c n)"), psG[:, 2, 0:n * P], ACT.Copy)
            c = qi + 1
            act.activation(B_wt[0:TAIL, c, :], psG[0:TAIL, 2 + c // 4, (c % 4) * P:(c % 4) * P + P], ACT.Copy)\
                .then_inc(b_wt, 1)

        def key(i, s):
            n = 2 * i + s
            raw_and_square(KC + n, GK + 3 * n, 0, s, T)

        def key_root(i, s):
            root(KC + 2 * i + s, psG[:, 0:2, 0:TH], T)

        def value(i, s):
            n = 2 * i + s
            act.wait_ge(g_done, G0 + GK + 3 * n + 2)
            act.activation(fold(B_v[:, :], T), bank(0, T), ACT.Copy).then_inc(b_v, 1)

        def head(i, s, nxt, more=True, first=False):
            ni, ns = (i, 1) if s == 0 else (i + 1, 0)
            exps(i, s, 0, first)
            if more:
                key(ni, ns)
            turned(i, s, 0, first)
            exps(i, s, 1, first)
            if more:
                key_root(ni, ns)
                value(ni, ns)
            turned(i, s, 1)
            exps(i, s, 2)
            nxt()
            turned(i, s, 2)
            exps(i, s, 3)
            turned(i, s, 3)

        key(0, 0)
        key_root(0, 0)
        value(0, 0)
        own.body(0, 2)
        head(0, 0, lambda: high("b_kv", 1, 0, GK + 2), first=True)
        head(0, 1, lambda: high("b_kv", 1, 1, GK + 5))
        own.end(1)

        def heads(i):
            own.body(i - 1, 2)
            head(i, 0, lambda: high("b_kv", i + 1, 0, GK + 6 * i + 2))
            head(i, 1, lambda: high("b_kv", i + 1, 1, GK + 6 * i + 5))
        repeat(act, 1, 3, heads)
        own.end(2)
        own.body(0, 1)
        head(3, 0, lambda: high("b_o", 0, 0, GK + 20))
        head(3, 1, lambda: high("b_o", 0, 1, GK + 23), more=False)
        own.end(1)

        for n in range(KC + 1):
            if n < KC:
                if n == 0:
                    act.wait_ge(b_o, 32)
                else:
                    act.wait_ge(l_ss, n)
                if n >= 2:
                    act.wait_ge(l_ss, n - 1)
                act.activation(B_t[:, n % 2, 0:SEQ], B_o[:, n, 0:SEQ], ACT.Square).then_inc(l_sq, 1)
                act.wait_ge(l_ss, n + 1)
                if n >= 2:
                    act.wait_ge(l_t, n - 1)
                r = B_raw[:, n % 2, 0:SEQ]
                own.done(act.activation(r, psA[:, n % 4, :], ACT.Ln, scale=1.0 / P, bias=EPS))
                act.activation(r, r, ACT.Exp, scale=-0.5).then_inc(l_root, 1)
            if n >= 1:
                act.wait_ge(l_t, n)
                act.activation(xhi[:, n - 1, META:], B_p[:, (n - 1) % 2, 0, 0:SEQ], ACT.Copy).then_inc(l_hi, 1)
        GO = 232
        high("b_o", 1, 0, GO + 2)
        high("b_o", 1, 1, GO + 4)
        high("mlp1", 0, 0, GO + 6)
        high("mlp1", 0, 1, GO + 8)
        over()
        norm_root((META, T))
        norm_high((META, T))
        mlp("mlp1", NEXT["mlp1"], SEQ, 32, GO + 8)
        over()

        act.wait_ge(c_con, 64)
        norm_root((0, T))
        norm_high((0, T))
        act.wait_ge(c_lb, 1)
        act.activation(C_lb[:, 0:2, :], C_lb[:, 0:2, :], ACT.Exp).then_inc(c_lb, 1)

        def softplus_log(dst, src, step=True):
            own.done(act.activation(dst, src, ACT.Abs))
            own.done(act.activation(dst, dst, ACT.Exp, scale=-1.0))
            return act.activation(dst, dst, ACT.Ln, bias=1.0)

        act.wait_ge(c_gate, 1)
        fold2 = lambda x: x.rearrange("p (b n) -> p b n", b=2)
        own.done(act.activation(fold2(F_g[:, 0, :]), psA[0:KC, 0:2, 0:TH], ACT.Identity, bias=gains[0:KC, QG + 3:QG + 4]))
        softplus_log(F_g[:, 1, :], F_g[:, 0, :]).then_inc(f_sig, 1)

        def forget_exp(p, hh, qi, first=False):
            u = 8 * p + 4 * hh + qi
            par, L = qi % 2, META + P * (qi + 1)
            act.wait_ge(f_max, u + 1)
            if not (first and hh == 0 and qi < 2):
                act.wait_ge(f_T, u - 1)
            if L > 512:
                src, dst = psA[:, 2 * par:2 * par + 2, 0:L // 2], fold2(F_p[:, par, 0:L])
            else:
                src, dst = psA[:, 2 * par, 0:L], F_p[:, par, 0:L]
            act.activation(dst, src, ACT.Exp, bias=stat[:, par, 1:2], accum_out=stat[:, par, 2:3]).then_inc(f_exp, 1)

        def forget_turned(p, hh, qi, first=False):
            u = 8 * p + 4 * hh + qi
            act.wait_ge(f_T, u + 1)
            if not first:
                act.wait_ge(f_pv, u)
            n = min(qi + 1, 4)
            act.activation(F_wt[:, 0:n, :].rearrange("p c n -> p (c n)"), psG[:, 2, 0:n * P], ACT.Copy)
            c = qi + 1
            act.activation(F_wt[0:TAIL, c, :], psG[0:TAIL, 2 + c // 4, (c % 4) * P:(c % 4) * P + P], ACT.Copy)\
                .then_inc(f_wt, 1)

        def forget_pair(p, first=False, nxt=None):
            g = GC + 3 * p
            act.wait_ge(g_done, G0 + g + 1)
            act.activation(fold2(F_q[:, :]), psG[:, 0:2, 0:TH], ACT.Copy, scale=HD ** -0.5).then_inc(f_stage, 1)
            act.wait_ge(g_done, G0 + g + 2)
            act.activation(fold2(F_k[:, :]), psG[:, 2:4, 0:TH], ACT.Copy).then_inc(f_stage, 1)
            act.wait_ge(g_done, G0 + g + 3)
            act.activation(fold2(F_v[:, :]), psG[:, 0:2, 0:TH], ACT.Copy).then_inc(f_stage, 1)
            for hh in range(2):
                for qi in range(4):
                    forget_exp(p, hh, qi, first)
                    if (hh, qi) == (0, 1):
                        high(nxt or "c_f", 0 if nxt else p + 1, 0, g + 2)
                    if (hh, qi) == (1, 1):
                        high(nxt or "c_f", 0 if nxt else p + 1, 1, g + 3)
                    forget_turned(p, hh, qi, first and hh == 0 and qi == 0)
        forget_pair(0, True)
        repeat(act, 1, 3, forget_pair)
        forget_pair(3, nxt="c_h")
        over()

        def hgrn_head(n, nxt=None):
            own.body(n, 5)
            g = GC + 12 + 4 * n
            b = 0 if nxt else n + 1
            act.wait_ge(g_done, G0 + g + 1)
            act.activation(R_q[:, :], psG[:, 0, :], ACT.Copy, scale=P ** -0.5).then_inc(r_q, 1)
            act.wait_ge(g_done, G0 + g + 2)
            softplus_log(fold2(R_l[:, :]), psG[:, 2:4, 0:TH]).then_inc(r_fl, 1)
            act.wait_ge(r_fm, n + 1)
            act.activation(R_s[:, :], R_s[:, :], ACT.Exp).then_inc(r_sig, 1)
            act.wait_ge(g_done, G0 + g + 3)
            act.activation(fold2(R_v[:, :]), psG[:, 0:2, 0:TH], ACT.Copy).then_inc(r_v, 1)
            act.wait_ge(r_fv, n + 1)
            act.activation(R_s[:, :], R_s[:, :], ACT.Ln).then_inc(r_lf, 1)
            act.wait_ge(r_vT, n + 1)
            act.activation(R_vt[:, 1:NT, :].rearrange("p c n -> p (c n)"), psG[:, 0, :], ACT.Copy)
            act.activation(R_vt[0:META, 0, :], psG[0:META, 1, 0:P], ACT.Copy).then_inc(r_kvs, 1)
            act.wait_ge(r_b, n + 1)
            for c in range(4):
                lo, hi = (0, META) if c == 0 else (META + (c - 1) * P, META + c * P)
                act.activation(R_kd[:, lo:hi], R_b[:, lo:hi], ACT.Exp, scale=-1.0, bias=R_b[:, hi - 1:hi])
                act.activation(R_d[:, c:c + 1], R_b[:, hi - 1:hi], ACT.Exp)
            act.activation(R_eb[:, :], R_b[:, META:], ACT.Exp).then_inc(r_eb, 1)
            act.wait_ge(r_d, n + 1)
            act.activation(R_x[:, :, :], R_x[:, :, :], ACT.Exp).then_inc(r_ex, 1)
            act.wait_ge(r_kT, n + 1)
            act.activation(R_kt[:, 1:4, :].rearrange("p c n -> p (c n)"), psG[:, 1, P:], ACT.Copy)
            act.activation(R_kt[0:META, 0, :], psG[0:META, 3, 0:P], ACT.Copy).then_inc(r_kvs, 1)
            act.wait_ge(g_done, G0 + g + 4)
            softplus_log(R_gl[:, :], psG[:, 2, :]).then_inc(r_gl, 1)
            act.wait_ge(r_gm, n + 1)
            act.activation(R_g[:, :], R_g[:, :], ACT.Exp).then_inc(r_gs, 1)
            high(nxt or "c_h", b, 0, g + 2)
            high(nxt or "c_h", b, 1, g + 4)
            act.wait_ge(r_o, n + 1)
            act.activation(R_sq[:, :], psA[:, 3, :], ACT.Square).then_inc(r_sq, 1)
            act.wait_ge(r_ss, n + 1)
            own.done(act.activation(R_r[:, :], psA[:, 2, :], ACT.Ln, scale=1.0 / P, bias=EPS))
            act.activation(R_r[:, :], R_r[:, :], ACT.Exp, scale=-0.5).then_inc(r_r, 1)
        repeat(act, 0, 7, hgrn_head)
        hgrn_head(7, "c_mix")
        own.end(8)
        over()

        for c in range(12):
            dst, src = (X_ah[:, c, :], C_oa[:, c, :]) if c < 4 else (X_hh[:, c - 4, :], C_oh[:, c - 4, :])
            act.activation(dst, src, ACT.Copy).then_inc(x_hi, 1)

        def mix(m, nxt=None):
            own.body(m, 2)
            g = GC + 44 + 4 * m
            b = 0 if nxt else m + 1
            act.wait_ge(g_done, G0 + g + 3)
            if nxt or not isinstance(m, int) or m:
                act.wait_ge(x_end, m)
            softplus_log(X_t[:, :, :], psG[:, 0:2, :]).then_inc(x_l, 1)
            act.wait_ge(x_m, m + 1)
            act.activation(X_t[:, :, :], X_t[:, :, :], ACT.Exp).then_inc(x_s, 1)
            high(nxt or "c_mix", b, 0, g + 2)
            high(nxt or "c_mix", b, 1, g + 4)
        mix(0)
        repeat(act, 1, 7, mix)
        mix(7, "c_o")
        own.end(8)
        for c in range(KC):
            if c == 0:
                act.wait_ge(x_end, KC)
            act.activation(xhi[:, c, META:], X_m[:, c, :], ACT.Copy).then_inc(y_hi, 1)
        GX = GC + 76
        high("c_o", 1, 0, GX + 2)
        high("c_o", 1, 1, GX + 4)
        over()

        norm_root((META, T))
        act.wait_ge(e_d, 1)
        act.activation(E_e[:, :], E_e[:, :], ACT.Exp).then_inc(e_x, 1)
        for t in range(4):
            b = 2 * (t % 2)
            act.wait_ge(e_tr, t + 1)
            act.activation(E_vhi[:, t, :], psA[:, b:b + 2, :].rearrange("p b n -> p (b n)"), ACT.Copy).then_inc(e_vhi, 1)

        def expert(n, e, s, i, first=False):
            own.body(n, 2)
            act.wait_ge(e_gath, n + 1)
            act.activation(E_x[:, :, :].rearrange("p c n -> p (c n)"), psG[:, 0:2, :].rearrange("p b n -> p (b n)"),
                           ACT.Copy).then_inc(e_xT, 1)
            act.wait_ge(e_in, n + 1)
            if not first:
                act.wait_ge(e_hid, n)
            softplus_log(E_l[:, :], psA[:, 0, :]).then_inc(e_l, 1)
            act.wait_ge(e_min, n + 1)
            act.activation(E_s[:, :], E_s[:, :], ACT.Exp).then_inc(e_sig, 1)
            act.wait_ge(e_hT, n + 1)
            act.activation(E_hT[:, :, :].rearrange("p k n -> p (k n)"), psA[:, 2, :], ACT.Copy).then_inc(e_hTs, 1)
            act.wait_ge(e_out, n + 1)
            if not first:
                act.wait_ge(y_stored, 16 * n)
            act.activation(E_y[:, 0:512], psG[:, 2, :], ACT.Copy).then_inc(e_y, 1)
        experts(act, expert)
        over()

        for t in range(4):
            act.wait_ge(e_acc, t + 1)
            act.activation(E_win[:, 1, 4 + t, :], E_h[:, t, :], ACT.Square, accum_out=E_e[:, t:t + 1]).then_inc(e_sq, 1)
        act.wait_ge(e_sq, 4)
        act.activation(E_e[:, 4:8], E_e[:, 0:4], ACT.Ln, scale=1.0 / D, bias=EPS).then_inc(e_rr, 1)
        act.wait_ge(e_rr, 1)
        act.activation(E_e[:, 4:8], E_e[:, 4:8], ACT.Exp, scale=-0.5).then_inc(e_rr, 1)

    @block.vector
    def _(dve):
        own = Steps(dve, dve_own)
        phases = 0

        def over():
            nonlocal phases
            phases += 1
            dve.drain().then_inc(s_phase, 1)
            dve.wait_ge(s_phase, 4 * phases)

        def low(name, i, s):
            tiles = TILES[name][s]
            u = use(name, i, s)
            dve.wait_ge(w_high[s], u + 1)
            dve.tensor_tensor(wlo[:, s, 0:tiles * P], raw[:, s, 0:tiles * P],
                              whi[:, s, 0:tiles * P].bitcast(F32), ALU.subtract).then_inc(w_split[s], 1)

        roots = scalings = 0

        def newton(r, v, t, width):
            own.done(dve.tensor_scalar(t[0], v, -0.5 / width, -0.5 * EPS, ALU.mult, ALU.add))
            own.done(dve.tensor_tensor(t[1], t[1], r, ALU.mult))
            own.done(dve.tensor_tensor(t[1], t[1], r, ALU.mult))
            own.done(dve.scalar_tensor_tensor(out=r, in0=t[1], scalar=1.5, in1=r, op0=ALU.add, op1=ALU.mult))

        def fold(x, tok):
            return x.rearrange("p (b n) -> p b n", b=2) if tok > 512 else x

        def norm_root(cols):
            nonlocal roots
            c0, c1 = cols
            dve.wait_ge(n_r0, roots + 1)
            t = N_t[:, c0:c1]
            v = psA[:, 0:2, 0:(c1 - c0) // 2] if c1 - c0 > 512 else psA[:, 0, 0:c1 - c0]
            newton(N_r[:, c0:c1], v, (fold(t, c1 - c0), t), D)
            roots += 1

        def norm_scale(cols, gain, split=True):
            nonlocal scalings
            c0, c1 = cols
            for c in range(KC):
                dve.scalar_tensor_tensor(out=N_sq[:, c, c0:c1], in0=h[:, c, c0:c1],
                                         scalar=gains[:, gain * KC + c:gain * KC + c + 1], in1=N_r[:, c0:c1],
                                         op0=ALU.mult, op1=ALU.mult).then_inc(n_t, 1)
            for c in range(KC if split else 0):
                dve.wait_ge(n_hi, scalings * KC + c + 1)
                dve.tensor_tensor(xlo[:, c, c0:c1], N_sq[:, c, c0:c1], xhi[:, c, c0:c1].bitcast(F32),
                                  ALU.subtract).then_inc(n_lo, 1)
            scalings += 1

        own.done(dve.memset(A_k[:, :, T:TP], 0.0))
        dve.wait_ge(s_con, 32)
        norm_root((0, T))
        norm_scale((0, T), 0)

        def softplus(n, u):
            c0, c1 = (0, SP_A) if u == 0 else (SP_A, SP_A + SP_B)
            src = psA[:, 0, 0:SP_A] if u == 0 else psA[:, 1:3, :].rearrange("p b n -> p (b n)")[:, 0:SP_B]
            dve.wait_ge(a_abs, 2 * n + u + 1)
            dve.scalar_tensor_tensor(out=A_sp[:, c0:c1], in0=src, scalar=0.0, in1=A_t[:, c0:c1],
                                     op0=ALU.max, op1=ALU.add).then_inc(a_sp, 1)

        def vt(i, s):
            t = 8 * i + 4 * s + 3
            dve.wait_ge(g_done, G0 + t + 1)
            dve.tensor_copy(A_vt[:, s, 0:4, :].rearrange("p c n -> p (c n)"), psG[:, 2, :])
            dve.tensor_copy(A_vt[0:TAIL, s, 4, :], psG[0:TAIL, 3, 0:P]).then_inc(a_vt, 1)

        def outputs(i, s, hh):
            n = 4 * i + 2 * s + hh
            rows = slice(HD * hh, HD * hh + HD)
            dve.wait_ge(a_o, n + 1)
            chunk = A_o[rows, bass.ds(2 * i + s, 1), :].rearrange("p a n -> p (a n)")
            dve.tensor_copy(chunk[:, 0:512], psA[rows, 3, :])
            dve.tensor_copy(chunk[:, 512:T], psA[rows, 0, SP_A:SP_A + TAIL]).then_inc(a_free, 1)

        def pair(i, s, more=True, nxt="a_qkv"):
            ni, ns = (i, 1) if s == 0 else (i + 1, 0)
            p = 2 * i + s
            b = p + 2 if nxt == "a_qkv" else 0
            for hh in range(2):
                n = 2 * p + hh
                softplus(n, 0)
                softplus(n, 1)
                if more and hh == 1:
                    vt(ni, ns)
                outputs(i, s, hh)
                if more:
                    low(nxt, b, hh)

        low("a_qkv", 0, 0)
        low("a_qkv", 0, 1)
        vt(0, 0)
        low("a_qkv", 1, 0)
        low("a_qkv", 1, 1)

        def both(i):
            pair(i, 0)
            pair(i, 1)
        repeat(dve, 0, 3, both)
        pair(3, 0, nxt="a_o")
        pair(3, 1, more=False)

        for c in range(KC):
            dve.wait_ge(o_hi, c + 1)
            dve.tensor_tensor(xlo[:, c, :], A_o[:, c, :], xhi[:, c, :].bitcast(F32), ALU.subtract).then_inc(o_lo, 1)

        def residual(g, m, par, tok):
            dve.wait_ge(g_done, G0 + g + 1)
            hm = h[:, m, T - tok:]
            if tok > 512:
                src, hm = psG[:, 2 * par:2 * par + 2, 0:tok // 2], hm.rearrange("p (b n) -> p b n", b=2)
            else:
                src = psG[:, 2 * par, 0:tok]
            dve.tensor_tensor(hm, hm, src, ALU.add).then_inc(r_add, 1)

        def project(name, nxt, tok, g0):
            for b in range(4):
                for j in range(2):
                    residual(g0 + 2 * b + j, 2 * b + j, j, tok)
                if b < 2:
                    low(name, 1, b)
                elif nxt:
                    low(nxt, 0, b - 2)
        project("a_o", "mlp0", T, 32)
        over()
        norm_root((0, T))
        norm_scale((0, T), 1)

        def mlp(name, nxt, tok, before, g0):
            def into(step, buf, first=False):
                for j in range(2):
                    if not first:
                        dve.wait_ge(m_lo, before + 2 * step + j - 1)
                    dve.wait_ge(m_r, before + 2 * step + j + 1)
                    dve.tensor_tensor(M_t[:, j, 0:tok], M_r[:, j, 0:tok], M_r[:, j, 0:tok], ALU.mult).then_inc(m_t, 1)
                for j in range(2):
                    dve.wait_ge(m_hi, before + 2 * step + j + 1)
                    dve.tensor_tensor(M_lo[:, buf, j, 0:tok], M_t[:, j, 0:tok],
                                      M_hi[:, buf, j, 0:tok].bitcast(F32), ALU.subtract).then_inc(m_lo, 1)

            into(0, 0, first=True)
            low(name, 1, 0)

            def step(j, buf, nxt0=None):
                into(j + 1, 1 - buf)
                low(name, j + 1, 1)
                for m in range(KC):
                    residual(g0 + 4 + 10 * j + m, m, m % 2, tok)
                if nxt0 is None:
                    low(name, j + 2, 0)
                else:
                    low(nxt0, 0, 0)

            def two(i):
                step(2 * i, 0)
                step(2 * i + 1, 1)
            repeat(dve, 0, 7, two)
            step(14, 0, nxt)
            for m in range(KC):
                residual(g0 + 152 + m, m, m % 2, tok)
            low(nxt, 0, 1)
        mlp("mlp0", NEXT["mlp0"], T, 0, 40)
        over()

        norm_root((0, T))
        norm_scale((META, T), 2)
        dve.wait_ge(b_con, 32)
        for m in range(2):
            own.done(dve.tensor_tensor(N_t[:, m * HD:(m + 1) * HD], B_lam[:, 2 * m * HD:(2 * m + 1) * HD],
                                       B_lam[:, (2 * m + 1) * HD:(2 * m + 2) * HD], ALU.mult))
            ins = dve.tensor_reduce(lam[:, m:m + 1], N_t[:, m * HD:(m + 1) * HD], AX.X, ALU.add)
        ins.then_inc(b_lam, 1)

        def scale_head(n, v, tok, par, gain):
            dve.wait_ge(b_root, n + 1)
            if not isinstance(n, int) or n >= 2:
                dve.wait_ge(b_rope, n - 1)
            t = B_t[:, par, 0:tok]
            newton(B_r[:, 0:tok], v, (fold(t, tok), t), HD)
            dve.scalar_tensor_tensor(out=t, in0=B_raw[:, par, 0:tok], scalar=gains[:, gain:gain + 1],
                                     in1=B_r[:, 0:tok], op0=ALU.mult, op1=ALU.mult).then_inc(b_t, 1)

        def rope(n, rot, tok, par, dst):
            dve.wait_ge(b_rot, n + 1)
            t, x, c0 = B_t[:, par, 0:tok], N_t[:, 0:tok], T - tok
            own.mark(dve.tensor_tensor(t, t, cosine[:, c0:], ALU.mult))
            if not isinstance(n, int) or n >= 1:
                dve.wait_ge(b_rope, n)
            own.done(dve.tensor_tensor(fold(x, tok), rot, fold(sine[:, c0:], tok), ALU.mult))
            dve.tensor_tensor(dst, t, x, ALU.add).then_inc(b_rope, 1)

        own.done(dve.memset(stat[:, :, :], 0.0))
        own.done(dve.tensor_scalar(gains[:, QG + 2:QG + 3], gains[:, QG + 2:QG + 3], 1.0 - LAM_INIT,
                                   None, ALU.mult))
        for m in range(KC + 2):
            if 2 <= m:
                rope(m - 2, psA[:, 2, :], SEQ, m % 2, B_q[:, m - 2, :])
            if 1 <= m <= KC:
                scale_head(m - 1, psA[:, 0, :], SEQ, (m - 1) % 2, QG)
            if m in (1, 3):
                low("b_q", 1, m // 2)
            if m in (5, 7):
                low("b_kv", 0, (m - 5) // 2)
        norm_scale((0, T), 3)
        dve.wait_ge(b_lam, 2)
        own.done(dve.tensor_tensor(lam[:, 3:4], lam[:, 1:2], lam[:, 0:1], ALU.subtract))
        own.done(dve.tensor_scalar(lam[:, 2:3], lam[:, 3:4], -LAM_INIT, None, ALU.add))

        GK = 208

        def key_scale(i, s):
            scale_head(KC + 2 * i + s, psG[:, 0:2, 0:TH], T, s, QG + 1)

        def key_rope(i, s):
            if not isinstance(i, int) or 2 * i + s >= 2:
                dve.wait_ge(b_s, 4 * (2 * i + s) - 4)
            rope(KC + 2 * i + s, psG[:, 0:2, 0:TH], T, s, B_k[:, s, :])

        def value(i, s):
            n = 2 * i + s
            dve.wait_ge(g_done, G0 + GK + 3 * n + 3)
            if not isinstance(i, int) or n >= 2:
                dve.wait_ge(b_pv, 4 * n - 4)
            dve.tensor_copy(B_vt[:, s, 0:4, :].rearrange("p c n -> p (c n)"), psG[:, 0, :])
            dve.tensor_copy(B_vt[0:TAIL, s, 4, :], psG[0:TAIL, 1, 0:P]).then_inc(b_vt, 1)

        def maxima(i, s, qi):
            u = 4 * (2 * i + s) + qi
            par, L = qi % 2, META + P * (qi + 1)
            dve.wait_ge(b_s, u + 1)
            for m in range(2):
                if L > 512:
                    own.mark(dve.tensor_reduce(stat[:, par, m:m + 1], psA[:, 2 * m:2 * m + 2, 0:L // 2], AX.XY, ALU.max))
                else:
                    own.mark(dve.tensor_reduce(stat[:, par, m:m + 1], psA[:, 2 * m, 0:L], AX.X, ALU.max))
            dve.wait_ge(dve_own, own.at + own.k)
            dve.tensor_scalar(stat[:, par, 2:4], stat[:, par, 0:2], -(HD ** -0.5), None, ALU.mult).then_inc(b_max, 1)

        def combine(i, s, qi, first=False):
            u = 4 * (2 * i + s) + qi
            par, L = qi % 2, META + P * (qi + 1)
            dve.wait_ge(b_exp, 2 * u + 2)
            own.done(dve.reciprocal(stat[:, par, 6:8], stat[:, par, 4:6]))
            if not (first and qi == 0):
                dve.wait_ge(b_T, u)
            own.done(dve.tensor_scalar(B_w[:, 0:L], B_p[:, par, 1, 0:L], stat[:, par, 7:8], lam[:, 2:3],
                                       ALU.mult, ALU.mult))
            dve.scalar_tensor_tensor(out=B_w[:, 0:L], in0=B_p[:, par, 0, 0:L], scalar=stat[:, par, 6:7],
                                     in1=B_w[:, 0:L], op0=ALU.mult, op1=ALU.add).then_inc(b_w, 1)

        def outputs(i, s, qi):
            u = 4 * (2 * i + s) + qi
            dve.wait_ge(b_pv, u + 1)
            dst = B_o[:, bass.ds(2 * i + s, 1), qi * P:(qi + 1) * P].rearrange("p a n -> p (a n)")
            dve.tensor_copy(dst, psG[:, 3, 128:256]).then_inc(b_o, 1)

        def head(i, s, nxt, more=True, first=False):
            ni, ns = (i, 1) if s == 0 else (i + 1, 0)
            maxima(i, s, 0)
            combine(i, s, 0, first)
            maxima(i, s, 1)
            outputs(i, s, 0)
            if more:
                key_scale(ni, ns)
            combine(i, s, 1)
            maxima(i, s, 2)
            outputs(i, s, 1)
            nxt()
            if more:
                value(ni, ns)
            combine(i, s, 2)
            maxima(i, s, 3)
            outputs(i, s, 2)
            if more:
                key_rope(ni, ns)
            combine(i, s, 3)
            outputs(i, s, 3)

        key_scale(0, 0)
        value(0, 0)
        key_rope(0, 0)
        PER = 4 + 2 + 4 * 4
        own.body(0, 2 * PER)
        head(0, 0, lambda: low("b_kv", 1, 0), first=True)
        head(0, 1, lambda: low("b_kv", 1, 1))
        own.end(1)

        def heads(i):
            own.body(i - 1, 2 * PER)
            head(i, 0, lambda: low("b_kv", i + 1, 0))
            head(i, 1, lambda: low("b_kv", i + 1, 1))
        repeat(dve, 1, 3, heads)
        own.end(2)
        own.body(0, PER + 16)
        head(3, 0, lambda: low("b_o", 0, 0))
        head(3, 1, lambda: low("b_o", 0, 1), more=False)
        own.end(1)

        for n in range(KC + 1):
            if n < KC:
                dve.wait_ge(l_root, n + 1)
                if n >= 2:
                    dve.wait_ge(l_lo, n - 1)
                t = B_p[:, n % 2, 1, 0:SEQ]
                newton(B_raw[:, n % 2, 0:SEQ], psA[:, n % 4, :], (t, t), P)
                dve.scalar_tensor_tensor(out=B_p[:, n % 2, 0, 0:SEQ], in0=B_o[:, n, 0:SEQ],
                                         scalar=gains[:, QG + 2:QG + 3], in1=B_raw[:, n % 2, 0:SEQ],
                                         op0=ALU.mult, op1=ALU.mult).then_inc(l_t, 1)
            if n >= 1:
                dve.wait_ge(l_hi, n)
                dve.tensor_tensor(xlo[:, n - 1, META:], B_p[:, (n - 1) % 2, 0, 0:SEQ],
                                  xhi[:, n - 1, META:].bitcast(F32), ALU.subtract).then_inc(l_lo, 1)
        GO = 232
        project("b_o", "mlp1", SEQ, GO)
        over()
        norm_root((META, T))
        norm_scale((META, T), 4)
        mlp("mlp1", NEXT["mlp1"], SEQ, 32, GO + 8)
        over()

        dve.wait_ge(c_con, 64)
        norm_root((0, T))
        norm_scale((0, T), 5)
        lb0, lb1 = gains[:, QG + 5:QG + 5 + KC], gains[:, QG + 5 + KC:QG + 5 + 2 * KC]
        own.done(dve.tensor_tensor(C_lb[:, 2, :], lb0, lb1, ALU.max))
        own.mark(dve.tensor_tensor(C_lb[:, 0, :], lb0, C_lb[:, 2, :], ALU.subtract))
        dve.tensor_tensor(C_lb[:, 1, :], lb1, C_lb[:, 2, :], ALU.subtract).then_inc(c_lb, 1)
        dve.wait_ge(c_lb, 2)
        own.done(dve.tensor_tensor(C_lb[:, 2, :], C_lb[:, 0, :], C_lb[:, 1, :], ALU.add))
        own.done(dve.reciprocal(C_lb[:, 3, :], C_lb[:, 2, :]))
        own.done(dve.tensor_tensor(C_lb[:, 2, :], C_lb[:, 0, :], C_lb[:, 3, :], ALU.mult))
        own.done(dve.tensor_scalar(C_lb[:, 3, :], C_lb[:, 2, :], -1.0, 1.0, ALU.mult, ALU.add))
        own.done(dve.tensor_scalar(C_lb[:, 4, :], C_lb[:, 3, :], -1.0, None, ALU.mult))
        dve.wait_ge(f_sig, 1)
        own.done(dve.scalar_tensor_tensor(out=F_g[:, 2, :], in0=F_g[:, 0, :], scalar=0.0, in1=F_g[:, 1, :],
                                          op0=ALU.min, op1=ALU.subtract))
        own.done(dve.memset(F_g[:, 1, :], 1.0))
        own.done(dve.tensor_tensor_scan(F_g[:, 0, :], F_g[:, 1, :], F_g[:, 2, :], 0.0, ALU.mult, ALU.add))
        dve.tensor_scalar(F_g[:, 2, :], F_g[:, 0, :], -1.0, None, ALU.mult).then_inc(f_cum, 1)

        def forget_max(p, hh, qi):
            u = 8 * p + 4 * hh + qi
            par, L = qi % 2, META + P * (qi + 1)
            dve.wait_ge(f_s, u + 1)
            if L > 512:
                ins = dve.tensor_reduce(stat[:, par, 0:1], psA[:, 2 * par:2 * par + 2, 0:L // 2], AX.XY, ALU.max)
            else:
                ins = dve.tensor_reduce(stat[:, par, 0:1], psA[:, 2 * par, 0:L], AX.X, ALU.max)
            own.done(ins)
            dve.tensor_scalar(stat[:, par, 1:2], stat[:, par, 0:1], -1.0, None, ALU.mult).then_inc(f_max, 1)

        def forget_weights(p, hh, qi):
            u = 8 * p + 4 * hh + qi
            par, L = qi % 2, META + P * (qi + 1)
            dve.wait_ge(f_exp, u + 1)
            own.done(dve.reciprocal(stat[:, par, 3:4], stat[:, par, 2:3]))
            dve.tensor_scalar(F_p[:, par, 0:L], F_p[:, par, 0:L], stat[:, par, 3:4], None, ALU.mult).then_inc(f_w, 1)

        def forget_out(p, hh, qi):
            u = 8 * p + 4 * hh + qi
            rows = slice(HD * hh, HD * hh + HD)
            dve.wait_ge(f_pv, u + 1)
            dst = C_oa[rows, bass.ds(p, 1), qi * P:(qi + 1) * P].rearrange("p a n -> p (a n)")
            dve.tensor_copy(dst, psG[rows, 3, 128:256]).then_inc(f_o, 1)

        def forget_pair(p, nxt=None):
            own.body(p, 16)
            dve.wait_ge(f_vT, p + 1)
            dve.tensor_copy(F_vt[:, 0:4, :].rearrange("p c n -> p (c n)"), psG[:, 2, :])
            dve.tensor_copy(F_vt[0:TAIL, 4, :], psG[0:TAIL, 3, 0:P]).then_inc(f_vt, 1)
            units = [(hh, qi) for hh in range(2) for qi in range(4)]
            forget_max(p, 0, 0)
            for k, (hh, qi) in enumerate(units):
                forget_weights(p, hh, qi)
                if k < 7:
                    forget_max(p, *units[k + 1])
                if k in (2, 6):
                    low(nxt or "c_f", 0 if nxt else p + 1, k // 4)
                forget_out(p, hh, qi)
        repeat(dve, 0, 3, forget_pair)
        forget_pair(3, "c_h")
        own.end(4)
        over()

        def hgrn_head(n, nxt=None):
            own.body(n, HG)
            b = 0 if nxt else n + 1
            one = lambda row: C_lb[:, row, bass.ds(n, 1)]
            dve.wait_ge(r_fl, n + 1)
            fold2 = lambda x: x.rearrange("p (b n) -> p b n", b=2)
            dve.scalar_tensor_tensor(out=fold2(R_s[:, :]), in0=psG[:, 2:4, 0:TH], scalar=0.0, in1=fold2(R_l[:, :]),
                                     op0=ALU.min, op1=ALU.subtract).then_inc(r_fm, 1)
            dve.wait_ge(r_sig, n + 1)
            own.done(dve.tensor_scalar(R_k[:, :], R_s[:, :], one(4), one(3), ALU.mult, ALU.add))
            dve.tensor_scalar(R_s[:, :], R_s[:, :], one(3), one(2), ALU.mult, ALU.add).then_inc(r_fv, 1)
            dve.wait_ge(r_lf, n + 1)
            dve.tensor_tensor_scan(R_b[:, :], resets, R_s[:, :], 0.0, ALU.mult, ALU.add).then_inc(r_b, 1)
            dve.wait_ge(r_b, n + 1)
            for l in range(LEVELS):
                m = 1 << l
                bv = R_b[:, META:].rearrange("p (g h j) -> p g h j", h=2, j=m)
                xv = R_x[:, l, :].rearrange("p (g h j) -> p g h j", h=2, j=m)
                G = SEQ // (2 * m)
                ref = bv[:, :, 0, m - 1:m].broadcast_to([P, G, m])
                dve.tensor_tensor(xv[:, :, 0, :], ref, bv[:, :, 0, :], ALU.subtract)
                ins = dve.tensor_tensor(xv[:, :, 1, :], bv[:, :, 1, :], ref, ALU.subtract)
            ins.then_inc(r_d, 1)
            dve.wait_ge(r_eb, n + 1)
            dve.tensor_tensor(R_kd[:, 0:META + 3 * P], R_kd[:, 0:META + 3 * P], R_k[:, 0:META + 3 * P], ALU.mult).then_inc(r_kd, 1)
            own.mark(dve.tensor_tensor(R_qb[:, :], R_q[:, :], R_eb[:, :], ALU.mult))
            dve.wait_ge(r_ex, n + 1)
            for l in range(LEVELS):
                m = 1 << l
                view = lambda x: x.rearrange("p (g h j) -> p g h j", h=2, j=m)
                xv, kv, qv = view(R_x[:, l, :]), view(R_k[:, META:]), view(R_q[:, :])
                dve.tensor_tensor(xv[:, :, 0, :], xv[:, :, 0, :], kv[:, :, 0, :], ALU.mult)
                ins = dve.tensor_tensor(xv[:, :, 1, :], xv[:, :, 1, :], qv[:, :, 1, :], ALU.mult)
            ins.then_inc(r_x, 1)
            dve.wait_ge(r_gl, n + 1)
            dve.scalar_tensor_tensor(out=R_g[:, :], in0=psG[:, 2, :], scalar=0.0, in1=R_gl[:, :],
                                     op0=ALU.min, op1=ALU.subtract).then_inc(r_gm, 1)
            dve.wait_ge(r_U, n + 1)
            own.done(dve.tensor_copy(R_S[:, 0, :], psA[:, 2, 0:P]))
            for c in range(1, 4):
                ins = dve.scalar_tensor_tensor(out=R_S[:, c, :], in0=R_S[:, c - 1, :], scalar=R_d[:, c:c + 1],
                                               in1=psA[:, 2, c * P:(c + 1) * P], op0=ALU.mult, op1=ALU.add)
                if c < 3:
                    own.done(ins)
            ins.then_inc(r_S, 1)
            for j in range(4):
                dve.wait_ge(r_sc, 4 * n + j + 1)
                dve.tensor_tensor(R_m[:, :, :], psA[:, 0:2, :].rearrange("p b (l n) -> p (b l) n", l=4), level_masks,
                                  ALU.mult).then_inc(r_A, 1)
                dve.wait_ge(r_A, 4 * n + j + 1)
                dve.tensor_reduce(R_at[:, j, :], R_m[:, :, :].rearrange("p l n -> p n l"), AX.X, ALU.add).then_inc(r_at, 1)
                if j < 3:
                    dve.wait_ge(r_at, 4 * n + j + 1)
            low(nxt or "c_h", b, 0)
            low(nxt or "c_h", b, 1)
            dve.wait_ge(r_r, n + 1)
            newton(R_r[:, :], psA[:, 2, :], (R_t[:, :], R_t[:, :]), P)
            own.done(dve.scalar_tensor_tensor(out=R_t[:, :], in0=psA[:, 3, :], scalar=gains[:, QG + 4:QG + 5],
                                              in1=R_r[:, :], op0=ALU.mult, op1=ALU.mult))
            dve.wait_ge(r_gs, n + 1)
            dst = C_oh[:, bass.ds(n, 1), :].rearrange("p a n -> p (a n)")
            dve.tensor_tensor(dst, R_t[:, :], R_g[:, :], ALU.mult).then_inc(r_end, 1)
        HG = 10
        repeat(dve, 0, 7, hgrn_head)
        hgrn_head(7, "c_mix")
        own.end(8)
        over()

        for c in range(12):
            dve.wait_ge(x_hi, c + 1)
            hi_, lo_, src = (X_ah[:, c, :], X_al[:, c, :], C_oa[:, c, :]) if c < 4 else \
                (X_hh[:, c - 4, :], X_hl[:, c - 4, :], C_oh[:, c - 4, :])
            dve.tensor_tensor(lo_, src, hi_.bitcast(F32), ALU.subtract).then_inc(x_lo, 1)

        def mix(m, nxt=None):
            own.body(m, 1)
            b = 0 if nxt else m + 1
            dve.wait_ge(x_l, m + 1)
            dve.scalar_tensor_tensor(out=X_t[:, :, :], in0=psG[:, 0:2, :], scalar=0.0, in1=X_t[:, :, :],
                                     op0=ALU.min, op1=ALU.subtract).then_inc(x_m, 1)
            dve.wait_ge(g_done, G0 + GC + 44 + 4 * m + 4)
            dve.wait_ge(x_s, m + 1)
            own.done(dve.tensor_tensor(X_t[:, :, :], X_t[:, :, :], psG[:, 2:4, :], ALU.mult))
            dst = X_m[:, bass.ds(m, 1), :].rearrange("p a n -> p (a n)")
            dve.tensor_tensor(dst, X_t[:, 0, :], X_t[:, 1, :], ALU.add).then_inc(x_end, 1)
            low(nxt or "c_mix", b, 0)
            low(nxt or "c_mix", b, 1)
        repeat(dve, 0, 7, mix)
        mix(7, "c_o")
        own.end(8)
        for c in range(KC):
            dve.wait_ge(y_hi, c + 1)
            dve.tensor_tensor(xlo[:, c, META:], X_m[:, c, :], xhi[:, c, META:].bitcast(F32), ALU.subtract).then_inc(y_lo, 1)
        project("c_o", None, SEQ, GC + 76)
        over()

        norm_root((META, T))
        norm_scale((META, T), 6, split=False)
        dve.wait_ge(e_lg, 1)
        dve.tensor_copy(E_lg[:, :, :].rearrange("p t n -> p (t n)"), psG[:, 3, 0:4 * ROUTES]).then_inc(e_lgd, 1)
        dve.wait_ge(e_lgd, 1)
        dve.wait_ge(e_con, 48)

        def first_max(v, n, mx, oh):
            c = E_c[:, :, 0:n]
            over_n = lambda x: x.rearrange("p (t o) -> p t o", o=1).broadcast_to([P, 4, n])
            own.done(dve.tensor_reduce(mx, v, AX.X, ALU.max))
            own.done(dve.tensor_tensor(c, v, over_n(mx), ALU.is_equal))
            own.done(dve.scalar_tensor_tensor(out=c, in0=c, scalar=-64.0,
                                              in1=slot_of[:, 0:n].rearrange("p (o n) -> p o n", o=1).broadcast_to([P, 4, n]),
                                              op0=ALU.mult, op1=ALU.add))
            own.done(dve.tensor_reduce(E_mx[:, 3, :], c, AX.X, ALU.min))
            own.done(dve.tensor_tensor(oh, c, over_n(E_mx[:, 3, :]), ALU.is_equal))

        groups = E_lg[:, :, 0:GROUPS]
        over4 = lambda x, n: x.rearrange("p (t o) -> p t o", o=1).broadcast_to([P, 4, n])
        first_max(groups, GROUPS, E_mx[:, 0, :], E_oh[:, 0, :, 0:GROUPS])
        own.done(dve.tensor_tensor(E_e[:, 0:16].rearrange("p (t g) -> p t g", t=4), groups, over4(E_mx[:, 0, :], GROUPS),
                                   ALU.subtract))
        for g in range(GROUPS):
            own.done(dve.tensor_tensor(E_c[:, :, :], E_lg[:, :, GROUPS + g * PER_GROUP:GROUPS + (g + 1) * PER_GROUP],
                                       E_oh[:, 0, :, g:g + 1].broadcast_to([P, 4, PER_GROUP]), ALU.mult))
            if g == 0:
                own.done(dve.tensor_copy(E_sel[:, :, :], E_c[:, :, :]))
            else:
                own.done(dve.tensor_tensor(E_sel[:, :, :], E_sel[:, :, :], E_c[:, :, :], ALU.add))
        first_max(E_sel[:, :, :], PER_GROUP, E_mx[:, 1, :], E_oh[:, 1, :, :])
        own.done(dve.scalar_tensor_tensor(out=E_sel[:, :, :], in0=E_oh[:, 1, :, :], scalar=NEG, in1=E_sel[:, :, :],
                                          op0=ALU.mult, op1=ALU.add))
        first_max(E_sel[:, :, :], PER_GROUP, E_mx[:, 2, :], E_oh[:, 2, :, :])
        dve.tensor_tensor(E_e[:, 16:20], E_mx[:, 2, :], E_mx[:, 1, :], ALU.subtract).then_inc(e_d, 1)
        for c in range(2):
            for g in range(GROUPS):
                own.mark(dve.tensor_tensor(E_M[:, c, :, g * PER_GROUP:(g + 1) * PER_GROUP], E_oh[:, 1 + c, :, :],
                                           E_oh[:, 0, :, g:g + 1].broadcast_to([P, 4, PER_GROUP]), ALU.mult))
        dve.wait_ge(dve_own, own.base)
        dve.tensor_tensor(E_M[:, 2, :, :], E_M[:, 0, :, :], E_M[:, 1, :, :], ALU.add).then_inc(e_m, 1)
        dve.wait_ge(e_x, 1)
        own.done(dve.tensor_reduce(E_g[:, 0, :], E_e[:, 0:16].rearrange("p (t g) -> p t g", t=4), AX.X, ALU.add))
        own.done(dve.tensor_scalar(E_g[:, 1, :], E_e[:, 16:20], 1.0, None, ALU.add))
        own.done(dve.tensor_tensor(E_g[:, 1, :], E_g[:, 1, :], E_g[:, 0, :], ALU.mult))
        own.done(dve.reciprocal(E_g[:, 2, :], E_g[:, 1, :]))
        own.done(dve.tensor_tensor(E_g[:, 3, :], E_g[:, 2, :], E_e[:, 16:20], ALU.mult))
        for t in range(4):
            b = 2 * (t % 2)
            dve.wait_ge(e_tr, t + 1)
            dve.tensor_copy(E_h[:, t, :], psG[:, b:b + 2, :].rearrange("p b n -> p (b n)")).then_inc(e_ht, 1)
            dve.wait_ge(e_vhi, t + 1)
            dve.tensor_tensor(E_vlo[:, t, :], psA[:, b:b + 2, :].rearrange("p b n -> p (b n)"),
                              E_vhi[:, t, :].bitcast(F32), ALU.subtract).then_inc(e_vlo, 1)
        dve.wait_ge(e_rank, 1)
        own.done(dve.tensor_tensor(E_t[:, :, :], psG[:, 0, 0:P].rearrange("p (t e) -> p t e", t=4),
                                   first_row[:, 0:EXPERTS].rearrange("p (o n) -> p o n", o=1).broadcast_to([P, 4, EXPERTS]),
                                   ALU.add))
        for k in range(1, SEQ // SLOTS):
            own.done(dve.tensor_scalar(E_M[:, 2, :, :], psG[:, 0, 0:P].rearrange("p (t e) -> p t e", t=4), SLOTS * k - 0.5,
                                       float((EXPERTS - 1) * SLOTS), ALU.is_gt, ALU.mult))
            own.done(dve.tensor_tensor(E_t[:, :, :], E_t[:, :, :], E_M[:, 2, :, :], ALU.add))
        for c in range(2):
            own.done(dve.tensor_tensor(E_M[:, c, :, :], E_M[:, c, :, :], E_t[:, :, :], ALU.mult))
            own.done(dve.tensor_reduce(E_pos[:, 4 * c:4 * c + 4], E_M[:, c, :, :], AX.X, ALU.add))
        own.done(dve.tensor_copy(E_idx[:, :], E_pos[:, :]))
        own.done(dve.tensor_reduce(E_cnt[:, 0:1], psG[:, 0, P:P + EXPERTS], AX.X, ALU.max))
        own.done(dve.tensor_scalar(E_cnt[:, 1:2], E_cnt[:, 0:1], float(SLOTS), None, ALU.is_gt))
        dve.tensor_copy(E_flag[:, :], E_cnt[:, 1:2]).then_inc(e_route, 1)

        def expert(n, e, s, i, first=False):
            own.body(n, 5)
            if not first:
                dve.wait_ge(e_gath, n)
            own.done(dve.tensor_scalar(E_rel[:, :], E_pos[:, :], first_row[:, bass.ds(n, 1)], None, ALU.subtract))
            for t in range(4):
                ins = dve.tensor_scalar(E_S[:, t, :], slot_of, E_rel[:, t:t + 1], None, ALU.is_equal)
                own.mark(ins)
            dve.wait_ge(dve_own, own.at + own.k)
            for t in range(4):
                ins = dve.scalar_tensor_tensor(out=E_S[:, t, :], in0=slot_of, scalar=E_rel[:, 4 + t:5 + t], in1=E_S[:, t, :].bitcast(F32),
                                               op0=ALU.is_equal, op1=ALU.add)
            ins.then_inc(e_S, 1)
            dve.wait_ge(e_l, n + 1)
            dve.scalar_tensor_tensor(out=E_s[:, :], in0=psA[:, 0, :], scalar=0.0, in1=E_l[:, :],
                                     op0=ALU.min, op1=ALU.subtract).then_inc(e_min, 1)
            dve.wait_ge(e_min, n + 1)
            dve.tensor_copy(E_l[:, :], psA[:, 1, :])
            if not first:
                dve.wait_ge(e_hT, n)
            dve.wait_ge(e_sig, n + 1)
            dve.tensor_tensor(E_hid[:, :], E_s[:, :], psA[:, 0, :], ALU.mult).then_inc(e_prod, 1)
            dve.wait_ge(e_prod, n + 1)
            dve.tensor_tensor(E_hid[:, :], E_hid[:, :], E_l[:, :], ALU.mult).then_inc(e_hid, 1)
            dve.wait_ge(e_out, n + 1)
            if not first:
                dve.wait_ge(y_stored, 16 * n)
            dve.tensor_copy(E_y[:, 512:D], psG[:, 3, :]).then_inc(e_y, 1)
        experts(dve, expert)
        over()

        for t in range(4):
            if t == 0:
                dve.wait_ge(e_rows, 16 * 9)
            for c in range(2):
                ins = dve.scalar_tensor_tensor(out=E_h[:, t, :], in0=E_win[:, 0, 2 * t + c, :],
                                               scalar=E_g[:, 2 + c, t:t + 1], in1=E_h[:, t, :], op0=ALU.mult, op1=ALU.add)
                if c == 0:
                    ins.then_inc(e_add, 1)
                    dve.wait_ge(e_add, t + 1)
            ins.then_inc(e_acc, 1)
        dve.wait_ge(e_rr, 2)
        r, v, q = E_e[:, 4:8], E_e[:, 0:4], E_e[:, 8:12]
        fin = 0
        for ins in (lambda: dve.tensor_scalar(q, v, -0.5 / D, -0.5 * EPS, ALU.mult, ALU.add),
                    lambda: dve.tensor_tensor(q, q, r, ALU.mult),
                    lambda: dve.tensor_tensor(q, q, r, ALU.mult),
                    lambda: dve.scalar_tensor_tensor(out=r, in0=q, scalar=1.5, in1=r, op0=ALU.add, op1=ALU.mult)):
            ins().then_inc(e_newton, 1)
            fin += 1
            dve.wait_ge(e_newton, fin)
        for t in range(4):
            dve.scalar_tensor_tensor(out=E_win[:, 1, t, :], in0=E_h[:, t, :], scalar=r[:, t:t + 1],
                                     in1=E_wout[:, 0, 0, :], op0=ALU.mult, op1=ALU.mult).then_inc(e_fin, 1)

    @block.gpsimd
    def _(pool):
        own = Steps(pool, pool_own)
        phases = 0

        def over():
            nonlocal phases
            phases += 1
            pool.drain().then_inc(s_phase, 1)
            pool.wait_ge(s_phase, 4 * phases)

        def past(dst, blocks, width):
            return pool.affine_select(out=dst, in_=dst, compare_op=ALU.is_gt, fill=0.0, base=0,
                                      pattern=[[0, blocks], [1, width]], channel_multiplier=-1)

        def mask(n, u, src, ready, done):
            pool.wait_ge(ready, 2 * n + u + 1)
            pool.sem_inc(a_begun, 1)
            if u == 0:
                past(src[:, 0:512].rearrange("p (a n) -> p a n", a=2)[:, :, 0:P], 2, P)
                ins = past(src[:, 448:464].rearrange("p (a n) -> p a n", a=1), 1, TAIL)
            else:
                past(src[:, SP_A + 512:SP_A + 640].rearrange("p (a n) -> p a n", a=1), 1, P)
                ins = past(src[:, SP_A + 768:SP_A + 896].rearrange("p (a n) -> p a n", a=1), 1, P)
            ins.then_inc(done, 1)

        def body(i):
            for hh in range(2):
                n = 2 * i + hh
                for src, ready, done in ((A_sp, a_sp, a_spm), (A_w, a_w, a_wm)):
                    mask(n, 0, src, ready, done)
                    mask(n, 1, src, ready, done)
        repeat(pool, 0, 8, body)
        over()
        over()

        pool.dma_start(B_con[:, :], a["b_con"]).then_inc(b_con, 16)
        pool.dma_start(B_lam[:, :], a["b_lam"]).then_inc(b_con, 16)

        def queries(i, s, first=False):
            n = 2 * i + s
            if not first:
                pool.wait_ge(b_s, 4 * n - 4)
            pool.tensor_copy(B_qs[:, s, :], B_q[:, bass.ds(n, 1), :].rearrange("p a n -> p (a n)")).then_inc(b_qs, 1)
        pool.wait_ge(b_rope, KC)
        queries(0, 0, True)
        queries(0, 1, True)

        def heads(i):
            queries(i, 0)
            queries(i, 1)
        repeat(pool, 1, 4, heads)
        over()
        over()

        pool.dma_start(h[:, :, 0:META], a["meta2"]).then_inc(c_con, 16)
        pool.dma_start(C_con[:, :], a["c_con"]).then_inc(c_con, 16)
        pool.dma_start(F_w[:, :, :], a["w_fa"]).then_inc(c_con, 16)
        pool.dma_start(stat[:, :, :], a["zero16"]).then_inc(c_con, 16)
        pool.wait_ge(f_cum, 1)
        pool.dma_start(F_row[0:1, :].rearrange("o (h n) -> o h n", h=KC), F_g[:, 2, :]).then_inc(f_row, 16)
        over()
        over()
        over()

        pool.dma_start(E_con[:, :], a["e_con"]).then_inc(e_con, 16)
        pool.dma_start(E_wr[:, :, :], a["w_er"]).then_inc(e_con, 16)
        pool.dma_start(E_br[:, :], a["e_br"]).then_inc(e_con, 16)

        def store(n):
            pool.wait_ge(e_y, 2 * n + 2)
            pool.dma_start(y_rows[bass.ds(n * SLOTS, SLOTS), :], E_y[:, :]).then_inc(y_stored, 16)
        with pool.Fori(0, EXPERTS) as e:
            store(e)
        pool.wait_ge(y_stored, 16 * EXPERTS)
        pool.wait_ge(e_route, 1)
        more = pool.value_load(E_flag[0:1, 0:1], min_val=0, max_val=1)
        with pool.If(more > 0):
            with pool.Fori(EXPERTS, BLOCKS_IN_ALL) as n:
                store(n)
            pool.wait_ge(y_stored, 16 * BLOCKS_IN_ALL)
        over()

        pool.dma_start(E_wout[:, 0, 0, :], a["e_gain"]).then_inc(e_rows, 16)
        def rows_of_tokens(rows):
            for t in range(4):
                for c in range(2):
                    pool.indirect_dma_start(E_win[:, 0, 2 * t + c, :], None, rows,
                                            bass.IndirectOffsetOnAxis(E_idx[:, 4 * c + t:4 * c + t + 1], 0)).then_inc(e_rows, 16)
        with pool.If(more > 0):
            rows_of_tokens(y_rows[:, :])
        with pool.If(more < 1):
            rows_of_tokens(y_rows[0:EXPERTS * SLOTS, :])

    top.close()


def blocks_of(w, tiles_k, cols):
    k, m = w.shape
    x = w.reshape(k // (P * tiles_k), tiles_k, P, m // (P * cols), cols, P)
    return x


def pack(tiles):
    return np.stack([np.concatenate(b, axis=1) for b in tiles])


def pack_pairs(pairs):
    most = max(len(b) for pair in pairs for b in pair)
    empty = np.zeros((P, P), np.float32)
    return pack([b + [empty] * (most - len(b)) for pair in pairs for b in pair])


def tile_of(w, k, m):
    return w[k * P:(k + 1) * P, m * P:(m + 1) * P]


def columns(w, ms, ks=range(KC)):
    return [tile_of(w, k, m) for m in ms for k in ks]


def mlp_blocks(w_in, w_out):
    into = [columns(w_in, (2 * j, 2 * j + 1)) for j in range(MLP_STEPS)]
    out = [columns(w_out, range(KC), (2 * j, 2 * j + 1)) for j in range(MLP_STEPS)]
    order = [into[0]]
    for j in range(MLP_STEPS - 1):
        order += [into[j + 1], out[j]]
    return pack(order + [out[MLP_STEPS - 1]])


def feature_major(x):
    return np.ascontiguousarray(x.T.reshape(-1, P, x.shape[0]).transpose(1, 0, 2))


def per_feature(v):
    return np.ascontiguousarray(v.reshape(-1, P).T)


def kernel(**x):
    from concourse import bacc
    from concourse.bass_utils import run_bass_kernel_spmd

    x = {k: np.asarray(v) for k, v in x.items()}
    r = np.arange(P)
    tri = -(r[:, None] >= r[None, :]).astype(np.float32)
    half = HD // 8
    freq = np.float32(500000.0) ** (-np.arange(0, 2 * half, 2, dtype=np.float32) / np.float32(2 * half))
    ang = (np.arange(T, dtype=np.float32)[None, :] * freq[:, None]).astype(np.float32)
    f = r % HD
    turns = (f < 2 * half)[:, None]
    cos_t = np.where(turns, np.cos(ang)[f % half], 1.0)
    sin_t = np.where(turns, np.sin(ang)[f % half], 0.0)
    rot = np.zeros((P, P))
    for m in range(P):
        if m % HD < half:
            rot[m + half, m] = -1.0
        elif m % HD < 2 * half:
            rot[m - half, m] = 1.0
    b_con = np.concatenate([(r[:, None] // HD == r[None, :] // HD), rot, np.where(r[None, :] > r[:, None], NEG, 0.0),
                            cos_t, sin_t], axis=1).astype(np.float32)
    masks = []
    for l in range(LEVELS):
        m = 1 << l
        masks.append((r[:, None] // (2 * m) == r[None, :] // (2 * m)) & (r[:, None] % (2 * m) < m) & (r[None, :] % (2 * m) >= m))
    masks.append(r[:, None] == r[None, :])
    starts = np.ones(T)
    starts[[0] + [META + c * P for c in range(4)]] = 0.0
    c_con = np.concatenate(masks + [np.where(r[None, :] > r[:, None], NEG, 0.0), np.broadcast_to(starts, (P, T))],
                           axis=1).astype(np.float32)
    parts = np.split(x["w_in_2"][0], np.cumsum([512, 512, 512, 8, D, D, D, D, D, D])[:-1], axis=1)
    data = {
        "con": np.concatenate([np.eye(P), np.ones((P, P)), tri, -np.ones((P, P))], axis=1).astype(np.float32),
        "h": feature_major(np.concatenate([x["meta_tokens"], x["x"][0]])),
        "gains": np.concatenate([per_feature(g) for g in (
            x["a_norm_g"][0], x["mlp_norm_g"][0], x["b_norm_g"][0], x["kv_norm_g"], x["mlp_norm_g"][1],
            x["norm_mix_w_2"][0], x["norm_ffn_w_2"][0], x["b_q_norm_g"][0].reshape(-1), x["kv_k_norm_g"].reshape(-1), x["b_subln_g"][0],
            np.concatenate([x["attn_forget_b_2"][0], np.zeros(P - KC, np.float32)]), x["hgrn_norm_w_2"][0],
            x["hgrn_lb_logits_2"].reshape(-1))], axis=1),
        "b_con": b_con,
        "b_lam": np.ascontiguousarray(np.broadcast_to(x["b_lambda"][0].reshape(1, -1), (P, 4 * HD))),
        "w_b_q": pack([columns(x["b_w_q"][0], (2 * b, 2 * b + 1)) for b in range(4)]),
        "w_b_kv": pack([columns(x["kv_w"], (n, 8 + n)) for n in range(8)]),
        "w_b_o": pack([columns(x["b_w_o"][0], (2 * b, 2 * b + 1)) for b in range(4)]),
        "w_mlp1": mlp_blocks(x["mlp_w_in"][1], x["mlp_w_out"][1]),
        "w_a_qkv": pack_pairs([(columns(x["a_w_qkv"][0], (p, 8 + p)), columns(x["a_w_qkv"][0], (16 + p,))) for p in range(8)]),
        "w_a_o": pack([columns(x["a_w_o"][0], (2 * b, 2 * b + 1)) for b in range(4)]),
        "w_mlp0": mlp_blocks(x["mlp_w_in"][0], x["mlp_w_out"][0]),
        "e_con": np.concatenate([np.broadcast_to(r[None, :], (P, P)),
                                 np.broadcast_to(r[None, :] * SLOTS, (P, P))],
                                axis=1).astype(np.float32),
        "w_er": np.ascontiguousarray(np.concatenate([x["w_router_group_2"][0], x["w_router_expert_2"][0]], axis=1)
                                     .reshape(KC, P, ROUTES).transpose(1, 0, 2)),
        "e_br": np.concatenate([x["b_router_group_2"][0], x["b_router_expert_2"][0]])[None, :],
        "e_gain": np.ascontiguousarray(np.broadcast_to(x["norm_final_w_2"][None, :], (P, D))),
        "w_ein": np.ascontiguousarray(x["w_expert_in_2"][0].reshape(EXPERTS, KC, P, 2 * EFF).transpose(0, 2, 1, 3)
                                      .reshape(EXPERTS, P, -1)),
        "w_eout": np.ascontiguousarray(x["w_expert_out_2"][0].reshape(EXPERTS, EFF // P, P, D).transpose(0, 2, 1, 3)
                                       .reshape(EXPERTS, P, -1)),
        "meta2": feature_major(x["meta_tokens_2"]),
        "c_con": c_con,
        "zero16": np.zeros((P, 2, 8), np.float32),
        "w_fa": np.ascontiguousarray(parts[3].reshape(KC, P, KC).transpose(1, 0, 2)),
        "w_c_f": pack_pairs([(columns(parts[0], (p,)) + columns(parts[1], (p,)), columns(parts[2], (p,))) for p in range(4)]),
        "w_c_h": pack([b for n in range(KC) for b in (columns(parts[4], (n,)) + columns(parts[5], (n,)),
                                                      columns(parts[6], (n,)) + columns(parts[7], (n,)))]),
        "w_c_mix": pack_pairs([(columns(parts[8], (m,)) + columns(x["w_attn_out_2"][0], (m,), range(4)),
                                columns(parts[9], (m,)) + columns(x["w_hgrn_out_2"][0], (m,))) for m in range(KC)]),
        "w_c_o": pack([columns(x["w_o_2"][0], (2 * b, 2 * b + 1)) for b in range(4)]),
    }
    nc = bacc.Bacc("TRN2", target_bir_lowering=False, num_devices=1)
    args = {k: nc.dram_tensor("in_" + k, v.shape, mybir.dt.from_np(v.dtype), kind="ExternalInput").ap() for k, v in data.items()}
    args["out"] = nc.dram_tensor("out_final", (SEQ, D), F32, kind="ExternalOutput").ap()
    build(nc, args)
    got = run_bass_kernel_spmd(nc, [{"in_" + k: v for k, v in data.items()}], core_ids=[0]).results[0]["out_final"]
    return got.reshape(1, SEQ, D)
```

```python
import numpy as np
import concourse.bass as bass
from concourse import mybir
from contextlib import ExitStack

F32 = mybir.dt.float32
F32R = mybir.dt.float32r
I32 = mybir.dt.int32
U32 = mybir.dt.uint32
ALU = mybir.AluOpType
ACT = mybir.ActivationFunctionType
AX = mybir.AxisListType

P = 128
D = 1024
KC = D // P
META = 16
SEQ = 512
T = META + SEQ
TH = T // 2
NT = 5
TAIL = T - 4 * P
TP = NT * P
HD = 64
EPS = 1e-6
RING = 16
MLP_STEPS = 16
NEG = -1e30
LEVELS = 7
EXPERTS, EFF, SLOTS = 32, 512, 128
GROUPS, PER_GROUP = 4, 8
ROUTES = GROUPS + EXPERTS
BLOCKS_IN_ALL = EXPERTS * SEQ // SLOTS
LAM_INIT = 0.8 - 0.6 * float(np.exp(-0.3))
QG = 7 * KC
G0 = 4

SP_A = 3 * P + NT * TAIL
SP_B = 7 * P


class Steps:

    def __init__(self, eng, sem):
        self.eng, self.sem, self.base, self.per, self.at, self.k = eng, sem, 0, 0, 0, 0

    def body(self, i, per):
        self.per, self.at, self.k = per, self.base + i * per, 0

    def end(self, count):
        assert self.k == self.per, (self.k, self.per)
        self.base += self.per * count
        self.at, self.k, self.per = self.base, 0, 0

    def mark(self, ins):
        ins.then_inc(self.sem, 1)
        self.k += 1
        if not self.per:
            self.base += 1
            self.at, self.k = self.base, 0
        return self.at + self.k

    def done(self, ins):
        self.eng.wait_ge(self.sem, self.mark(ins))


def repeat(eng, first, last, body):
    if last - first > 1:
        with eng.Fori(first, last) as i:
            body(i)
    elif last > first:
        body(first)


def build(nc, a):
    top = ExitStack()

    def sb(name, shape, dt=F32, ctx=top):
        return ctx.enter_context(nc.sbuf_tensor(name, shape, dt))

    def sem(name):
        return top.enter_context(nc.semaphore(name))

    psG = top.enter_context(nc.psum_tensor("psG", [P, 4, 512], F32))
    psA = top.enter_context(nc.psum_tensor("psA", [P, 4, 512], F32))

    h = sb("h", [P, KC, T])
    con = sb("con", [P, 4 * P])
    gains = sb("gains", [P, a["gains"].shape[1]])
    N_r = sb("N_r", [P, T])
    N_t = sb("N_t", [P, T])
    stat = sb("stat", [P, 2, 8])
    lam = sb("lam", [P, 4])
    ident, ones, neg_tri, neg_ones = (con[:, i * P:(i + 1) * P] for i in range(4))

    pr = ExitStack()
    whi = sb("whi", [P, 2, RING * P], F32R, ctx=pr)
    wlo = sb("wlo", [P, 2, RING * P], F32R, ctx=pr)
    raw = sb("raw", [P, 2, RING * P], ctx=pr)
    xhi = sb("xhi", [P, KC, T], F32R, ctx=pr)
    xlo = sb("xlo", [P, KC, T], F32R, ctx=pr)

    pa = ExitStack()
    A_o = sb("A_o", [P, KC, T], ctx=pa)
    A_q = sb("A_q", [P, 2, T], ctx=pa)
    A_k = sb("A_k", [P, 2, TP], ctx=pa)
    A_v = sb("A_v", [P, T], ctx=pa)
    A_vt = sb("A_vt", [P, 2, NT, P], ctx=pa)
    A_t = sb("A_t", [P, SP_A + SP_B], ctx=pa)
    A_sp = sb("A_sp", [P, SP_A + SP_B], ctx=pa)
    A_w = sb("A_w", [P, SP_A + SP_B], ctx=pa)
    pa.close()
    pn = ExitStack()
    N_sq = sb("N_sq", [P, KC, T], ctx=pn)
    pn.close()
    pb = ExitStack()
    B_o = sb("B_o", [P, KC, T], ctx=pb)
    B_q = sb("B_q", [P, KC, SEQ], ctx=pb)
    B_k = sb("B_k", [P, 2, T], ctx=pb)
    B_qs = sb("B_qs", [P, 2, SEQ], ctx=pb)
    B_v = sb("B_v", [P, T], ctx=pb)
    B_vt = sb("B_vt", [P, 2, NT, P], ctx=pb)
    B_raw = sb("B_raw", [P, 2, T], ctx=pb)
    B_sq = sb("B_sq", [P, T], ctx=pb)
    B_r = sb("B_r", [P, T], ctx=pb)
    B_t = sb("B_t", [P, 2, T], ctx=pb)
    B_con = sb("B_con", [P, 3 * P + 2 * T], ctx=pb)
    B_p = sb("B_p", [P, 2, 2, T], ctx=pb)
    B_w = sb("B_w", [P, T], ctx=pb)
    B_wt = sb("B_wt", [P, NT, P], ctx=pb)
    B_lam = sb("B_lam", [P, 4 * HD], ctx=pb)
    pb.close()
    head_ones, rotate, future = (B_con[:, i * P:(i + 1) * P] for i in range(3))
    cosine, sine = (B_con[:, 3 * P + i * T:3 * P + (i + 1) * T] for i in range(2))
    pc = ExitStack()
    C_hold = sb("C_hold", [P, KC, T], ctx=pc)
    C_con = sb("C_con", [P, 9 * P + T], ctx=pc)
    C_oa = sb("C_oa", [P, 4, SEQ], ctx=pc)
    C_oh = sb("C_oh", [P, KC, SEQ], ctx=pc)
    C_lb = sb("C_lb", [P, 5, KC], ctx=pc)
    pf = ExitStack()
    F_w = sb("F_w", [P, KC, KC], ctx=pf)
    F_q = sb("F_q", [P, T], ctx=pf)
    F_k = sb("F_k", [P, T], ctx=pf)
    F_v = sb("F_v", [P, T], ctx=pf)
    F_vt = sb("F_vt", [P, NT, P], ctx=pf)
    F_p = sb("F_p", [P, 2, T], ctx=pf)
    F_wt = sb("F_wt", [P, NT, P], ctx=pf)
    F_g = sb("F_g", [KC, 3, T], ctx=pf)
    F_row = sb("F_row", [1, KC * T], ctx=pf)
    pf.close()
    ph = ExitStack()
    R_q = sb("R_q", [P, SEQ], ctx=ph)
    R_qb = sb("R_qb", [P, SEQ], ctx=ph)
    R_k = sb("R_k", [P, T], ctx=ph)
    R_l = sb("R_l", [P, T], ctx=ph)
    R_s = sb("R_s", [P, T], ctx=ph)
    R_b = sb("R_b", [P, T], ctx=ph)
    R_v = sb("R_v", [P, T], ctx=ph)
    R_gl = sb("R_gl", [P, SEQ], ctx=ph)
    R_g = sb("R_g", [P, SEQ], ctx=ph)
    R_kd = sb("R_kd", [P, T], ctx=ph)
    R_eb = sb("R_eb", [P, SEQ], ctx=ph)
    R_d = sb("R_d", [P, NT], ctx=ph)
    R_x = sb("R_x", [P, LEVELS, SEQ], ctx=ph)
    R_m = sb("R_m", [P, LEVELS + 1, P], ctx=ph)
    R_at = sb("R_at", [P, 4, P], ctx=ph)
    R_vt = sb("R_vt", [P, NT, P], ctx=ph)
    R_kt = sb("R_kt", [P, NT, P], ctx=ph)
    R_S = sb("R_S", [P, 4, P], ctx=ph)
    R_sq = sb("R_sq", [P, SEQ], ctx=ph)
    R_r = sb("R_r", [P, SEQ], ctx=ph)
    R_t = sb("R_t", [P, SEQ], ctx=ph)
    ph.close()
    px = ExitStack()
    X_ah = sb("X_ah", [P, 4, SEQ], F32R, ctx=px)
    X_al = sb("X_al", [P, 4, SEQ], F32R, ctx=px)
    X_hh = sb("X_hh", [P, KC, SEQ], F32R, ctx=px)
    X_hl = sb("X_hl", [P, KC, SEQ], F32R, ctx=px)
    X_t = sb("X_t", [P, 2, SEQ], ctx=px)
    px.close()
    pc.close()
    X_m = C_hold[:, :, 0:SEQ]
    level_masks, future2 = C_con[:, 0:8 * P].rearrange("p (l n) -> p l n", l=8), C_con[:, 8 * P:9 * P]
    resets = C_con[:, 9 * P:9 * P + T]
    pm = ExitStack()
    M_r = sb("M_r", [P, 2, T], ctx=pm)
    M_t = sb("M_t", [P, 2, T], ctx=pm)
    M_hi = sb("M_hi", [P, 2, 2, T], F32R, ctx=pm)
    M_lo = sb("M_lo", [P, 2, 2, T], F32R, ctx=pm)
    pm.close()
    pr.close()
    pw = ExitStack()
    E_whi = sb("E_whi", [P, 3, 2 * D], F32R, ctx=pw)
    E_wlo = sb("E_wlo", [P, 3, 2 * D], F32R, ctx=pw)
    pw.close()
    F_rows = sb("F_rows", [P, 12, D])
    E_raw = sb("E_raw", [P, 4, 2 * D])
    slot_of = sb("slot_of", [P, 2 * SLOTS])
    E_hold = sb("E_hold", [P, KC, T])
    first_row = sb("first_row", [P, EXPERTS + 2 * EXPERTS + 1])
    E_l = sb("E_l", [P, 2, EFF])
    E_y = sb("E_y", [P, D])
    E_hh = sb("E_hh", [P, 4, SLOTS], F32R)
    E_hl = sb("E_hl", [P, 4, SLOTS], F32R)
    E_S = sb("E_S", [P, 4, 2 * SLOTS], F32R)
    E_A = sb("E_A", [P, 4, 2 * SLOTS])
    E_s = sb("E_s", [P, 2, EFF])
    E_hid = sb("E_hid", [P, 2, EFF])
    E_vhi = sb("E_vhi", [P, 4, D], F32R)
    E_vlo = sb("E_vlo", [P, 4, D], F32R)
    E_xh = sb("E_xh", [P, KC, 2 * SLOTS], F32R)
    E_xl = sb("E_xl", [P, KC, 2 * SLOTS], F32R)
    E_wr = sb("E_wr", [P, KC, ROUTES])
    E_br = sb("E_br", [1, ROUTES])
    E_lg = sb("E_lg", [P, 4, ROUTES])
    E_t = sb("E_t", [P, 4, EXPERTS])
    E_M = sb("E_M", [P, 3, 4, EXPERTS])
    E_sel = sb("E_sel", [P, 4, PER_GROUP])
    E_c = sb("E_c", [P, 4, PER_GROUP])
    E_oh = sb("E_oh", [P, 3, 4, PER_GROUP])
    E_mx = sb("E_mx", [P, 4, 4])
    E_e = sb("E_e", [P, 20])
    E_g = sb("E_g", [P, 4, 4])
    E_pos = sb("E_pos", [P, 8])
    E_idx = sb("E_idx", [P, 8], U32)
    E_rel = sb("E_rel", [P, 8])
    E_base = sb("E_base", [P, 1])
    E_cnt = sb("E_cnt", [P, 2])
    E_flag = sb("E_flag", [P, 1], I32)
    y_rows = nc.dram_tensor("y_rows", (EXPERTS * SEQ, D), F32).ap()
    s_con = sem("constants_loaded")
    s_h = sem("hidden_loaded")
    s_out = sem("output_stored")
    w_loaded = [sem(f"weights_loaded{s}") for s in range(2)]
    w_high = [sem(f"weights_high{s}") for s in range(2)]
    w_split = [sem(f"weights_split{s}") for s in range(2)]
    g_done = sem("product_done")
    s_phase = sem("phase_over")
    act_own, dve_own, begun = sem("act_steps"), sem("dve_steps"), sem("steps_begun")
    n_sq, n_sum, n_r0, n_t, n_hi, n_lo = (sem(f"norm_{x}") for x in ("squares", "sums", "root", "scaled", "high", "low"))
    a_stage, a_vt, a_z, a_abs, a_sp, a_spm, a_cum, a_w, a_wm, a_o, a_free = (
        sem(f"stick_{x}") for x in ("staged", "vt", "scores", "softplus_log", "softplus", "masked", "summed",
                                    "weights", "weights_masked", "outputs", "free"))
    o_hi, o_lo = sem("attn_high"), sem("attn_low")
    m_r, m_t, m_hi, m_lo = (sem(f"mlp_{x}") for x in ("relu", "square", "high", "low"))
    r_add = sem("residual_added")
    b_con, b_lam = sem("diff_constants"), sem("diff_lambda")
    b_sq, b_ss, b_root, b_t, b_rot, b_rope = (
        sem(f"diff_{x}") for x in ("squares", "sums", "root", "scaled", "rotated", "roped"))
    b_v, b_vt, b_qs, b_s, b_max, b_exp, b_w, b_T, b_wt, b_pv, b_o = (
        sem(f"diff_{x}") for x in ("v", "v_turned", "queries_staged", "scores", "max", "exp", "weights", "turned", "turned_read",
                                   "outputs", "outputs_read"))
    l_sq, l_ss, l_root, l_t, l_hi, l_lo = (sem(f"subln_{x}") for x in ("squares", "sums", "root", "scaled", "high", "low"))

    c_con, c_gate, c_lb = sem("block2_constants"), sem("forget_gates"), sem("lower_bounds")
    f_sig, f_cum, f_row, f_stage, f_vT, f_vt, f_s, f_max, f_exp, f_w, f_T, f_wt, f_pv, f_o = (
        sem(f"forget_{x}") for x in ("softplus", "sums", "row", "staged", "v_turned", "v", "scores", "max", "exp",
                                     "weights", "turned", "turned_read", "outputs", "outputs_read"))
    r_q, r_fl, r_fm, r_sig, r_fv, r_lf, r_b, r_v, r_gl, r_gm, r_gs, r_d, r_eb, r_ex, r_kd, r_x = (
        sem(f"hgrn_{x}") for x in ("q", "f_log", "f_minus", "f_sigmoid", "f_values", "log_f", "sums", "v", "g_log",
                                   "g_minus", "g_sigmoid", "differences", "decays", "level_decays", "k_decayed",
                                   "levels"))
    r_vT, r_kT, r_kvs, r_U, r_S, r_sc, r_A, r_at, r_o, r_sq, r_ss, r_r, r_end = (
        sem(f"hgrn_{x}") for x in ("v_turned", "k_turned", "turned_read", "updates", "states", "scores", "masked",
                                   "matrix", "outputs", "squares", "norm_sums", "root", "head_over"))
    x_hi, x_lo, x_l, x_m, x_s, x_end, y_hi, y_lo = (
        sem(f"mix_{x}") for x in ("high", "low", "log", "minus", "sigmoid", "over", "mixed_high", "mixed_low"))

    e_con, e_lg, e_d, e_dx, e_m, e_rank, e_route, e_vhi, e_vlo, e_ht, e_tr = (
        sem(f"route_{x}") for x in ("constants", "logits", "differences", "exponentials", "chosen", "ranks", "rows",
                                    "v_high", "v_low", "h_turned", "turned"))
    e_lgd = sem("route_logits_read")
    e_rel, e_S, e_gath, e_xh, e_xl, e_l, e_min, e_sig, e_prod, e_hid, e_hT, e_hTs, e_y, y_stored = (
        sem(f"expert_{x}") for x in ("offsets", "slots", "gathered", "inputs_high", "inputs_low", "log", "minus", "sigmoid", "silu", "gated",
                                     "turned", "turned_read", "outputs", "stored"))
    e_rows, e_acc, e_sq, e_rr, e_fin = (sem(f"final_{x}") for x in ("rows", "added", "squares", "root", "normed"))

    STREAM = [("a_qkv", 16, (16, 8)), ("a_o", 4, 16), ("mlp0", 32, 16), ("b_q", 4, 16), ("b_kv", 8, 16), ("b_o", 4, 16),
              ("mlp1", 32, 16), ("c_f", 8, (16, 8)), ("c_h", 16, 16), ("c_mix", 16, (12, 16)), ("c_o", 4, 16)]
    FIRST = {}
    n = 0
    for name, blocks, tiles in STREAM:
        FIRST[name] = n
        n += blocks
    TILES = {name: tiles if isinstance(tiles, tuple) else (tiles, tiles) for name, _, tiles in STREAM}
    BLOCKS = {name: blocks for name, blocks, _ in STREAM}
    NEXT = {x[0]: y[0] for x, y in zip(STREAM, STREAM[1:])}
    GC = 400
    GM = 484

    e_high, e_split = sem("expert_weights_high"), sem("expert_weights_split")
    e_loaded = [sem(f"expert_weights_loaded{s}") for s in range(4)]

    block = top.enter_context(nc.Block())

    def use(name, i, s):
        return FIRST[name] // 2 + i

    def pairs(eng, step):
        step(0, first=True)
        repeat(eng, 1, EXPERTS // 2, step)
        eng.wait_ge(e_route, 1)
        more = eng.value_load(E_flag[0:1, 0:1], min_val=0, max_val=1)
        with eng.If(more > 0):
            with eng.Fori(EXPERTS // 2, BLOCKS_IN_ALL // 2) as q:
                step(q)

    @block.sync
    def _(sp):
        sp.dma_start(con[:, :], a["con"]).then_inc(s_con, 16)
        sp.dma_start(gains[:, :], a["gains"]).then_inc(s_con, 16)
        sp.dma_start(h[:, :, :], a["h"]).then_inc(s_h, 16)
        for name, blocks, _ in STREAM:
            src = a["w_" + name]
            def load(i, s, first=False):
                if not first:
                    sp.wait_ge(w_split[s], use(name, i, s))
                n = TILES[name][s] * P
                sp.dma_start(raw[:, s, 0:n],
                             src[bass.ds(2 * i + s, 1), :, 0:n].rearrange("a p n -> p (a n)")).then_inc(w_loaded[s], 16)
            start = 0
            if FIRST[name] == 0:
                load(0, 0, True)
                load(0, 1, True)
                start = 1
            def body(i):
                load(i, 0)
                load(i, 1)
            repeat(sp, start, blocks // 2, body)
        def load_expert(n, q, b):
            if not (isinstance(q, int) and b < 4):
                sp.wait_ge(e_split, 12 * q + b - 3)
            sp.dma_start(E_raw[:, b % 4, :], a["w_moe"][bass.ds(n, 1)].rearrange("a p n -> p (a n)")).then_inc(e_loaded[b % 4], 16)

        sp.wait_ge(s_phase, 4 * 7)
        for b in range(4):
            load_expert(b, 0, b)
        def blocks_of_pair(i, q):
            for b in range(4, 16):
                load_expert(12 * i + b, q, b)
        with sp.Fori(0, EXPERTS // 2) as i:
            blocks_of_pair(i, i)
        sp.wait_ge(e_route, 1)
        more = sp.value_load(E_flag[0:1, 0:1], min_val=0, max_val=1)
        with sp.If(more > 0):
            with sp.Fori(1, SEQ // SLOTS) as k:
                with sp.Fori(0, EXPERTS // 2) as i:
                    blocks_of_pair(i, EXPERTS // 2 * k + i)
        for t in range(4):
            sp.wait_ge(e_fin, t + 1)
            sp.dma_start(a["out"][t * P:(t + 1) * P, :], E_raw[:, t, 0:D]).then_inc(s_out, 16)
        sp.wait_ge(s_out, 64)

    @block.tensor
    def _(pe):
        tiles_before = 0
        pe.sem_inc(g_done, G0)
        phases = 0

        def product(par, wslot, k0, xh, xl, tok, ks=KC, bank=None):
            halves = [(0, tok)] if tok <= 512 else [(0, tok // 2), (tok // 2, tok)]
            for b, (lo, hi) in enumerate(halves):
                out = psG[:, (2 * par if bank is None else bank) + b, 0:hi - lo]
                for k in range(ks):
                    wt = slice((k0 + k) * P, (k0 + k + 1) * P)
                    pe.matmul(out, whi[:, wslot, wt], xh[:, k, lo:hi], start=(k == 0), stop=False)
                    pe.matmul(out, whi[:, wslot, wt], xl[:, k, lo:hi], start=False, stop=False)
                    mm = pe.matmul(out, wlo[:, wslot, wt], xh[:, k, lo:hi], start=False, stop=(k == ks - 1))
            mm.then_inc(g_done, 1)

        def over():
            nonlocal phases
            phases += 1
            pe.drain().then_inc(s_phase, 1)
            pe.wait_ge(s_phase, 4 * phases)

        norms = 0

        def norm_sums(cols):
            nonlocal norms
            width = cols[1] - cols[0]
            halves = [(0, width)] if width <= 512 else [(0, width // 2), (width // 2, width)]
            for c in range(KC):
                pe.wait_ge(n_sq, norms * KC + c + 1)
                for b, (lo, hi) in enumerate(halves):
                    mm = pe.matmul(psA[:, b, 0:hi - lo], ones, N_sq[:, c, cols[0] + lo:cols[0] + hi],
                                   start=(c == 0), stop=(c == KC - 1), skip_group_check=True)
            mm.then_inc(n_sum, 1)
            norms += 1

        pe.wait_ge(s_con, 32)
        norm_sums((0, T))
        pe.wait_ge(n_lo, KC)


        def qkv(i, s, j, first=False):
            p = 2 * i + s
            if j != 1:
                pe.wait_ge(w_split[j // 2], use("a_qkv", p, 0) + 1)
            if j == 0 and not first:
                pe.wait_ge(a_stage, 3 * p)
            if j == 1 and not first:
                pe.wait_ge(a_vt, p)
            if j == 2:
                pe.wait_ge(a_stage, 3 * p + 1)
            product(j % 2, j // 2, (j % 2) * KC, xhi, xlo, T)

        def vt(i, s):
            par = 1
            pe.wait_ge(a_stage, 3 * (2 * i + s) + 3)
            for c in range(NT):
                w = P if c < 4 else TAIL
                mm = pe.transpose(psG[0:w, 2 * par + c // 4, (c % 4) * P:(c % 4) * P + P],
                                  A_v[:, c * P:c * P + w], ident)
            mm.then_inc(g_done, 1)

        def scores(i, s, hh, first=False):
            n = 4 * i + 2 * s + hh
            rows = slice(HD * hh, HD * hh + HD)
            q, k = A_q[rows, s, :], A_k[rows, s, :]
            if not first:
                pe.wait_ge(a_free, n)
            if hh == 0:
                pe.wait_ge(a_stage, 3 * (2 * i + s) + 3)
                pe.wait_ge(a_vt, 2 * i + s + 1)

            def z(bank, col, c, q0, q1, start=False):
                return pe.matmul(psA[:, bank, col:col + q1 - q0], k[:, c * P:c * P + P], q[:, q0:q1],
                                 start=start, stop=False, skip_group_check=True)
            z(0, 0, 0, 0, 256, True)
            z(0, 256, 1, 128, 256)
            for c in range(NT):
                mm = z(0, 384 + TAIL * c, c, 512, T)
            mm.then_inc(a_z, 1)
            z(1, 0, 0, 256, 512, True)
            z(1, 256, 1, 256, 512)
            z(2, 0, 2, 256, 512, True)
            z(2, 256, 3, 384, 512).then_inc(a_z, 1)

        def sums(i, s, hh):
            n = 4 * i + 2 * s + hh

            def take(bank, c0, c1, tri, src):
                return pe.matmul(psA[:, bank, c0:c1], tri, src, start=False, stop=False, skip_group_check=True)
            pe.wait_ge(a_spm, 2 * n + 1)
            take(0, 0, SP_A, neg_tri, A_sp[:, 0:SP_A])
            take(0, 128, 256, neg_ones, A_sp[:, 256:384])
            for c in range(1, NT):
                src = A_sp[:, 384 + TAIL * c:384 + TAIL * (c + 1)].rearrange("p (a n) -> p a n", a=1)
                mm = take(0, 384, 384 + TAIL * c, neg_ones, src.broadcast_to([P, c, TAIL]))
            mm.then_inc(a_cum, 1)
            pe.wait_ge(a_spm, 2 * n + 2)
            B = SP_A
            take(1, 0, 512, neg_tri, A_sp[:, B:B + 512])
            take(2, 0, 384, neg_tri, A_sp[:, B + 512:B + 896])
            take(1, 0, 256, neg_ones, A_sp[:, B + 256:B + 512])
            src = A_sp[:, B + 512:B + 768].rearrange("p (a n) -> p a n", a=1)
            take(1, 0, 512, neg_ones, src.broadcast_to([P, 2, 256]))
            src = A_sp[:, B + 768:B + 896].rearrange("p (a n) -> p a n", a=1)
            pe.matmul(psA[:, 1, :].rearrange("p (a n) -> p a n", a=2)[:, :, 128:256], neg_ones,
                      src.broadcast_to([P, 2, 128]), start=False, stop=False, skip_group_check=True)
            take(2, 128, 256, neg_ones, A_sp[:, B + 768:B + 896]).then_inc(a_cum, 1)

        def values(i, s, hh):
            n = 4 * i + 2 * s + hh
            rows = slice(HD * hh, HD * hh + HD)

            def pv(out, c, src, start=False, keys=P):
                return pe.matmul(out, A_vt[0:keys, s, c, rows], src[0:keys], start=start, stop=False,
                                 skip_group_check=True)
            o, B = psA[rows, 3, :], SP_A
            pe.wait_ge(a_wm, 2 * n + 1)
            pv(o[:, 0:256], 0, A_w[:, 0:256], True)
            pv(o[:, 128:256], 1, A_w[:, 256:384])
            for c in range(NT):
                keys = P if c < 4 else TAIL
                pv(psA[rows, 0, SP_A:SP_A + TAIL], c, A_w[:, 384 + TAIL * c:384 + TAIL * (c + 1)], keys=keys)
            pe.wait_ge(a_wm, 2 * n + 2)
            for c in range(3):
                pv(o[:, 256:512], c, A_w[:, B + 256 * c:B + 256 * c + 256])
            pv(o[:, 384:512], 3, A_w[:, B + 768:B + 896]).then_inc(a_o, 1)

        def pair(i, s, more=True, first=False):
            ni, ns = (i, 1) if s == 0 else (i + 1, 0)
            for hh in range(2):
                scores(i, s, hh, first=first and hh == 0)
                if more:
                    qkv(ni, ns, 2 * hh)
                sums(i, s, hh)
                if more and hh == 0:
                    qkv(ni, ns, 1)
                if more and hh == 1:
                    vt(ni, ns)
                values(i, s, hh)

        for j in range(3):
            qkv(0, 0, j, first=True)
        vt(0, 0)

        def both(i):
            pair(i, 0)
            pair(i, 1)
        pair(0, 0, first=True)
        pair(0, 1)
        repeat(pe, 1, 3, both)
        pair(3, 0)
        pair(3, 1, more=False)

        def project(name, tok, r0):
            for b in range(4):
                i, s = b // 2, b % 2
                pe.wait_ge(w_split[s], use(name, i, s) + 1)
                for j in range(2):
                    if b:
                        pe.wait_ge(r_add, r0 + 2 * b + j - 1)
                    product(j, s, j * KC, xhi[:, :, T - tok:], xlo[:, :, T - tok:], tok)

        pe.wait_ge(o_lo, KC)
        project("a_o", T, 0)
        over()
        norm_sums((0, T))
        pe.wait_ge(n_lo, 2 * KC)

        def mlp(name, tok, before, r0):
            xh, xl = xhi[:, :, T - tok:], xlo[:, :, T - tok:]

            def into(s):
                for j in range(2):
                    product(j, s, j * KC, xh, xl, tok)

            def step(j, buf, last=False, first=False):
                if not last:
                    pe.wait_ge(w_split[1], FIRST[name] // 2 + j + 1)
                    if first:
                        pe.wait_ge(m_r, before + 2)
                    else:
                        pe.wait_ge(r_add, r0 + KC * j)
                    into(1)
                s = 1 if last else 0
                pe.wait_ge(w_split[s], FIRST[name] // 2 + j + (1 if last else 2))
                pe.wait_ge(m_lo, before + 2 * j + 2)
                for m in range(KC):
                    if m < 2 and not last:
                        pe.wait_ge(m_r, before + 2 * j + 3 + m)
                    else:
                        pe.wait_ge(r_add, r0 + KC * j + m - 1)
                    product(m % 2, s, 2 * m, M_hi[:, buf, :, 0:tok], M_lo[:, buf, :, 0:tok], tok, ks=2)

            pe.wait_ge(w_split[0], FIRST[name] // 2 + 1)
            into(0)
            step(0, 0, first=True)
            step(1, 1)

            def two(i):
                step(2 * i, 0)
                step(2 * i + 1, 1)
            repeat(pe, 1, 7, two)
            step(14, 0)
            step(15, 1, last=True)
        mlp("mlp0", T, 0, 8)
        over()

        def product_q(m):
            i, s = m // 4, (m // 2) % 2
            if m % 2 == 0:
                pe.wait_ge(w_split[s], use("b_q", i, s) + 1)
            if m >= 2:
                pe.wait_ge(b_sq, m - 1)
            product(m % 2, s, (m % 2) * KC, xhi[:, :, META:], xlo[:, :, META:], SEQ)

        def halves_of(tok):
            return [(0, tok)] if tok <= 512 else [(0, tok // 2), (tok // 2, tok)]

        def head_sums(n, ps, tok):
            pe.wait_ge(b_sq, n + 1)
            for b, (lo, hi) in enumerate(halves_of(tok)):
                mm = pe.matmul(ps[:, b, 0:hi - lo], head_ones, B_sq[:, lo:hi], start=True, stop=True)
            mm.then_inc(b_ss, 1)

        def head_rotation(n, ps, tok, par):
            pe.wait_ge(b_t, n + 1)
            for b, (lo, hi) in enumerate(halves_of(tok)):
                mm = pe.matmul(ps[:, b, 0:hi - lo], rotate, B_t[:, par, lo:hi], start=True, stop=True)
            mm.then_inc(b_rot, 1)

        norm_sums((0, T))
        pe.wait_ge(n_lo, 3 * KC)
        pe.wait_ge(b_con, 32)
        for m in range(KC + 2):
            if m < KC:
                product_q(m)
            if 1 <= m <= KC:
                if m >= 2:
                    pe.wait_ge(b_t, m - 1)
                head_sums(m - 1, psA[:, 0:1, :], SEQ)
            if m >= 2:
                if m >= 3:
                    pe.wait_ge(b_rope, m - 2)
                head_rotation(m - 2, psA[:, 2:3, :], SEQ, m % 2)

        def kv_k(i, s):
            if not isinstance(i, int) or 2 * i + s > 0:
                pe.wait_ge(b_rope, KC + 2 * i + s)
            pe.wait_ge(w_split[s], use("b_kv", i, s) + 1)
            product(0, s, 0, xhi, xlo, T)

        def kv_v(i, s):
            n = 2 * i + s
            pe.wait_ge(b_t, KC + n + 1)
            product(0, s, KC, xhi, xlo, T)

        def kv_vt(i, s):
            n = 2 * i + s
            pe.wait_ge(b_v, n + 1)
            for c in range(NT):
                w = P if c < 4 else TAIL
                mm = pe.transpose(psG[0:w, c // 4, (c % 4) * P:(c % 4) * P + P], B_v[:, c * P:c * P + w], ident)
            mm.then_inc(g_done, 1)

        def kv_rot(i, s):
            n = 2 * i + s
            pe.wait_ge(b_vt, n + 1)
            head_rotation(KC + n, psG[:, 0:2, :], T, s)

        def s_qi(i, s, qi, first=False):
            u = 4 * (2 * i + s) + qi
            L = META + P * (qi + 1)
            if qi == 0:
                pe.wait_ge(b_rope, KC + 2 * i + s + 1)
                pe.wait_ge(b_qs, 2 * i + s + 1)
            if not first:
                pe.wait_ge(b_exp, 2 * u)
            for m in range(2):
                rows = slice(HD * m, HD * m + HD)
                for b, (lo, hi) in enumerate(halves_of(L)):
                    pe.matmul(psA[:, 2 * m + b, 0:hi - lo], B_qs[rows, s, qi * P:(qi + 1) * P], B_k[rows, s, lo:hi],
                              start=True, stop=(hi < L))
                    if hi == L:
                        mm = pe.matmul(psA[:, 2 * m + b, hi - lo - P:hi - lo], ident, future, start=False, stop=True)
            mm.then_inc(b_s, 1)

        def t_qi(i, s, qi, first=False):
            u = 4 * (2 * i + s) + qi
            pe.wait_ge(b_w, u + 1)
            if not first:
                pe.wait_ge(b_wt, u)
                pe.wait_ge(b_o, u)
            for c in range(qi + 2):
                w = P if c <= qi else TAIL
                mm = pe.transpose(psG[0:w, 2 + c // 4, (c % 4) * P:(c % 4) * P + P], B_w[:, c * P:c * P + w], ident)
            mm.then_inc(b_T, 1)

        def v_qi(i, s, qi):
            u = 4 * (2 * i + s) + qi
            pe.wait_ge(b_wt, u + 1)
            if qi == 0:
                pe.wait_ge(b_vt, 2 * i + s + 1)
            for c in range(qi + 2):
                w = P if c <= qi else TAIL
                mm = pe.matmul(psG[:, 3, 128:256], B_vt[0:w, s, c, :], B_wt[0:w, c, :], start=(c == 0), stop=(c == qi + 1),
                               skip_group_check=True)
            mm.then_inc(b_pv, 1)

        def head(i, s, more=True, first=False):
            ni, ns = (i, 1) if s == 0 else (i + 1, 0)
            s_qi(i, s, 0, first)
            if more:
                kv_k(ni, ns)
            s_qi(i, s, 1)
            t_qi(i, s, 0, first)
            v_qi(i, s, 0)
            if more:
                pe.wait_ge(b_sq, KC + 2 * ni + ns + 1)
                head_sums(KC + 2 * ni + ns, psG[:, 0:2, :], T)
                kv_v(ni, ns)
            s_qi(i, s, 2)
            t_qi(i, s, 1)
            v_qi(i, s, 1)
            if more:
                kv_vt(ni, ns)
            s_qi(i, s, 3)
            t_qi(i, s, 2)
            v_qi(i, s, 2)
            if more:
                kv_rot(ni, ns)
            t_qi(i, s, 3)
            v_qi(i, s, 3)

        pe.wait_ge(n_lo, 4 * KC)
        kv_k(0, 0)
        pe.wait_ge(b_sq, KC + 1)
        head_sums(KC, psG[:, 0:2, :], T)
        kv_v(0, 0)
        kv_vt(0, 0)
        kv_rot(0, 0)

        def heads(i):
            head(i, 0)
            head(i, 1)
        head(0, 0, first=True)
        head(0, 1)
        repeat(pe, 1, 3, heads)
        head(3, 0)
        head(3, 1, more=False)
        for n in range(KC):
            pe.wait_ge(l_sq, n + 1)
            if n >= 4:
                pe.wait_ge(l_t, n - 3)
            pe.matmul(psA[:, n % 4, :], ones, B_t[:, n % 2, 0:SEQ], start=True, stop=True).then_inc(l_ss, 1)
        pe.wait_ge(l_lo, KC)
        project("b_o", SEQ, 136)
        over()
        norm_sums((META, T))
        pe.wait_ge(n_lo, 5 * KC)
        mlp("mlp1", SEQ, 32, 144)
        over()

        norm_sums((0, T))
        pe.wait_ge(n_lo, 6 * KC)
        for b in range(2):
            for c in range(KC):
                mm = pe.matmul(psA[0:KC, b, 0:TH], F_w[:, c, :], N_sq[:, c, b * TH:(b + 1) * TH],
                               start=(c == 0), stop=(c == KC - 1))
        mm.then_inc(c_gate, 1)

        def f_scores(p, hh, qi, first=False):
            u = 8 * p + 4 * hh + qi
            L, bank, rows = META + P * (qi + 1), 2 * (qi % 2), slice(HD * hh, HD * hh + HD)
            if not first:
                pe.wait_ge(f_exp, u - 1)
            for b, (lo, hi) in enumerate(halves_of(L)):
                pe.matmul(psA[:, bank + b, 0:hi - lo], F_q[rows, META + qi * P:META + (qi + 1) * P], F_k[rows, lo:hi],
                          start=True, stop=False)
                mm = pe.matmul(psA[:, bank + b, 0:hi - lo], ones[0:1, :], F_row[0:1, bass.ds((2 * p + hh) * T + lo, hi - lo)],
                               start=False, stop=(hi < L))
                if hi == L:
                    mm = pe.matmul(psA[:, bank + b, hi - lo - P:hi - lo], ident, future2, start=False, stop=True)
            mm.then_inc(f_s, 1)

        def f_turn(p, hh, qi, first=False):
            u = 8 * p + 4 * hh + qi
            pe.wait_ge(f_w, u + 1)
            if not first:
                pe.wait_ge(f_wt, u)
                pe.wait_ge(f_o, u)
            for c in range(qi + 2):
                w = P if c <= qi else TAIL
                mm = pe.transpose(psG[0:w, 2 + c // 4, (c % 4) * P:(c % 4) * P + P],
                                  F_p[:, qi % 2, c * P:c * P + w], ident)
            mm.then_inc(f_T, 1)
            pe.wait_ge(f_wt, u + 1)
            rows = slice(HD * hh, HD * hh + HD)
            for c in range(qi + 2):
                w = P if c <= qi else TAIL
                mm = pe.matmul(psG[rows, 3, 128:256], F_vt[0:w, c, rows], F_wt[0:w, c, :], start=(c == 0),
                               stop=(c == qi + 1), skip_group_check=True)
            mm.then_inc(f_pv, 1)

        def forget_pair(p, first=False):
            pe.wait_ge(w_split[0], use("c_f", p, 0) + 1)
            if not first:
                pe.wait_ge(f_o, 8 * p)
            product(0, 0, 0, xhi, xlo, T)
            product(1, 0, KC, xhi, xlo, T)
            pe.wait_ge(w_split[1], use("c_f", p, 1) + 1)
            pe.wait_ge(f_stage, 3 * p + 1)
            product(0, 1, 0, xhi, xlo, T)
            pe.wait_ge(f_stage, 3 * p + 3)
            for c in range(NT):
                w = P if c < 4 else TAIL
                mm = pe.transpose(psG[0:w, 2 + c // 4, (c % 4) * P:(c % 4) * P + P], F_v[:, c * P:c * P + w], ident)
            mm.then_inc(f_vT, 1)
            units = [(hh, qi) for hh in range(2) for qi in range(4)]
            f_scores(p, 0, 0, first)
            for k, (hh, qi) in enumerate(units):
                if k < 7:
                    f_scores(p, *units[k + 1], first=first and k < 1)
                if k == 0:
                    pe.wait_ge(f_vt, p + 1)
                f_turn(p, hh, qi, first and k == 0)

        pe.wait_ge(f_row, 16)
        forget_pair(0, True)
        repeat(pe, 1, 4, forget_pair)
        over()

        def hgrn_head(n, first=False):
            g = GC + 12 + 4 * n
            pe.wait_ge(w_split[0], use("c_h", n, 0) + 1)
            if not first:
                pe.wait_ge(r_end, n)
            product(0, 0, 0, xhi[:, :, META:], xlo[:, :, META:], SEQ)
            product(1, 0, KC, xhi, xlo, T)
            pe.wait_ge(w_split[1], use("c_h", n, 1) + 1)
            pe.wait_ge(r_q, n + 1)
            product(0, 1, 0, xhi, xlo, T)
            pe.wait_ge(r_fm, n + 1)
            product(1, 1, KC, xhi[:, :, META:], xlo[:, :, META:], SEQ)
            pe.wait_ge(r_v, n + 1)
            for c in range(1, NT):
                pe.transpose(psG[:, 0, (c - 1) * P:c * P], R_v[:, META + (c - 1) * P:META + c * P], ident)
            pe.transpose(psG[0:META, 1, 0:P], R_v[:, 0:META], ident).then_inc(r_vT, 1)
            pe.wait_ge(r_kd, n + 1)
            for c in range(1, 4):
                pe.transpose(psG[:, 1, c * P:(c + 1) * P], R_kd[:, META + (c - 1) * P:META + c * P], ident)
            pe.transpose(psG[0:META, 3, 0:P], R_kd[:, 0:META], ident).then_inc(r_kT, 1)
            pe.wait_ge(r_kvs, 2 * n + 2)
            for c in range(4):
                w = META if c == 0 else P
                mm = pe.matmul(psA[:, 2, c * P:(c + 1) * P], R_kt[0:w, c, :], R_vt[0:w, c, :], start=(c == 0), stop=(c == 3),
                               skip_group_check=True)
            mm.then_inc(r_U, 1)
            pe.wait_ge(r_x, n + 1)
            for j in range(5):
                if j < 4:
                    if j:
                        pe.wait_ge(r_A, 4 * n + j)
                    t = slice(j * P, (j + 1) * P)
                    for l in range(LEVELS):
                        pe.matmul(psA[:, l // 4, (l % 4) * P:(l % 4 + 1) * P], R_x[:, l, t], R_x[:, l, t],
                                  start=(l % 4 == 0), stop=False, skip_group_check=True)
                    pe.matmul(psA[:, 1, 3 * P:4 * P], R_k[:, META + j * P:META + (j + 1) * P], R_q[:, t],
                              start=False, stop=True, skip_group_check=True).then_inc(r_sc, 1)
                if j:
                    c = j - 1
                    t = slice(c * P, (c + 1) * P)
                    if c == 0:
                        pe.wait_ge(r_S, n + 1)
                    pe.matmul(psA[:, 3, t], R_S[:, c, :], R_qb[:, t], start=(c == 0), stop=False, skip_group_check=True)
                    pe.wait_ge(r_at, 4 * n + c + 1)
                    mm = pe.matmul(psA[:, 3, t], R_vt[:, c + 1, :], R_at[:, c, :], start=False, stop=(c == 3),
                                   skip_group_check=True)
            mm.then_inc(r_o, 1)
            pe.wait_ge(r_sq, n + 1)
            pe.matmul(psA[:, 2, :], ones, R_sq[:, :], start=True, stop=True).then_inc(r_ss, 1)
        hgrn_head(0, True)
        repeat(pe, 1, 8, hgrn_head)
        over()

        def mix(m, first=False):
            pe.wait_ge(w_split[0], use("c_mix", m, 0) + 1)
            if not first:
                pe.wait_ge(x_end, m)
            product(0, 0, 0, xhi[:, :, META:], xlo[:, :, META:], SEQ, bank=0)
            product(0, 0, KC, X_ah, X_al, SEQ, ks=4, bank=2)
            pe.wait_ge(w_split[1], use("c_mix", m, 1) + 1)
            product(0, 1, 0, xhi[:, :, META:], xlo[:, :, META:], SEQ, bank=1)
            product(0, 1, KC, X_hh, X_hl, SEQ, bank=3)
        pe.wait_ge(x_lo, 12)
        mix(0, True)
        repeat(pe, 1, 8, mix)
        pe.wait_ge(y_lo, KC)
        project("c_o", SEQ, 272)
        over()

        norm_sums((META, T))
        pe.wait_ge(n_t, 7 * KC)
        pe.wait_ge(e_con, 64)
        for t in range(4):
            for c in range(KC):
                pe.matmul(psG[:, 3, t * ROUTES:(t + 1) * ROUTES], N_sq[:, c, META + t * P:META + (t + 1) * P], E_wr[:, c, :],
                          start=(t == 0 and c == 0), stop=False, skip_group_check=True)
            mm = pe.matmul(psG[:, 3, t * ROUTES:(t + 1) * ROUTES], ones[0:1, :], E_br[0:1, :], start=False, stop=(t == 3),
                           skip_group_check=True)
        mm.then_inc(e_lg, 1)
        for t in range(4):
            b = 2 * (t % 2)
            if t >= 2:
                pe.wait_ge(e_vlo, t - 1)
            tok = slice(META + t * P, META + (t + 1) * P)
            for c in range(KC):
                mm = pe.transpose(psA[:, b + c // 4, (c % 4) * P:(c % 4 + 1) * P], N_sq[:, c, tok], ident)
            mm.then_inc(e_tr, 1)
        pe.wait_ge(e_m, 1)
        for t in range(4):
            out = psG[:, 0, t * EXPERTS:(t + 1) * EXPERTS]
            for u in range(t + 1):
                pe.matmul(out, ones, E_M[:, 2, u, :], start=(t == 0), stop=False, skip_group_check=True)
            pe.matmul(out, neg_tri, E_M[:, 2, t, :], start=False, stop=False, skip_group_check=True)
        for u in range(4):
            mm = pe.matmul(psG[:, 0, P:P + EXPERTS], ones, E_M[:, 2, u, :], start=False, stop=(u == 3), skip_group_check=True)
        mm.then_inc(e_rank, 1)
        pe.wait_ge(e_vlo, 4)

        def gather(q):
            pe.wait_ge(e_S, q + 1)
            for piece in range(4):
                bank = 2 - 2 * (piece % 2)
                if piece == 1 and (not isinstance(q, int) or q > 0):
                    pe.wait_ge(e_y, 4 * q - 2)
                if piece >= 2:
                    pe.wait_ge(e_xh, 4 * q + piece - 1)
                    pe.wait_ge(e_xl, 4 * q + piece - 1)
                for half in range(2):
                    c = 2 * piece + half
                    for v, part in ((E_vhi, 0), (E_vlo, 1)):
                        for t in range(4):
                            mm = pe.matmul(psG[:, bank + part, half * 2 * SLOTS:(half + 1) * 2 * SLOTS],
                                           v[:, t, c * P:(c + 1) * P], E_S[:, t, :], start=(half == 0 and t == 0), stop=(t == 3),
                                           skip_group_check=True)
                mm.then_inc(e_gath, 1)

        def in_product(q, j, first):
            bank = 2 * j
            if j == 0:
                pe.wait_ge(e_xh, 4 * q + 4)
                pe.wait_ge(e_xl, 4 * q + 4)
            elif not first:
                pe.wait_ge(e_hTs, 4 * q)
            slots = slice(j * SLOTS, (j + 1) * SLOTS)
            for b in range(4):
                s = (4 * j + b) % 3
                pe.wait_ge(e_split, 12 * q + 4 * j + b + 1)
                for kk in range(2):
                    k = 2 * b + kk
                    for half in range(2):
                        out, w = psA[:, bank + half, :], slice(kk * D + half * EFF, kk * D + (half + 1) * EFF)
                        pe.matmul(out, E_xh[:, k, slots], E_whi[:, s, w], start=(k == 0), stop=False)
                        pe.matmul(out, E_xl[:, k, slots], E_whi[:, s, w], start=False, stop=False)
                        mm = pe.matmul(out, E_xh[:, k, slots], E_wlo[:, s, w], start=False, stop=(k == KC - 1))
                mm.then_inc(g_done, 1)

        def out_product(q, j, first):
            pe.wait_ge(e_hid, 2 * q + j + 1)
            for k in range(4):
                mm = pe.transpose(psA[:, 2 * j, k * P:(k + 1) * P], E_hid[:, j, k * P:(k + 1) * P], ident)
            mm.then_inc(e_hT, 1)
            pe.wait_ge(e_hTs, 4 * q + 2 * j + 2)
            if j == 1:
                pe.wait_ge(e_xh, 4 * q + 8)
                pe.wait_ge(e_xl, 4 * q + 8)
            elif not first:
                pe.wait_ge(e_y, 4 * q)
            for b in range(2):
                s = (8 + 2 * j + b) % 3
                pe.wait_ge(e_split, 12 * q + 8 + 2 * j + b + 1)
                for kk in range(2):
                    k = 2 * b + kk
                    for half in range(2):
                        out, w = psG[:, half, :], slice(kk * D + half * 512, kk * D + (half + 1) * 512)
                        pe.matmul(out, E_hh[:, k, :], E_whi[:, s, w], start=(k == 0), stop=False)
                        pe.matmul(out, E_hl[:, k, :], E_whi[:, s, w], start=False, stop=False)
                        mm = pe.matmul(out, E_hh[:, k, :], E_wlo[:, s, w], start=False, stop=(k == 3))
                mm.then_inc(g_done, 1)

        def pair_of_experts(q, first=False):
            in_product(q, 0, first)
            in_product(q, 1, first)
            out_product(q, 0, first)
            gather(q + 1)
            out_product(q, 1, first)
        gather(0)
        pairs(pe, pair_of_experts)
        over()

        for t in range(4):
            ps = psG if t < 2 else psA
            for c in range(KC):
                mm = pe.transpose(ps[:, 2 * (t % 2) + c // 4, (c % 4) * P:(c % 4 + 1) * P],
                                  h[:, c, META + t * P:META + (t + 1) * P], ident)
            mm.then_inc(e_ht, 1)

    @block.scalar
    def _(act):
        act.preload_act_table_set("natural_log_exp_and_others")
        own = Steps(act, act_own)
        phases = 0

        def over():
            nonlocal phases
            phases += 1
            act.drain().then_inc(s_phase, 1)
            act.wait_ge(s_phase, 4 * phases)

        def high(name, i, s, over):
            tiles = TILES[name][s]
            act.wait_ge(w_loaded[s], 16 * use(name, i, s) + 16)
            if over is not None:
                act.wait_ge(g_done, G0 + over)
            act.activation(whi[:, s, 0:tiles * P], raw[:, s, 0:tiles * P], ACT.Copy).then_inc(w_high[s], 1)

        roots = scalings = 0

        def norm_root(cols):
            nonlocal roots
            width = cols[1] - cols[0]
            halves = 1 if width <= 512 else 2
            for c in range(KC):
                act.activation(N_sq[:, c, cols[0]:cols[1]], h[:, c, cols[0]:cols[1]], ACT.Square).then_inc(n_sq, 1)
            act.wait_ge(n_sum, roots + 1)
            r = N_r[:, cols[0]:cols[1]].rearrange("p (b n) -> p b n", b=halves)
            own.done(act.activation(r, psA[:, 0:halves, 0:width // halves], ACT.Ln, scale=1.0 / D, bias=EPS))
            act.activation(r, r, ACT.Exp, scale=-0.5).then_inc(n_r0, 1)
            roots += 1

        def norm_high(cols):
            nonlocal scalings
            for c in range(KC):
                act.wait_ge(n_t, scalings * KC + c + 1)
                act.activation(xhi[:, c, cols[0]:cols[1]], N_sq[:, c, cols[0]:cols[1]], ACT.Copy).then_inc(n_hi, 1)
            scalings += 1

        act.wait_ge(s_con, 32)
        act.wait_ge(s_h, 16)
        norm_root((0, T))
        norm_high((0, T))

        def stage(i, s, j):
            t = 8 * i + 4 * s + j
            par = j % 2
            act.wait_ge(g_done, G0 + t + 1)
            src = psG[:, 2 * par:2 * par + 2, 0:TH]
            if j == 0:
                dst, scale = A_q[:, s, :], HD ** -0.5
            elif j == 1:
                dst, scale = A_k[:, s, 0:T], 1.0
            else:
                dst, scale = A_v[:, :], 1.0
            act.activation(dst.rearrange("p (b n) -> p b n", b=2), src, ACT.Copy, scale=scale).then_inc(a_stage, 1)

        def exps(n, u):
            c0, c1 = (0, SP_A) if u == 0 else (SP_A, SP_A + SP_B)
            act.wait_ge(a_z, 2 * n + u + 1)
            if u == 0:
                src = psA[:, 0, 0:SP_A]
            else:
                src = psA[:, 1:3, :].rearrange("p b n -> p (b n)")[:, 0:SP_B]
            own.done(act.activation(A_t[:, c0:c1], src, ACT.Abs))
            own.done(act.activation(A_t[:, c0:c1], A_t[:, c0:c1], ACT.Exp, scale=-1.0))
            act.activation(A_t[:, c0:c1], A_t[:, c0:c1], ACT.Ln, bias=1.0).then_inc(a_abs, 1)

        def weights(n, u):
            c0, c1 = (0, SP_A) if u == 0 else (SP_A, SP_A + SP_B)
            act.wait_ge(a_cum, 2 * n + u + 1)
            if u == 0:
                src = psA[:, 0, 0:SP_A]
            else:
                src = psA[:, 1:3, :].rearrange("p b n -> p (b n)")[:, 0:SP_B]
            act.activation(A_w[:, c0:c1], src, ACT.Exp).then_inc(a_w, 1)

        def pair(i, s, more=True, nxt="a_qkv"):
            ni, ns = (i, 1) if s == 0 else (i + 1, 0)
            p = 2 * i + s
            b = p + 2 if nxt == "a_qkv" else 0
            for hh in range(2):
                n = 2 * p + hh
                exps(n, 0)
                exps(n, 1)
                if more:
                    stage(ni, ns, 2 * hh)
                weights(n, 0)
                weights(n, 1)
                if more and hh == 0:
                    stage(ni, ns, 1)
                    high(nxt, b, 0, 4 * p + 6)
                if more and hh == 1:
                    high(nxt, b, 1, 4 * p + 7)

        high("a_qkv", 0, 0, None)
        high("a_qkv", 0, 1, None)
        for j in range(3):
            stage(0, 0, j)
        high("a_qkv", 1, 0, 2)
        high("a_qkv", 1, 1, 3)

        def both(i):
            own.body(i, 16)
            pair(i, 0)
            pair(i, 1)
        repeat(act, 0, 3, both)
        own.end(3)
        own.body(0, 16)
        pair(3, 0, nxt="a_o")
        pair(3, 1, more=False)
        own.end(1)

        act.wait_ge(a_free, 16)
        for c in range(KC):
            act.activation(xhi[:, c, :], A_o[:, c, :], ACT.Copy).then_inc(o_hi, 1)
        high("a_o", 1, 0, 32 + 2)
        high("a_o", 1, 1, 32 + 4)
        high("mlp0", 0, 0, 32 + 6)
        high("mlp0", 0, 1, 32 + 8)
        over()
        norm_root((0, T))
        norm_high((0, T))

        def mlp(name, nxt, tok, before, g0):
            def into(step, at, first=False):
                for j in range(2):
                    act.wait_ge(g_done, G0 + g0 + at + j + 1)
                    if tok > 512:
                        src, dst = psG[:, 2 * j:2 * j + 2, 0:tok // 2], M_r[:, j, 0:tok].rearrange("p (b n) -> p b n", b=2)
                    else:
                        src, dst = psG[:, 2 * j, 0:tok], M_r[:, j, 0:tok]
                    if not first:
                        act.wait_ge(m_t, before + 2 * step + j - 1)
                    act.activation(dst, src, ACT.Relu).then_inc(m_r, 1)

            def highs(step, buf):
                for j in range(2):
                    act.wait_ge(m_t, before + 2 * step + j + 1)
                    act.activation(M_hi[:, buf, j, 0:tok], M_t[:, j, 0:tok], ACT.Copy).then_inc(m_hi, 1)

            into(0, 0, True)
            highs(0, 0)
            high(name, 1, 0, g0 + 2)

            def step(j, buf, nxt0=None):
                g = g0 + 2 + 10 * j
                into(j + 1, 2 + 10 * j)
                highs(j + 1, 1 - buf)
                act_high_at(name, j + 1, 1, g + 2)
                if nxt0 is None:
                    act_high_at(name, j + 2, 0, g + 10)
                else:
                    high(nxt0, 0, 0, g + 10)

            def act_high_at(name, i, s, over):
                high(name, i, s, over)

            def two(i):
                step(2 * i, 0)
                step(2 * i + 1, 1)
            repeat(act, 0, 7, two)
            step(14, 0, nxt)
            high(nxt, 0, 1, g0 + 160)
        mlp("mlp0", NEXT["mlp0"], T, 0, 40)
        over()

        norm_root((0, T))
        norm_high((META, T))

        def fold(x, tok):
            return x.rearrange("p (b n) -> p b n", b=2) if tok > 512 else x

        def bank(pair, tok):
            return psG[:, 2 * pair:2 * pair + 2, 0:tok // 2] if tok > 512 else psG[:, 2 * pair, 0:tok]

        def raw_and_square(n, g, pair, par, tok):
            act.wait_ge(g_done, G0 + g + 1)
            late = not isinstance(n, int)
            if late or n >= 2:
                act.wait_ge(b_t, n - 1)
            act.activation(fold(B_raw[:, par, 0:tok], tok), bank(pair, tok), ACT.Copy)
            if late or n >= 1:
                act.wait_ge(b_ss, n)
            act.activation(fold(B_sq[:, 0:tok], tok), bank(pair, tok), ACT.Square).then_inc(b_sq, 1)

        def root(n, src, tok):
            act.wait_ge(b_ss, n + 1)
            if not isinstance(n, int) or n >= 1:
                act.wait_ge(b_t, n)
            r = fold(B_r[:, 0:tok], tok)
            own.done(act.activation(r, src, ACT.Ln, scale=1.0 / HD, bias=EPS))
            act.activation(r, r, ACT.Exp, scale=-0.5).then_inc(b_root, 1)

        act.wait_ge(b_lam, 1)
        act.activation(lam[:, 0:2], lam[:, 0:2], ACT.Exp).then_inc(b_lam, 1)
        for m in range(KC + 1):
            if m < KC:
                raw_and_square(m, 200 + m, m % 2, m % 2, SEQ)
            if m >= 1:
                root(m - 1, psA[:, 0, :], SEQ)
            if m in (1, 3):
                high("b_q", 1, m // 2, 200 + m + 1)
            if m in (5, 7):
                high("b_kv", 0, (m - 5) // 2, 200 + m + 1)
        norm_high((0, T))

        GK = 208

        def exps(i, s, qi, first=False):
            u = 4 * (2 * i + s) + qi
            par, L = qi % 2, META + P * (qi + 1)
            act.wait_ge(b_max, u + 1)
            if not (first and qi < 2):
                act.wait_ge(b_w, u - 1)
            for m in range(2):
                if L > 512:
                    src, dst = psA[:, 2 * m:2 * m + 2, 0:L // 2], B_p[:, par, m, 0:L].rearrange("p (b n) -> p b n", b=2)
                else:
                    src, dst = psA[:, 2 * m, 0:L], B_p[:, par, m, 0:L]
                act.activation(dst, src, ACT.Exp, scale=HD ** -0.5, bias=stat[:, par, 2 + m:3 + m],
                               accum_out=stat[:, par, 4 + m:5 + m]).then_inc(b_exp, 1)

        def turned(i, s, qi, first=False):
            u = 4 * (2 * i + s) + qi
            act.wait_ge(b_T, u + 1)
            if not (first and qi == 0):
                act.wait_ge(b_pv, u)
            n = min(qi + 1, 4)
            act.activation(B_wt[:, 0:n, :].rearrange("p c n -> p (c n)"), psG[:, 2, 0:n * P], ACT.Copy)
            c = qi + 1
            act.activation(B_wt[0:TAIL, c, :], psG[0:TAIL, 2 + c // 4, (c % 4) * P:(c % 4) * P + P], ACT.Copy)\
                .then_inc(b_wt, 1)

        def key(i, s):
            n = 2 * i + s
            raw_and_square(KC + n, GK + 3 * n, 0, s, T)

        def key_root(i, s):
            root(KC + 2 * i + s, psG[:, 0:2, 0:TH], T)

        def value(i, s):
            n = 2 * i + s
            act.wait_ge(g_done, G0 + GK + 3 * n + 2)
            act.activation(fold(B_v[:, :], T), bank(0, T), ACT.Copy).then_inc(b_v, 1)

        def head(i, s, nxt, more=True, first=False):
            ni, ns = (i, 1) if s == 0 else (i + 1, 0)
            exps(i, s, 0, first)
            if more:
                key(ni, ns)
            turned(i, s, 0, first)
            exps(i, s, 1, first)
            if more:
                key_root(ni, ns)
                value(ni, ns)
            turned(i, s, 1)
            exps(i, s, 2)
            nxt()
            turned(i, s, 2)
            exps(i, s, 3)
            turned(i, s, 3)

        key(0, 0)
        key_root(0, 0)
        value(0, 0)
        own.body(0, 2)
        head(0, 0, lambda: high("b_kv", 1, 0, GK + 2), first=True)
        head(0, 1, lambda: high("b_kv", 1, 1, GK + 5))
        own.end(1)

        def heads(i):
            own.body(i - 1, 2)
            head(i, 0, lambda: high("b_kv", i + 1, 0, GK + 6 * i + 2))
            head(i, 1, lambda: high("b_kv", i + 1, 1, GK + 6 * i + 5))
        repeat(act, 1, 3, heads)
        own.end(2)
        own.body(0, 1)
        head(3, 0, lambda: high("b_o", 0, 0, GK + 20))
        head(3, 1, lambda: high("b_o", 0, 1, GK + 23), more=False)
        own.end(1)

        for n in range(KC + 1):
            if n < KC:
                if n == 0:
                    act.wait_ge(b_o, 32)
                else:
                    act.wait_ge(l_ss, n)
                if n >= 2:
                    act.wait_ge(l_ss, n - 1)
                act.activation(B_t[:, n % 2, 0:SEQ], B_o[:, n, 0:SEQ], ACT.Square).then_inc(l_sq, 1)
                act.wait_ge(l_ss, n + 1)
                if n >= 2:
                    act.wait_ge(l_t, n - 1)
                r = B_raw[:, n % 2, 0:SEQ]
                own.done(act.activation(r, psA[:, n % 4, :], ACT.Ln, scale=1.0 / P, bias=EPS))
                act.activation(r, r, ACT.Exp, scale=-0.5).then_inc(l_root, 1)
            if n >= 1:
                act.wait_ge(l_t, n)
                act.activation(xhi[:, n - 1, META:], B_p[:, (n - 1) % 2, 0, 0:SEQ], ACT.Copy).then_inc(l_hi, 1)
        GO = 232
        high("b_o", 1, 0, GO + 2)
        high("b_o", 1, 1, GO + 4)
        high("mlp1", 0, 0, GO + 6)
        high("mlp1", 0, 1, GO + 8)
        over()
        norm_root((META, T))
        norm_high((META, T))
        mlp("mlp1", NEXT["mlp1"], SEQ, 32, GO + 8)
        over()

        act.wait_ge(c_con, 64)
        norm_root((0, T))
        norm_high((0, T))
        act.wait_ge(c_lb, 1)
        act.activation(C_lb[:, 0:2, :], C_lb[:, 0:2, :], ACT.Exp).then_inc(c_lb, 1)

        def softplus_log(dst, src, step=True):
            own.done(act.activation(dst, src, ACT.Abs))
            own.done(act.activation(dst, dst, ACT.Exp, scale=-1.0))
            return act.activation(dst, dst, ACT.Ln, bias=1.0)

        act.wait_ge(c_gate, 1)
        fold2 = lambda x: x.rearrange("p (b n) -> p b n", b=2)
        own.done(act.activation(fold2(F_g[:, 0, :]), psA[0:KC, 0:2, 0:TH], ACT.Identity, bias=gains[0:KC, QG + 3:QG + 4]))
        softplus_log(F_g[:, 1, :], F_g[:, 0, :]).then_inc(f_sig, 1)

        def forget_exp(p, hh, qi, first=False):
            u = 8 * p + 4 * hh + qi
            par, L = qi % 2, META + P * (qi + 1)
            act.wait_ge(f_max, u + 1)
            if not (first and hh == 0 and qi < 2):
                act.wait_ge(f_T, u - 1)
            if L > 512:
                src, dst = psA[:, 2 * par:2 * par + 2, 0:L // 2], fold2(F_p[:, par, 0:L])
            else:
                src, dst = psA[:, 2 * par, 0:L], F_p[:, par, 0:L]
            act.activation(dst, src, ACT.Exp, bias=stat[:, par, 1:2], accum_out=stat[:, par, 2:3]).then_inc(f_exp, 1)

        def forget_turned(p, hh, qi, first=False):
            u = 8 * p + 4 * hh + qi
            act.wait_ge(f_T, u + 1)
            if not first:
                act.wait_ge(f_pv, u)
            n = min(qi + 1, 4)
            act.activation(F_wt[:, 0:n, :].rearrange("p c n -> p (c n)"), psG[:, 2, 0:n * P], ACT.Copy)
            c = qi + 1
            act.activation(F_wt[0:TAIL, c, :], psG[0:TAIL, 2 + c // 4, (c % 4) * P:(c % 4) * P + P], ACT.Copy)\
                .then_inc(f_wt, 1)

        def forget_pair(p, first=False, nxt=None):
            g = GC + 3 * p
            act.wait_ge(g_done, G0 + g + 1)
            act.activation(fold2(F_q[:, :]), psG[:, 0:2, 0:TH], ACT.Copy, scale=HD ** -0.5).then_inc(f_stage, 1)
            act.wait_ge(g_done, G0 + g + 2)
            act.activation(fold2(F_k[:, :]), psG[:, 2:4, 0:TH], ACT.Copy).then_inc(f_stage, 1)
            act.wait_ge(g_done, G0 + g + 3)
            act.activation(fold2(F_v[:, :]), psG[:, 0:2, 0:TH], ACT.Copy).then_inc(f_stage, 1)
            for hh in range(2):
                for qi in range(4):
                    forget_exp(p, hh, qi, first)
                    if (hh, qi) == (0, 1):
                        high(nxt or "c_f", 0 if nxt else p + 1, 0, g + 2)
                    if (hh, qi) == (1, 1):
                        high(nxt or "c_f", 0 if nxt else p + 1, 1, g + 3)
                    forget_turned(p, hh, qi, first and hh == 0 and qi == 0)
        forget_pair(0, True)
        repeat(act, 1, 3, forget_pair)
        forget_pair(3, nxt="c_h")
        over()

        def hgrn_head(n, nxt=None):
            own.body(n, 5)
            g = GC + 12 + 4 * n
            b = 0 if nxt else n + 1
            act.wait_ge(g_done, G0 + g + 1)
            act.activation(R_q[:, :], psG[:, 0, :], ACT.Copy, scale=P ** -0.5).then_inc(r_q, 1)
            act.wait_ge(g_done, G0 + g + 2)
            softplus_log(fold2(R_l[:, :]), psG[:, 2:4, 0:TH]).then_inc(r_fl, 1)
            act.wait_ge(r_fm, n + 1)
            act.activation(R_s[:, :], R_s[:, :], ACT.Exp).then_inc(r_sig, 1)
            act.wait_ge(g_done, G0 + g + 3)
            act.activation(fold2(R_v[:, :]), psG[:, 0:2, 0:TH], ACT.Copy).then_inc(r_v, 1)
            act.wait_ge(r_fv, n + 1)
            act.activation(R_s[:, :], R_s[:, :], ACT.Ln).then_inc(r_lf, 1)
            act.wait_ge(r_vT, n + 1)
            act.activation(R_vt[:, 1:NT, :].rearrange("p c n -> p (c n)"), psG[:, 0, :], ACT.Copy)
            act.activation(R_vt[0:META, 0, :], psG[0:META, 1, 0:P], ACT.Copy).then_inc(r_kvs, 1)
            act.wait_ge(r_b, n + 1)
            for c in range(4):
                lo, hi = (0, META) if c == 0 else (META + (c - 1) * P, META + c * P)
                act.activation(R_kd[:, lo:hi], R_b[:, lo:hi], ACT.Exp, scale=-1.0, bias=R_b[:, hi - 1:hi])
                act.activation(R_d[:, c:c + 1], R_b[:, hi - 1:hi], ACT.Exp)
            act.activation(R_eb[:, :], R_b[:, META:], ACT.Exp).then_inc(r_eb, 1)
            act.wait_ge(r_d, n + 1)
            act.activation(R_x[:, :, :], R_x[:, :, :], ACT.Exp).then_inc(r_ex, 1)
            act.wait_ge(r_kT, n + 1)
            act.activation(R_kt[:, 1:4, :].rearrange("p c n -> p (c n)"), psG[:, 1, P:], ACT.Copy)
            act.activation(R_kt[0:META, 0, :], psG[0:META, 3, 0:P], ACT.Copy).then_inc(r_kvs, 1)
            act.wait_ge(g_done, G0 + g + 4)
            softplus_log(R_gl[:, :], psG[:, 2, :]).then_inc(r_gl, 1)
            act.wait_ge(r_gm, n + 1)
            act.activation(R_g[:, :], R_g[:, :], ACT.Exp).then_inc(r_gs, 1)
            high(nxt or "c_h", b, 0, g + 2)
            high(nxt or "c_h", b, 1, g + 4)
            act.wait_ge(r_o, n + 1)
            act.activation(R_sq[:, :], psA[:, 3, :], ACT.Square).then_inc(r_sq, 1)
            act.wait_ge(r_ss, n + 1)
            own.done(act.activation(R_r[:, :], psA[:, 2, :], ACT.Ln, scale=1.0 / P, bias=EPS))
            act.activation(R_r[:, :], R_r[:, :], ACT.Exp, scale=-0.5).then_inc(r_r, 1)
        repeat(act, 0, 7, hgrn_head)
        hgrn_head(7, "c_mix")
        own.end(8)
        over()

        for c in range(12):
            dst, src = (X_ah[:, c, :], C_oa[:, c, :]) if c < 4 else (X_hh[:, c - 4, :], C_oh[:, c - 4, :])
            act.activation(dst, src, ACT.Copy).then_inc(x_hi, 1)

        def mix(m, nxt=None):
            own.body(m, 2)
            g = GC + 44 + 4 * m
            b = 0 if nxt else m + 1
            act.wait_ge(g_done, G0 + g + 3)
            if nxt or not isinstance(m, int) or m:
                act.wait_ge(x_end, m)
            softplus_log(X_t[:, :, :], psG[:, 0:2, :]).then_inc(x_l, 1)
            act.wait_ge(x_m, m + 1)
            act.activation(X_t[:, :, :], X_t[:, :, :], ACT.Exp).then_inc(x_s, 1)
            high(nxt or "c_mix", b, 0, g + 2)
            high(nxt or "c_mix", b, 1, g + 4)
        mix(0)
        repeat(act, 1, 7, mix)
        mix(7, "c_o")
        own.end(8)
        for c in range(KC):
            if c == 0:
                act.wait_ge(x_end, KC)
            act.activation(xhi[:, c, META:], X_m[:, c, :], ACT.Copy).then_inc(y_hi, 1)
        GX = GC + 76
        high("c_o", 1, 0, GX + 2)
        high("c_o", 1, 1, GX + 4)
        over()

        norm_root((META, T))
        act.wait_ge(e_d, 1)
        act.activation(E_e[:, :], E_e[:, :], ACT.Exp).then_inc(e_dx, 1)
        for t in range(4):
            b = 2 * (t % 2)
            act.wait_ge(e_tr, t + 1)
            act.activation(E_vhi[:, t, :], psA[:, b:b + 2, :].rearrange("p b n -> p (b n)"), ACT.Copy).then_inc(e_vhi, 1)

        def high_expert(q, b):
            act.wait_ge(e_loaded[b % 4], 16 * (3 * q + b // 4) + 16)
            if b >= 3:
                act.wait_ge(g_done, G0 + GM + 12 * q + b - 2)
            act.activation(E_whi[:, b % 3, :], E_raw[:, b % 4, :], ACT.Copy).then_inc(e_high, 1)

        def inputs(q, piece):
            bank = 2 - 2 * (piece % 2)
            act.wait_ge(e_gath, 4 * q + piece + 1)
            act.activation(E_xh[:, 2 * piece:2 * piece + 2, :].rearrange("p c n -> p (c n)"), psG[:, bank, :], ACT.Copy)\
                .then_inc(e_xh, 1)

        def gate_log(q, j):
            act.wait_ge(g_done, G0 + GM + 12 * q + 4 * j + 4)
            softplus_log(E_l[:, j, :], psA[:, 2 * j, :]).then_inc(e_l, 1)

        def gate_exp(q, j):
            act.wait_ge(e_min, 2 * q + j + 1)
            act.activation(E_s[:, j, :], E_s[:, j, :], ACT.Exp).then_inc(e_sig, 1)

        def hidden_high(q, j, first=False):
            act.wait_ge(e_hT, 2 * q + j + 1)
            if not (first and j == 0):
                act.wait_ge(g_done, G0 + GM + 12 * q + (0 if j == 0 else 10))
            act.activation(E_hh[:, :, :].rearrange("p k n -> p (k n)"), psA[:, 2 * j, :], ACT.Copy).then_inc(e_hTs, 1)

        def outputs(q, j, first=False):
            act.wait_ge(g_done, G0 + GM + 12 * q + 10 + 2 * j)
            if not (first and j == 0):
                act.wait_ge(y_stored, 16 * (2 * q + j))
            act.activation(E_y[:, 0:512], psG[:, 0, :], ACT.Copy).then_inc(e_y, 1)

        def pair_of_experts(q, first=False):
            own.body(q, 4)
            for b in (3, 4, 5, 6):
                high_expert(q, b)
            gate_log(q, 0)
            high_expert(q, 7)
            gate_exp(q, 0)
            high_expert(q, 8)
            high_expert(q, 9)
            hidden_high(q, 0, first)
            high_expert(q, 10)
            gate_log(q, 1)
            gate_exp(q, 1)
            high_expert(q, 11)
            outputs(q, 0, first)
            inputs(q + 1, 0)
            high_expert(q, 12)
            for piece in (1, 2, 3):
                inputs(q + 1, piece)
            hidden_high(q, 1)
            high_expert(q, 13)
            outputs(q, 1)
            high_expert(q, 14)
        for b in range(3):
            high_expert(0, b)
        for piece in range(4):
            inputs(0, piece)
        pairs(act, pair_of_experts)
        over()

        for t in range(4):
            act.wait_ge(e_acc, t + 1)
            act.activation(E_hold[:, :, :].rearrange("p c n -> p (c n)")[:, t * D:(t + 1) * D], F_rows[:, 8 + t, :], ACT.Square, accum_out=E_e[:, t:t + 1]).then_inc(e_sq, 1)
        act.wait_ge(e_sq, 4)
        act.activation(E_e[:, 4:8], E_e[:, 0:4], ACT.Ln, scale=1.0 / D, bias=EPS).then_inc(e_rr, 1)
        act.wait_ge(e_rr, 1)
        act.activation(E_e[:, 4:8], E_e[:, 4:8], ACT.Exp, scale=-0.5).then_inc(e_rr, 1)

    @block.vector
    def _(dve):
        own = Steps(dve, dve_own)
        phases = 0

        def over():
            nonlocal phases
            phases += 1
            dve.drain().then_inc(s_phase, 1)
            dve.wait_ge(s_phase, 4 * phases)

        def low(name, i, s):
            tiles = TILES[name][s]
            u = use(name, i, s)
            dve.wait_ge(w_high[s], u + 1)
            dve.tensor_tensor(wlo[:, s, 0:tiles * P], raw[:, s, 0:tiles * P],
                              whi[:, s, 0:tiles * P].bitcast(F32), ALU.subtract).then_inc(w_split[s], 1)

        roots = scalings = 0

        def newton(r, v, t, width):
            own.done(dve.tensor_scalar(t[0], v, -0.5 / width, -0.5 * EPS, ALU.mult, ALU.add))
            own.done(dve.tensor_tensor(t[1], t[1], r, ALU.mult))
            own.done(dve.tensor_tensor(t[1], t[1], r, ALU.mult))
            own.done(dve.scalar_tensor_tensor(out=r, in0=t[1], scalar=1.5, in1=r, op0=ALU.add, op1=ALU.mult))

        def fold(x, tok):
            return x.rearrange("p (b n) -> p b n", b=2) if tok > 512 else x

        def norm_root(cols):
            nonlocal roots
            c0, c1 = cols
            dve.wait_ge(n_r0, roots + 1)
            t = N_t[:, c0:c1]
            v = psA[:, 0:2, 0:(c1 - c0) // 2] if c1 - c0 > 512 else psA[:, 0, 0:c1 - c0]
            newton(N_r[:, c0:c1], v, (fold(t, c1 - c0), t), D)
            roots += 1

        def norm_scale(cols, gain, split=True):
            nonlocal scalings
            c0, c1 = cols
            for c in range(KC):
                dve.scalar_tensor_tensor(out=N_sq[:, c, c0:c1], in0=h[:, c, c0:c1],
                                         scalar=gains[:, gain * KC + c:gain * KC + c + 1], in1=N_r[:, c0:c1],
                                         op0=ALU.mult, op1=ALU.mult).then_inc(n_t, 1)
            for c in range(KC if split else 0):
                dve.wait_ge(n_hi, scalings * KC + c + 1)
                dve.tensor_tensor(xlo[:, c, c0:c1], N_sq[:, c, c0:c1], xhi[:, c, c0:c1].bitcast(F32),
                                  ALU.subtract).then_inc(n_lo, 1)
            scalings += 1

        own.done(dve.memset(A_k[:, :, T:TP], 0.0))
        dve.wait_ge(s_con, 32)
        norm_root((0, T))
        norm_scale((0, T), 0)

        def softplus(n, u):
            c0, c1 = (0, SP_A) if u == 0 else (SP_A, SP_A + SP_B)
            src = psA[:, 0, 0:SP_A] if u == 0 else psA[:, 1:3, :].rearrange("p b n -> p (b n)")[:, 0:SP_B]
            dve.wait_ge(a_abs, 2 * n + u + 1)
            dve.scalar_tensor_tensor(out=A_sp[:, c0:c1], in0=src, scalar=0.0, in1=A_t[:, c0:c1],
                                     op0=ALU.max, op1=ALU.add).then_inc(a_sp, 1)

        def vt(i, s):
            t = 8 * i + 4 * s + 3
            dve.wait_ge(g_done, G0 + t + 1)
            dve.tensor_copy(A_vt[:, s, 0:4, :].rearrange("p c n -> p (c n)"), psG[:, 2, :])
            dve.tensor_copy(A_vt[0:TAIL, s, 4, :], psG[0:TAIL, 3, 0:P]).then_inc(a_vt, 1)

        def outputs(i, s, hh):
            n = 4 * i + 2 * s + hh
            rows = slice(HD * hh, HD * hh + HD)
            dve.wait_ge(a_o, n + 1)
            chunk = A_o[rows, bass.ds(2 * i + s, 1), :].rearrange("p a n -> p (a n)")
            dve.tensor_copy(chunk[:, 0:512], psA[rows, 3, :])
            dve.tensor_copy(chunk[:, 512:T], psA[rows, 0, SP_A:SP_A + TAIL]).then_inc(a_free, 1)

        def pair(i, s, more=True, nxt="a_qkv"):
            ni, ns = (i, 1) if s == 0 else (i + 1, 0)
            p = 2 * i + s
            b = p + 2 if nxt == "a_qkv" else 0
            for hh in range(2):
                n = 2 * p + hh
                softplus(n, 0)
                softplus(n, 1)
                if more and hh == 1:
                    vt(ni, ns)
                outputs(i, s, hh)
                if more:
                    low(nxt, b, hh)

        low("a_qkv", 0, 0)
        low("a_qkv", 0, 1)
        vt(0, 0)
        low("a_qkv", 1, 0)
        low("a_qkv", 1, 1)

        def both(i):
            pair(i, 0)
            pair(i, 1)
        repeat(dve, 0, 3, both)
        pair(3, 0, nxt="a_o")
        pair(3, 1, more=False)

        for c in range(KC):
            dve.wait_ge(o_hi, c + 1)
            dve.tensor_tensor(xlo[:, c, :], A_o[:, c, :], xhi[:, c, :].bitcast(F32), ALU.subtract).then_inc(o_lo, 1)

        def residual(g, m, par, tok):
            dve.wait_ge(g_done, G0 + g + 1)
            hm = h[:, m, T - tok:]
            if tok > 512:
                src, hm = psG[:, 2 * par:2 * par + 2, 0:tok // 2], hm.rearrange("p (b n) -> p b n", b=2)
            else:
                src = psG[:, 2 * par, 0:tok]
            dve.tensor_tensor(hm, hm, src, ALU.add).then_inc(r_add, 1)

        def project(name, nxt, tok, g0):
            for b in range(4):
                for j in range(2):
                    residual(g0 + 2 * b + j, 2 * b + j, j, tok)
                if b < 2:
                    low(name, 1, b)
                elif nxt:
                    low(nxt, 0, b - 2)
        project("a_o", "mlp0", T, 32)
        over()
        norm_root((0, T))
        norm_scale((0, T), 1)

        def mlp(name, nxt, tok, before, g0):
            def into(step, buf, first=False):
                for j in range(2):
                    if not first:
                        dve.wait_ge(m_lo, before + 2 * step + j - 1)
                    dve.wait_ge(m_r, before + 2 * step + j + 1)
                    dve.tensor_tensor(M_t[:, j, 0:tok], M_r[:, j, 0:tok], M_r[:, j, 0:tok], ALU.mult).then_inc(m_t, 1)
                for j in range(2):
                    dve.wait_ge(m_hi, before + 2 * step + j + 1)
                    dve.tensor_tensor(M_lo[:, buf, j, 0:tok], M_t[:, j, 0:tok],
                                      M_hi[:, buf, j, 0:tok].bitcast(F32), ALU.subtract).then_inc(m_lo, 1)

            into(0, 0, first=True)
            low(name, 1, 0)

            def step(j, buf, nxt0=None):
                into(j + 1, 1 - buf)
                low(name, j + 1, 1)
                for m in range(KC):
                    residual(g0 + 4 + 10 * j + m, m, m % 2, tok)
                if nxt0 is None:
                    low(name, j + 2, 0)
                else:
                    low(nxt0, 0, 0)

            def two(i):
                step(2 * i, 0)
                step(2 * i + 1, 1)
            repeat(dve, 0, 7, two)
            step(14, 0, nxt)
            for m in range(KC):
                residual(g0 + 152 + m, m, m % 2, tok)
            low(nxt, 0, 1)
        mlp("mlp0", NEXT["mlp0"], T, 0, 40)
        over()

        norm_root((0, T))
        norm_scale((META, T), 2)
        dve.wait_ge(b_con, 32)
        for m in range(2):
            own.done(dve.tensor_tensor(N_t[:, m * HD:(m + 1) * HD], B_lam[:, 2 * m * HD:(2 * m + 1) * HD],
                                       B_lam[:, (2 * m + 1) * HD:(2 * m + 2) * HD], ALU.mult))
            ins = dve.tensor_reduce(lam[:, m:m + 1], N_t[:, m * HD:(m + 1) * HD], AX.X, ALU.add)
        ins.then_inc(b_lam, 1)

        def scale_head(n, v, tok, par, gain):
            dve.wait_ge(b_root, n + 1)
            if not isinstance(n, int) or n >= 2:
                dve.wait_ge(b_rope, n - 1)
            t = B_t[:, par, 0:tok]
            newton(B_r[:, 0:tok], v, (fold(t, tok), t), HD)
            dve.scalar_tensor_tensor(out=t, in0=B_raw[:, par, 0:tok], scalar=gains[:, gain:gain + 1],
                                     in1=B_r[:, 0:tok], op0=ALU.mult, op1=ALU.mult).then_inc(b_t, 1)

        def rope(n, rot, tok, par, dst):
            dve.wait_ge(b_rot, n + 1)
            t, x, c0 = B_t[:, par, 0:tok], N_t[:, 0:tok], T - tok
            own.mark(dve.tensor_tensor(t, t, cosine[:, c0:], ALU.mult))
            if not isinstance(n, int) or n >= 1:
                dve.wait_ge(b_rope, n)
            own.done(dve.tensor_tensor(fold(x, tok), rot, fold(sine[:, c0:], tok), ALU.mult))
            dve.tensor_tensor(dst, t, x, ALU.add).then_inc(b_rope, 1)

        own.done(dve.memset(stat[:, :, :], 0.0))
        own.done(dve.tensor_scalar(gains[:, QG + 2:QG + 3], gains[:, QG + 2:QG + 3], 1.0 - LAM_INIT,
                                   None, ALU.mult))
        for m in range(KC + 2):
            if 2 <= m:
                rope(m - 2, psA[:, 2, :], SEQ, m % 2, B_q[:, m - 2, :])
            if 1 <= m <= KC:
                scale_head(m - 1, psA[:, 0, :], SEQ, (m - 1) % 2, QG)
            if m in (1, 3):
                low("b_q", 1, m // 2)
            if m in (5, 7):
                low("b_kv", 0, (m - 5) // 2)
        norm_scale((0, T), 3)
        dve.wait_ge(b_lam, 2)
        own.done(dve.tensor_tensor(lam[:, 3:4], lam[:, 1:2], lam[:, 0:1], ALU.subtract))
        own.done(dve.tensor_scalar(lam[:, 2:3], lam[:, 3:4], -LAM_INIT, None, ALU.add))

        GK = 208

        def key_scale(i, s):
            scale_head(KC + 2 * i + s, psG[:, 0:2, 0:TH], T, s, QG + 1)

        def key_rope(i, s):
            if not isinstance(i, int) or 2 * i + s >= 2:
                dve.wait_ge(b_s, 4 * (2 * i + s) - 4)
            rope(KC + 2 * i + s, psG[:, 0:2, 0:TH], T, s, B_k[:, s, :])

        def value(i, s):
            n = 2 * i + s
            dve.wait_ge(g_done, G0 + GK + 3 * n + 3)
            if not isinstance(i, int) or n >= 2:
                dve.wait_ge(b_pv, 4 * n - 4)
            dve.tensor_copy(B_vt[:, s, 0:4, :].rearrange("p c n -> p (c n)"), psG[:, 0, :])
            dve.tensor_copy(B_vt[0:TAIL, s, 4, :], psG[0:TAIL, 1, 0:P]).then_inc(b_vt, 1)

        def maxima(i, s, qi):
            u = 4 * (2 * i + s) + qi
            par, L = qi % 2, META + P * (qi + 1)
            dve.wait_ge(b_s, u + 1)
            for m in range(2):
                if L > 512:
                    own.mark(dve.tensor_reduce(stat[:, par, m:m + 1], psA[:, 2 * m:2 * m + 2, 0:L // 2], AX.XY, ALU.max))
                else:
                    own.mark(dve.tensor_reduce(stat[:, par, m:m + 1], psA[:, 2 * m, 0:L], AX.X, ALU.max))
            dve.wait_ge(dve_own, own.at + own.k)
            dve.tensor_scalar(stat[:, par, 2:4], stat[:, par, 0:2], -(HD ** -0.5), None, ALU.mult).then_inc(b_max, 1)

        def combine(i, s, qi, first=False):
            u = 4 * (2 * i + s) + qi
            par, L = qi % 2, META + P * (qi + 1)
            dve.wait_ge(b_exp, 2 * u + 2)
            own.done(dve.reciprocal(stat[:, par, 6:8], stat[:, par, 4:6]))
            if not (first and qi == 0):
                dve.wait_ge(b_T, u)
            own.done(dve.tensor_scalar(B_w[:, 0:L], B_p[:, par, 1, 0:L], stat[:, par, 7:8], lam[:, 2:3],
                                       ALU.mult, ALU.mult))
            dve.scalar_tensor_tensor(out=B_w[:, 0:L], in0=B_p[:, par, 0, 0:L], scalar=stat[:, par, 6:7],
                                     in1=B_w[:, 0:L], op0=ALU.mult, op1=ALU.add).then_inc(b_w, 1)

        def outputs(i, s, qi):
            u = 4 * (2 * i + s) + qi
            dve.wait_ge(b_pv, u + 1)
            dst = B_o[:, bass.ds(2 * i + s, 1), qi * P:(qi + 1) * P].rearrange("p a n -> p (a n)")
            dve.tensor_copy(dst, psG[:, 3, 128:256]).then_inc(b_o, 1)

        def head(i, s, nxt, more=True, first=False):
            ni, ns = (i, 1) if s == 0 else (i + 1, 0)
            maxima(i, s, 0)
            combine(i, s, 0, first)
            maxima(i, s, 1)
            outputs(i, s, 0)
            if more:
                key_scale(ni, ns)
            combine(i, s, 1)
            maxima(i, s, 2)
            outputs(i, s, 1)
            nxt()
            if more:
                value(ni, ns)
            combine(i, s, 2)
            maxima(i, s, 3)
            outputs(i, s, 2)
            if more:
                key_rope(ni, ns)
            combine(i, s, 3)
            outputs(i, s, 3)

        key_scale(0, 0)
        value(0, 0)
        key_rope(0, 0)
        PER = 4 + 2 + 4 * 4
        own.body(0, 2 * PER)
        head(0, 0, lambda: low("b_kv", 1, 0), first=True)
        head(0, 1, lambda: low("b_kv", 1, 1))
        own.end(1)

        def heads(i):
            own.body(i - 1, 2 * PER)
            head(i, 0, lambda: low("b_kv", i + 1, 0))
            head(i, 1, lambda: low("b_kv", i + 1, 1))
        repeat(dve, 1, 3, heads)
        own.end(2)
        own.body(0, PER + 16)
        head(3, 0, lambda: low("b_o", 0, 0))
        head(3, 1, lambda: low("b_o", 0, 1), more=False)
        own.end(1)

        for n in range(KC + 1):
            if n < KC:
                dve.wait_ge(l_root, n + 1)
                if n >= 2:
                    dve.wait_ge(l_lo, n - 1)
                t = B_p[:, n % 2, 1, 0:SEQ]
                newton(B_raw[:, n % 2, 0:SEQ], psA[:, n % 4, :], (t, t), P)
                dve.scalar_tensor_tensor(out=B_p[:, n % 2, 0, 0:SEQ], in0=B_o[:, n, 0:SEQ],
                                         scalar=gains[:, QG + 2:QG + 3], in1=B_raw[:, n % 2, 0:SEQ],
                                         op0=ALU.mult, op1=ALU.mult).then_inc(l_t, 1)
            if n >= 1:
                dve.wait_ge(l_hi, n)
                dve.tensor_tensor(xlo[:, n - 1, META:], B_p[:, (n - 1) % 2, 0, 0:SEQ],
                                  xhi[:, n - 1, META:].bitcast(F32), ALU.subtract).then_inc(l_lo, 1)
        GO = 232
        project("b_o", "mlp1", SEQ, GO)
        over()
        norm_root((META, T))
        norm_scale((META, T), 4)
        mlp("mlp1", NEXT["mlp1"], SEQ, 32, GO + 8)
        over()

        dve.wait_ge(c_con, 64)
        norm_root((0, T))
        norm_scale((0, T), 5)
        lb0, lb1 = gains[:, QG + 5:QG + 5 + KC], gains[:, QG + 5 + KC:QG + 5 + 2 * KC]
        own.done(dve.tensor_tensor(C_lb[:, 2, :], lb0, lb1, ALU.max))
        own.mark(dve.tensor_tensor(C_lb[:, 0, :], lb0, C_lb[:, 2, :], ALU.subtract))
        dve.tensor_tensor(C_lb[:, 1, :], lb1, C_lb[:, 2, :], ALU.subtract).then_inc(c_lb, 1)
        dve.wait_ge(c_lb, 2)
        own.done(dve.tensor_tensor(C_lb[:, 2, :], C_lb[:, 0, :], C_lb[:, 1, :], ALU.add))
        own.done(dve.reciprocal(C_lb[:, 3, :], C_lb[:, 2, :]))
        own.done(dve.tensor_tensor(C_lb[:, 2, :], C_lb[:, 0, :], C_lb[:, 3, :], ALU.mult))
        own.done(dve.tensor_scalar(C_lb[:, 3, :], C_lb[:, 2, :], -1.0, 1.0, ALU.mult, ALU.add))
        own.done(dve.tensor_scalar(C_lb[:, 4, :], C_lb[:, 3, :], -1.0, None, ALU.mult))
        dve.wait_ge(f_sig, 1)
        own.done(dve.scalar_tensor_tensor(out=F_g[:, 2, :], in0=F_g[:, 0, :], scalar=0.0, in1=F_g[:, 1, :],
                                          op0=ALU.min, op1=ALU.subtract))
        own.done(dve.memset(F_g[:, 1, :], 1.0))
        own.done(dve.tensor_tensor_scan(F_g[:, 0, :], F_g[:, 1, :], F_g[:, 2, :], 0.0, ALU.mult, ALU.add))
        dve.tensor_scalar(F_g[:, 2, :], F_g[:, 0, :], -1.0, None, ALU.mult).then_inc(f_cum, 1)

        def forget_max(p, hh, qi):
            u = 8 * p + 4 * hh + qi
            par, L = qi % 2, META + P * (qi + 1)
            dve.wait_ge(f_s, u + 1)
            if L > 512:
                ins = dve.tensor_reduce(stat[:, par, 0:1], psA[:, 2 * par:2 * par + 2, 0:L // 2], AX.XY, ALU.max)
            else:
                ins = dve.tensor_reduce(stat[:, par, 0:1], psA[:, 2 * par, 0:L], AX.X, ALU.max)
            own.done(ins)
            dve.tensor_scalar(stat[:, par, 1:2], stat[:, par, 0:1], -1.0, None, ALU.mult).then_inc(f_max, 1)

        def forget_weights(p, hh, qi):
            u = 8 * p + 4 * hh + qi
            par, L = qi % 2, META + P * (qi + 1)
            dve.wait_ge(f_exp, u + 1)
            own.done(dve.reciprocal(stat[:, par, 3:4], stat[:, par, 2:3]))
            dve.tensor_scalar(F_p[:, par, 0:L], F_p[:, par, 0:L], stat[:, par, 3:4], None, ALU.mult).then_inc(f_w, 1)

        def forget_out(p, hh, qi):
            u = 8 * p + 4 * hh + qi
            rows = slice(HD * hh, HD * hh + HD)
            dve.wait_ge(f_pv, u + 1)
            dst = C_oa[rows, bass.ds(p, 1), qi * P:(qi + 1) * P].rearrange("p a n -> p (a n)")
            dve.tensor_copy(dst, psG[rows, 3, 128:256]).then_inc(f_o, 1)

        def forget_pair(p, nxt=None):
            own.body(p, 16)
            dve.wait_ge(f_vT, p + 1)
            dve.tensor_copy(F_vt[:, 0:4, :].rearrange("p c n -> p (c n)"), psG[:, 2, :])
            dve.tensor_copy(F_vt[0:TAIL, 4, :], psG[0:TAIL, 3, 0:P]).then_inc(f_vt, 1)
            units = [(hh, qi) for hh in range(2) for qi in range(4)]
            forget_max(p, 0, 0)
            for k, (hh, qi) in enumerate(units):
                forget_weights(p, hh, qi)
                if k < 7:
                    forget_max(p, *units[k + 1])
                if k in (2, 6):
                    low(nxt or "c_f", 0 if nxt else p + 1, k // 4)
                forget_out(p, hh, qi)
        repeat(dve, 0, 3, forget_pair)
        forget_pair(3, "c_h")
        own.end(4)
        over()

        def hgrn_head(n, nxt=None):
            own.body(n, HG)
            b = 0 if nxt else n + 1
            one = lambda row: C_lb[:, row, bass.ds(n, 1)]
            dve.wait_ge(r_fl, n + 1)
            fold2 = lambda x: x.rearrange("p (b n) -> p b n", b=2)
            dve.scalar_tensor_tensor(out=fold2(R_s[:, :]), in0=psG[:, 2:4, 0:TH], scalar=0.0, in1=fold2(R_l[:, :]),
                                     op0=ALU.min, op1=ALU.subtract).then_inc(r_fm, 1)
            dve.wait_ge(r_sig, n + 1)
            own.done(dve.tensor_scalar(R_k[:, :], R_s[:, :], one(4), one(3), ALU.mult, ALU.add))
            dve.tensor_scalar(R_s[:, :], R_s[:, :], one(3), one(2), ALU.mult, ALU.add).then_inc(r_fv, 1)
            dve.wait_ge(r_lf, n + 1)
            dve.tensor_tensor_scan(R_b[:, :], resets, R_s[:, :], 0.0, ALU.mult, ALU.add).then_inc(r_b, 1)
            dve.wait_ge(r_b, n + 1)
            for l in range(LEVELS):
                m = 1 << l
                bv = R_b[:, META:].rearrange("p (g h j) -> p g h j", h=2, j=m)
                xv = R_x[:, l, :].rearrange("p (g h j) -> p g h j", h=2, j=m)
                G = SEQ // (2 * m)
                ref = bv[:, :, 0, m - 1:m].broadcast_to([P, G, m])
                dve.tensor_tensor(xv[:, :, 0, :], ref, bv[:, :, 0, :], ALU.subtract)
                ins = dve.tensor_tensor(xv[:, :, 1, :], bv[:, :, 1, :], ref, ALU.subtract)
            ins.then_inc(r_d, 1)
            dve.wait_ge(r_eb, n + 1)
            dve.tensor_tensor(R_kd[:, 0:META + 3 * P], R_kd[:, 0:META + 3 * P], R_k[:, 0:META + 3 * P], ALU.mult).then_inc(r_kd, 1)
            own.mark(dve.tensor_tensor(R_qb[:, :], R_q[:, :], R_eb[:, :], ALU.mult))
            dve.wait_ge(r_ex, n + 1)
            for l in range(LEVELS):
                m = 1 << l
                view = lambda x: x.rearrange("p (g h j) -> p g h j", h=2, j=m)
                xv, kv, qv = view(R_x[:, l, :]), view(R_k[:, META:]), view(R_q[:, :])
                dve.tensor_tensor(xv[:, :, 0, :], xv[:, :, 0, :], kv[:, :, 0, :], ALU.mult)
                ins = dve.tensor_tensor(xv[:, :, 1, :], xv[:, :, 1, :], qv[:, :, 1, :], ALU.mult)
            ins.then_inc(r_x, 1)
            dve.wait_ge(r_gl, n + 1)
            dve.scalar_tensor_tensor(out=R_g[:, :], in0=psG[:, 2, :], scalar=0.0, in1=R_gl[:, :],
                                     op0=ALU.min, op1=ALU.subtract).then_inc(r_gm, 1)
            dve.wait_ge(r_U, n + 1)
            own.done(dve.tensor_copy(R_S[:, 0, :], psA[:, 2, 0:P]))
            for c in range(1, 4):
                ins = dve.scalar_tensor_tensor(out=R_S[:, c, :], in0=R_S[:, c - 1, :], scalar=R_d[:, c:c + 1],
                                               in1=psA[:, 2, c * P:(c + 1) * P], op0=ALU.mult, op1=ALU.add)
                if c < 3:
                    own.done(ins)
            ins.then_inc(r_S, 1)
            for j in range(4):
                dve.wait_ge(r_sc, 4 * n + j + 1)
                dve.tensor_tensor(R_m[:, :, :], psA[:, 0:2, :].rearrange("p b (l n) -> p (b l) n", l=4), level_masks,
                                  ALU.mult).then_inc(r_A, 1)
                dve.wait_ge(r_A, 4 * n + j + 1)
                dve.tensor_reduce(R_at[:, j, :], R_m[:, :, :].rearrange("p l n -> p n l"), AX.X, ALU.add).then_inc(r_at, 1)
                if j < 3:
                    dve.wait_ge(r_at, 4 * n + j + 1)
            low(nxt or "c_h", b, 0)
            low(nxt or "c_h", b, 1)
            dve.wait_ge(r_r, n + 1)
            newton(R_r[:, :], psA[:, 2, :], (R_t[:, :], R_t[:, :]), P)
            own.done(dve.scalar_tensor_tensor(out=R_t[:, :], in0=psA[:, 3, :], scalar=gains[:, QG + 4:QG + 5],
                                              in1=R_r[:, :], op0=ALU.mult, op1=ALU.mult))
            dve.wait_ge(r_gs, n + 1)
            dst = C_oh[:, bass.ds(n, 1), :].rearrange("p a n -> p (a n)")
            dve.tensor_tensor(dst, R_t[:, :], R_g[:, :], ALU.mult).then_inc(r_end, 1)
        HG = 10
        repeat(dve, 0, 7, hgrn_head)
        hgrn_head(7, "c_mix")
        own.end(8)
        over()

        for c in range(12):
            dve.wait_ge(x_hi, c + 1)
            hi_, lo_, src = (X_ah[:, c, :], X_al[:, c, :], C_oa[:, c, :]) if c < 4 else \
                (X_hh[:, c - 4, :], X_hl[:, c - 4, :], C_oh[:, c - 4, :])
            dve.tensor_tensor(lo_, src, hi_.bitcast(F32), ALU.subtract).then_inc(x_lo, 1)

        def mix(m, nxt=None):
            own.body(m, 1)
            b = 0 if nxt else m + 1
            dve.wait_ge(x_l, m + 1)
            dve.scalar_tensor_tensor(out=X_t[:, :, :], in0=psG[:, 0:2, :], scalar=0.0, in1=X_t[:, :, :],
                                     op0=ALU.min, op1=ALU.subtract).then_inc(x_m, 1)
            dve.wait_ge(g_done, G0 + GC + 44 + 4 * m + 4)
            dve.wait_ge(x_s, m + 1)
            own.done(dve.tensor_tensor(X_t[:, :, :], X_t[:, :, :], psG[:, 2:4, :], ALU.mult))
            dst = X_m[:, bass.ds(m, 1), :].rearrange("p a n -> p (a n)")
            dve.tensor_tensor(dst, X_t[:, 0, :], X_t[:, 1, :], ALU.add).then_inc(x_end, 1)
            low(nxt or "c_mix", b, 0)
            low(nxt or "c_mix", b, 1)
        repeat(dve, 0, 7, mix)
        mix(7, "c_o")
        own.end(8)
        for c in range(KC):
            dve.wait_ge(y_hi, c + 1)
            dve.tensor_tensor(xlo[:, c, META:], X_m[:, c, :], xhi[:, c, META:].bitcast(F32), ALU.subtract).then_inc(y_lo, 1)
        project("c_o", None, SEQ, GC + 76)
        over()

        norm_root((META, T))
        norm_scale((META, T), 6, split=False)
        dve.wait_ge(e_lg, 1)
        dve.tensor_copy(E_lg[:, :, :].rearrange("p t n -> p (t n)"), psG[:, 3, 0:4 * ROUTES]).then_inc(e_lgd, 1)
        dve.wait_ge(e_lgd, 1)
        dve.wait_ge(e_con, 64)

        def first_max(v, n, mx, oh):
            c = E_c[:, :, 0:n]
            over_n = lambda x: x.rearrange("p (t o) -> p t o", o=1).broadcast_to([P, 4, n])
            own.done(dve.tensor_reduce(mx, v, AX.X, ALU.max))
            own.done(dve.tensor_tensor(c, v, over_n(mx), ALU.is_equal))
            own.done(dve.scalar_tensor_tensor(out=c, in0=c, scalar=-64.0,
                                              in1=slot_of[:, 0:n].rearrange("p (o n) -> p o n", o=1).broadcast_to([P, 4, n]),
                                              op0=ALU.mult, op1=ALU.add))
            own.done(dve.tensor_reduce(E_mx[:, 3, :], c, AX.X, ALU.min))
            own.done(dve.tensor_tensor(oh, c, over_n(E_mx[:, 3, :]), ALU.is_equal))

        groups = E_lg[:, :, 0:GROUPS]
        over4 = lambda x, n: x.rearrange("p (t o) -> p t o", o=1).broadcast_to([P, 4, n])
        first_max(groups, GROUPS, E_mx[:, 0, :], E_oh[:, 0, :, 0:GROUPS])
        own.done(dve.tensor_tensor(E_e[:, 0:16].rearrange("p (t g) -> p t g", t=4), groups, over4(E_mx[:, 0, :], GROUPS),
                                   ALU.subtract))
        for g in range(GROUPS):
            own.done(dve.tensor_tensor(E_c[:, :, :], E_lg[:, :, GROUPS + g * PER_GROUP:GROUPS + (g + 1) * PER_GROUP],
                                       E_oh[:, 0, :, g:g + 1].broadcast_to([P, 4, PER_GROUP]), ALU.mult))
            if g == 0:
                own.done(dve.tensor_copy(E_sel[:, :, :], E_c[:, :, :]))
            else:
                own.done(dve.tensor_tensor(E_sel[:, :, :], E_sel[:, :, :], E_c[:, :, :], ALU.add))
        first_max(E_sel[:, :, :], PER_GROUP, E_mx[:, 1, :], E_oh[:, 1, :, :])
        own.done(dve.scalar_tensor_tensor(out=E_sel[:, :, :], in0=E_oh[:, 1, :, :], scalar=NEG, in1=E_sel[:, :, :],
                                          op0=ALU.mult, op1=ALU.add))
        first_max(E_sel[:, :, :], PER_GROUP, E_mx[:, 2, :], E_oh[:, 2, :, :])
        dve.tensor_tensor(E_e[:, 16:20], E_mx[:, 2, :], E_mx[:, 1, :], ALU.subtract).then_inc(e_d, 1)
        for c in range(2):
            for g in range(GROUPS):
                own.mark(dve.tensor_tensor(E_M[:, c, :, g * PER_GROUP:(g + 1) * PER_GROUP], E_oh[:, 1 + c, :, :],
                                           E_oh[:, 0, :, g:g + 1].broadcast_to([P, 4, PER_GROUP]), ALU.mult))
        dve.wait_ge(dve_own, own.base)
        dve.tensor_tensor(E_M[:, 2, :, :], E_M[:, 0, :, :], E_M[:, 1, :, :], ALU.add).then_inc(e_m, 1)
        dve.wait_ge(e_dx, 1)
        own.done(dve.tensor_reduce(E_g[:, 0, :], E_e[:, 0:16].rearrange("p (t g) -> p t g", t=4), AX.X, ALU.add))
        own.done(dve.tensor_scalar(E_g[:, 1, :], E_e[:, 16:20], 1.0, None, ALU.add))
        own.done(dve.tensor_tensor(E_g[:, 1, :], E_g[:, 1, :], E_g[:, 0, :], ALU.mult))
        own.done(dve.reciprocal(E_g[:, 2, :], E_g[:, 1, :]))
        own.done(dve.tensor_tensor(E_g[:, 3, :], E_g[:, 2, :], E_e[:, 16:20], ALU.mult))
        for t in range(4):
            b = 2 * (t % 2)
            dve.wait_ge(e_tr, t + 1)
            dve.wait_ge(e_vhi, t + 1)
            dve.tensor_tensor(E_vlo[:, t, :], psA[:, b:b + 2, :].rearrange("p b n -> p (b n)"),
                              E_vhi[:, t, :].bitcast(F32), ALU.subtract).then_inc(e_vlo, 1)
        dve.wait_ge(e_rank, 1)
        own.done(dve.tensor_tensor(E_t[:, :, :], psG[:, 0, 0:P].rearrange("p (t e) -> p t e", t=4),
                                   first_row[:, 0:EXPERTS].rearrange("p (o n) -> p o n", o=1).broadcast_to([P, 4, EXPERTS]),
                                   ALU.add))
        for k in range(1, SEQ // SLOTS):
            own.done(dve.tensor_scalar(E_M[:, 2, :, :], psG[:, 0, 0:P].rearrange("p (t e) -> p t e", t=4), SLOTS * k - 0.5,
                                       float((EXPERTS - 1) * SLOTS), ALU.is_gt, ALU.mult))
            own.done(dve.tensor_tensor(E_t[:, :, :], E_t[:, :, :], E_M[:, 2, :, :], ALU.add))
        for c in range(2):
            own.done(dve.tensor_tensor(E_M[:, c, :, :], E_M[:, c, :, :], E_t[:, :, :], ALU.mult))
            own.done(dve.tensor_reduce(E_pos[:, 4 * c:4 * c + 4], E_M[:, c, :, :], AX.X, ALU.add))
        own.done(dve.tensor_copy(E_idx[:, :], E_pos[:, :]))
        own.done(dve.tensor_reduce(E_cnt[:, 0:1], psG[:, 0, P:P + EXPERTS], AX.X, ALU.max))
        own.done(dve.tensor_scalar(E_cnt[:, 1:2], E_cnt[:, 0:1], float(SLOTS), None, ALU.is_gt))
        dve.tensor_copy(E_flag[:, :], E_cnt[:, 1:2]).then_inc(e_route, 1)

        def low_expert(q, b):
            dve.wait_ge(e_high, 12 * q + b + 1)
            dve.tensor_tensor(E_wlo[:, b % 3, :], E_raw[:, b % 4, :], E_whi[:, b % 3, :].bitcast(F32), ALU.subtract)\
                .then_inc(e_split, 1)

        def inputs(q, piece):
            bank = 2 - 2 * (piece % 2)
            dve.wait_ge(e_gath, 4 * q + piece + 1)
            dve.tensor_copy(E_xl[:, 2 * piece:2 * piece + 2, :].rearrange("p c n -> p (c n)"), psG[:, bank + 1, :])\
                .then_inc(e_xl, 1)

        def gate_min(q, j, first):
            dve.wait_ge(e_l, 2 * q + j + 1)
            if not first:
                dve.wait_ge(e_prod, 2 * q + j - 1)
            dve.scalar_tensor_tensor(out=E_s[:, j, :], in0=psA[:, 2 * j, :], scalar=0.0, in1=E_l[:, j, :],
                                     op0=ALU.min, op1=ALU.subtract).then_inc(e_min, 1)

        def gated(q, j, first):
            dve.wait_ge(e_sig, 2 * q + j + 1)
            if not first:
                dve.wait_ge(e_hT, 2 * q + j - 1)
            dve.tensor_tensor(E_hid[:, j, :], E_s[:, j, :], psA[:, 2 * j, :], ALU.mult).then_inc(e_prod, 1)
            dve.wait_ge(e_prod, 2 * q + j + 1)
            dve.tensor_tensor(E_hid[:, j, :], E_hid[:, j, :], psA[:, 2 * j + 1, :], ALU.mult).then_inc(e_hid, 1)

        def hidden_low(q, j):
            dve.wait_ge(e_hTs, 4 * q + 2 * j + 1)
            dve.tensor_tensor(E_hl[:, :, :].rearrange("p k n -> p (k n)"), psA[:, 2 * j, :],
                              E_hh[:, :, :].rearrange("p k n -> p (k n)").bitcast(F32), ALU.subtract).then_inc(e_hTs, 1)

        def outputs(q, j, first=False):
            dve.wait_ge(g_done, G0 + GM + 12 * q + 10 + 2 * j)
            if not (first and j == 0):
                dve.wait_ge(y_stored, 16 * (2 * q + j))
            dve.tensor_copy(E_y[:, 512:D], psG[:, 1, :]).then_inc(e_y, 1)

        def pair_of_experts(q, first=False):
            for b in (3, 4, 5, 6):
                low_expert(q, b)
            gate_min(q, 0, first)
            low_expert(q, 7)
            gated(q, 0, first)
            low_expert(q, 8)
            low_expert(q, 9)
            hidden_low(q, 0)
            low_expert(q, 10)
            gate_min(q, 1, first)
            gated(q, 1, first)
            low_expert(q, 11)
            outputs(q, 0, first)
            inputs(q + 1, 0)
            low_expert(q, 12)
            for piece in (1, 2, 3):
                inputs(q + 1, piece)
            hidden_low(q, 1)
            low_expert(q, 13)
            outputs(q, 1)
            low_expert(q, 14)
        for b in range(3):
            low_expert(0, b)
        for piece in range(4):
            inputs(0, piece)
        pairs(dve, pair_of_experts)
        more = dve.value_load(E_flag[0:1, 0:1], min_val=0, max_val=1)
        dve.wait_ge(e_loaded[3], 16 * (3 * EXPERTS // 2 + 1))
        with dve.If(more > 0):
            dve.wait_ge(e_loaded[3], 16 * (3 * BLOCKS_IN_ALL // 2 + 1))
        over()

        for t in range(4):
            if t == 0:
                dve.wait_ge(e_rows, 16 * 9)
            dve.wait_ge(e_ht, t + 1)
            ps = psG if t < 2 else psA
            for c in range(2):
                hidden = ps[:, 2 * (t % 2):2 * (t % 2) + 2, :].rearrange("p b n -> p (b n)") if c == 0 else F_rows[:, 8 + t, :]
                ins = dve.scalar_tensor_tensor(out=F_rows[:, 8 + t, :], in0=F_rows[:, 2 * t + c, :],
                                               scalar=E_g[:, 2 + c, t:t + 1], in1=hidden, op0=ALU.mult, op1=ALU.add)
                if c == 0:
                    own.done(ins)
            ins.then_inc(e_acc, 1)
        dve.wait_ge(e_rr, 2)
        r, v, q = E_e[:, 4:8], E_e[:, 0:4], E_e[:, 8:12]
        for ins in (lambda: dve.tensor_scalar(q, v, -0.5 / D, -0.5 * EPS, ALU.mult, ALU.add),
                    lambda: dve.tensor_tensor(q, q, r, ALU.mult),
                    lambda: dve.tensor_tensor(q, q, r, ALU.mult),
                    lambda: dve.scalar_tensor_tensor(out=r, in0=q, scalar=1.5, in1=r, op0=ALU.add, op1=ALU.mult)):
            own.done(ins())
        for t in range(4):
            dve.scalar_tensor_tensor(out=E_raw[:, t, 0:D], in0=F_rows[:, 8 + t, :], scalar=r[:, t:t + 1],
                                     in1=E_y[:, :], op0=ALU.mult, op1=ALU.mult).then_inc(e_fin, 1)

    @block.gpsimd
    def _(pool):
        phases = 0

        def over():
            nonlocal phases
            phases += 1
            pool.drain().then_inc(s_phase, 1)
            pool.wait_ge(s_phase, 4 * phases)

        def past(dst, blocks, width):
            return pool.affine_select(out=dst, in_=dst, compare_op=ALU.is_gt, fill=0.0, base=0,
                                      pattern=[[0, blocks], [1, width]], channel_multiplier=-1)

        def mask(n, u, src, ready, done):
            pool.wait_ge(ready, 2 * n + u + 1)
            pool.sem_inc(begun, 1)
            if u == 0:
                past(src[:, 0:512].rearrange("p (a n) -> p a n", a=2)[:, :, 0:P], 2, P)
                ins = past(src[:, 448:464].rearrange("p (a n) -> p a n", a=1), 1, TAIL)
            else:
                past(src[:, SP_A + 512:SP_A + 640].rearrange("p (a n) -> p a n", a=1), 1, P)
                ins = past(src[:, SP_A + 768:SP_A + 896].rearrange("p (a n) -> p a n", a=1), 1, P)
            ins.then_inc(done, 1)

        def body(i):
            for hh in range(2):
                n = 2 * i + hh
                for src, ready, done in ((A_sp, a_sp, a_spm), (A_w, a_w, a_wm)):
                    mask(n, 0, src, ready, done)
                    mask(n, 1, src, ready, done)
        repeat(pool, 0, 8, body)
        over()
        over()

        pool.dma_start(B_con[:, :], a["b_con"]).then_inc(b_con, 16)
        pool.dma_start(B_lam[:, :], a["b_lam"]).then_inc(b_con, 16)

        def queries(i, s, first=False):
            n = 2 * i + s
            if not first:
                pool.wait_ge(b_s, 4 * n - 4)
            pool.tensor_copy(B_qs[:, s, :], B_q[:, bass.ds(n, 1), :].rearrange("p a n -> p (a n)")).then_inc(b_qs, 1)
        pool.wait_ge(b_rope, KC)
        queries(0, 0, True)
        queries(0, 1, True)

        def heads(i):
            queries(i, 0)
            queries(i, 1)
        repeat(pool, 1, 4, heads)
        over()
        over()

        pool.dma_start(h[:, :, 0:META], a["meta2"]).then_inc(c_con, 16)
        pool.dma_start(C_con[:, :], a["c_con"]).then_inc(c_con, 16)
        pool.dma_start(F_w[:, :, :], a["w_fa"]).then_inc(c_con, 16)
        pool.dma_start(stat[:, :, :], a["zero16"]).then_inc(c_con, 16)
        pool.wait_ge(f_cum, 1)
        pool.dma_start(F_row[0:1, :].rearrange("o (h n) -> o h n", h=KC), F_g[:, 2, :]).then_inc(f_row, 16)
        over()
        over()
        over()

        pool.dma_start(slot_of[:, :], a["e_slots"]).then_inc(e_con, 16)
        pool.dma_start(first_row[:, :], a["e_rows"]).then_inc(e_con, 16)
        pool.dma_start(E_wr[:, :, :], a["w_er"]).then_inc(e_con, 16)
        pool.dma_start(E_br[:, :], a["e_br"]).then_inc(e_con, 16)

        def slots(q, first=False):
            if not first:
                pool.wait_ge(e_gath, 4 * q)
            pool.tensor_copy(E_base[:, :], first_row[:, bass.ds(EXPERTS + q, 1)]).then_inc(e_rel, 1)
            pool.wait_ge(e_rel, 3 * q + 1)
            pool.sem_inc(begun, 1)
            pool.tensor_scalar(E_rel[:, :], E_pos[:, :], E_base[:, 0:1], None, ALU.subtract).then_inc(e_rel, 1)
            pool.wait_ge(e_rel, 3 * q + 2)
            pool.sem_inc(begun, 1)
            for t in range(4):
                pool.tensor_scalar(E_S[:, t, :], slot_of[:, :], E_rel[:, t:t + 1], None, ALU.is_equal)
                ins = pool.tensor_scalar(E_A[:, t, :], slot_of[:, :], E_rel[:, 4 + t:5 + t], None, ALU.is_equal)
            ins.then_inc(e_rel, 1)
            pool.wait_ge(e_rel, 3 * q + 3)
            pool.sem_inc(begun, 1)
            for t in range(4):
                ins = pool.tensor_tensor(E_S[:, t, :], E_S[:, t, :].bitcast(F32), E_A[:, t, :], ALU.add)
            ins.then_inc(e_S, 1)

        def store(q, j):
            pool.wait_ge(e_y, 4 * q + 2 * j + 2)
            pool.dma_start(y_rows[bass.ds((2 * q + j) * SLOTS, SLOTS), :], E_y[:, :]).then_inc(y_stored, 16)

        def pair_of_experts(q, first=False):
            slots(q + 1)
            store(q, 0)
            store(q, 1)
        pool.wait_ge(e_route, 1)
        slots(0, True)
        pairs(pool, pair_of_experts)
        more = pool.value_load(E_flag[0:1, 0:1], min_val=0, max_val=1)
        pool.wait_ge(y_stored, 16 * EXPERTS)
        with pool.If(more > 0):
            pool.wait_ge(y_stored, 16 * BLOCKS_IN_ALL)
        over()

        pool.dma_start(E_y[:, :], a["e_gain"]).then_inc(e_rows, 16)
        def rows_of_tokens(rows):
            for t in range(4):
                for c in range(2):
                    pool.indirect_dma_start(F_rows[:, 2 * t + c, :], None, rows,
                                            bass.IndirectOffsetOnAxis(E_idx[:, 4 * c + t:4 * c + t + 1], 0)).then_inc(e_rows, 16)
        with pool.If(more > 0):
            rows_of_tokens(y_rows[:, :])
        with pool.If(more < 1):
            rows_of_tokens(y_rows[0:EXPERTS * SLOTS, :])

    top.close()


def blocks_of(w, tiles_k, cols):
    k, m = w.shape
    x = w.reshape(k // (P * tiles_k), tiles_k, P, m // (P * cols), cols, P)
    return x


def pack(tiles):
    return np.stack([np.concatenate(b, axis=1) for b in tiles])


def pack_pairs(pairs):
    most = max(len(b) for pair in pairs for b in pair)
    empty = np.zeros((P, P), np.float32)
    return pack([b + [empty] * (most - len(b)) for pair in pairs for b in pair])


def tile_of(w, k, m):
    return w[k * P:(k + 1) * P, m * P:(m + 1) * P]


def columns(w, ms, ks=range(KC)):
    return [tile_of(w, k, m) for m in ms for k in ks]


def mlp_blocks(w_in, w_out):
    into = [columns(w_in, (2 * j, 2 * j + 1)) for j in range(MLP_STEPS)]
    out = [columns(w_out, range(KC), (2 * j, 2 * j + 1)) for j in range(MLP_STEPS)]
    order = [into[0]]
    for j in range(MLP_STEPS - 1):
        order += [into[j + 1], out[j]]
    return pack(order + [out[MLP_STEPS - 1]])


def expert_blocks(w_in, w_out):
    n = 2 * P * D
    both = [w.reshape(EXPERTS // 2, 2 * w.shape[1] * w.shape[2] // n, 2, P, D) for w in (w_in, w_out)]
    order = np.concatenate(both, axis=1).reshape(-1, 2, P, D).transpose(0, 2, 1, 3).reshape(-1, P, 2 * D)
    return np.concatenate([order, order[:4]])


def feature_major(x):
    return np.ascontiguousarray(x.T.reshape(-1, P, x.shape[0]).transpose(1, 0, 2))


def per_feature(v):
    return np.ascontiguousarray(v.reshape(-1, P).T)


def kernel(**x):
    from concourse import bacc
    from concourse.bass_utils import run_bass_kernel_spmd

    x = {k: np.asarray(v) for k, v in x.items()}
    r = np.arange(P)
    tri = -(r[:, None] >= r[None, :]).astype(np.float32)
    half = HD // 8
    freq = np.float32(500000.0) ** (-np.arange(0, 2 * half, 2, dtype=np.float32) / np.float32(2 * half))
    ang = (np.arange(T, dtype=np.float32)[None, :] * freq[:, None]).astype(np.float32)
    f = r % HD
    turns = (f < 2 * half)[:, None]
    cos_t = np.where(turns, np.cos(ang)[f % half], 1.0)
    sin_t = np.where(turns, np.sin(ang)[f % half], 0.0)
    rot = np.zeros((P, P))
    for m in range(P):
        if m % HD < half:
            rot[m + half, m] = -1.0
        elif m % HD < 2 * half:
            rot[m - half, m] = 1.0
    b_con = np.concatenate([(r[:, None] // HD == r[None, :] // HD), rot, np.where(r[None, :] > r[:, None], NEG, 0.0),
                            cos_t, sin_t], axis=1).astype(np.float32)
    masks = []
    for l in range(LEVELS):
        m = 1 << l
        masks.append((r[:, None] // (2 * m) == r[None, :] // (2 * m)) & (r[:, None] % (2 * m) < m) & (r[None, :] % (2 * m) >= m))
    masks.append(r[:, None] == r[None, :])
    starts = np.ones(T)
    starts[[0] + [META + c * P for c in range(4)]] = 0.0
    c_con = np.concatenate(masks + [np.where(r[None, :] > r[:, None], NEG, 0.0), np.broadcast_to(starts, (P, T))],
                           axis=1).astype(np.float32)
    parts = np.split(x["w_in_2"][0], np.cumsum([512, 512, 512, 8, D, D, D, D, D, D])[:-1], axis=1)
    data = {
        "con": np.concatenate([np.eye(P), np.ones((P, P)), tri, -np.ones((P, P))], axis=1).astype(np.float32),
        "h": feature_major(np.concatenate([x["meta_tokens"], x["x"][0]])),
        "gains": np.concatenate([per_feature(g) for g in (
            x["a_norm_g"][0], x["mlp_norm_g"][0], x["b_norm_g"][0], x["kv_norm_g"], x["mlp_norm_g"][1],
            x["norm_mix_w_2"][0], x["norm_ffn_w_2"][0], x["b_q_norm_g"][0].reshape(-1), x["kv_k_norm_g"].reshape(-1), x["b_subln_g"][0],
            np.concatenate([x["attn_forget_b_2"][0], np.zeros(P - KC, np.float32)]), x["hgrn_norm_w_2"][0],
            x["hgrn_lb_logits_2"].reshape(-1))], axis=1),
        "b_con": b_con,
        "b_lam": np.ascontiguousarray(np.broadcast_to(x["b_lambda"][0].reshape(1, -1), (P, 4 * HD))),
        "w_b_q": pack([columns(x["b_w_q"][0], (2 * b, 2 * b + 1)) for b in range(4)]),
        "w_b_kv": pack([columns(x["kv_w"], (n, 8 + n)) for n in range(8)]),
        "w_b_o": pack([columns(x["b_w_o"][0], (2 * b, 2 * b + 1)) for b in range(4)]),
        "w_mlp1": mlp_blocks(x["mlp_w_in"][1], x["mlp_w_out"][1]),
        "w_a_qkv": pack_pairs([(columns(x["a_w_qkv"][0], (p, 8 + p)), columns(x["a_w_qkv"][0], (16 + p,))) for p in range(8)]),
        "w_a_o": pack([columns(x["a_w_o"][0], (2 * b, 2 * b + 1)) for b in range(4)]),
        "w_mlp0": mlp_blocks(x["mlp_w_in"][0], x["mlp_w_out"][0]),
        "e_slots": np.broadcast_to(np.arange(2 * SLOTS, dtype=np.float32), (P, 2 * SLOTS)).copy(),
        "e_rows": np.broadcast_to(np.concatenate([np.arange(EXPERTS) * SLOTS, np.arange(2 * EXPERTS + 1) * 2 * SLOTS])
                                  .astype(np.float32), (P, 3 * EXPERTS + 1)).copy(),
        "w_er": np.ascontiguousarray(np.concatenate([x["w_router_group_2"][0], x["w_router_expert_2"][0]], axis=1)
                                     .reshape(KC, P, ROUTES).transpose(1, 0, 2)),
        "e_br": np.concatenate([x["b_router_group_2"][0], x["b_router_expert_2"][0]])[None, :],
        "e_gain": np.ascontiguousarray(np.broadcast_to(x["norm_final_w_2"][None, :], (P, D))),
        "w_moe": expert_blocks(x["w_expert_in_2"][0], x["w_expert_out_2"][0]),
        "meta2": feature_major(x["meta_tokens_2"]),
        "c_con": c_con,
        "zero16": np.zeros((P, 2, 8), np.float32),
        "w_fa": np.ascontiguousarray(parts[3].reshape(KC, P, KC).transpose(1, 0, 2)),
        "w_c_f": pack_pairs([(columns(parts[0], (p,)) + columns(parts[1], (p,)), columns(parts[2], (p,))) for p in range(4)]),
        "w_c_h": pack([b for n in range(KC) for b in (columns(parts[4], (n,)) + columns(parts[5], (n,)),
                                                      columns(parts[6], (n,)) + columns(parts[7], (n,)))]),
        "w_c_mix": pack_pairs([(columns(parts[8], (m,)) + columns(x["w_attn_out_2"][0], (m,), range(4)),
                                columns(parts[9], (m,)) + columns(x["w_hgrn_out_2"][0], (m,))) for m in range(KC)]),
        "w_c_o": pack([columns(x["w_o_2"][0], (2 * b, 2 * b + 1)) for b in range(4)]),
    }
    nc = bacc.Bacc("TRN2", target_bir_lowering=False, num_devices=1)
    args = {k: nc.dram_tensor("in_" + k, v.shape, mybir.dt.from_np(v.dtype), kind="ExternalInput").ap() for k, v in data.items()}
    args["out"] = nc.dram_tensor("out_final", (SEQ, D), F32, kind="ExternalOutput").ap()
    build(nc, args)
    got = run_bass_kernel_spmd(nc, [{"in_" + k: v for k, v in data.items()}], core_ids=[0]).results[0]["out_final"]
    return got.reshape(1, SEQ, D)
```
